# Optimizing a Trainium2 kernel written in Bass

```python
import jax, jax.numpy as jnp
from jax import lax
import numpy as np

D_MODEL = 1024
BATCH = 1
SEQ = 1024
DEPTH = 2

N_EVEN = (DEPTH + 1) // 2
N_ODD = DEPTH // 2
NORM_EPS = 1e-5

GLA_HEADS = 4
GLA_DK = 64
GLA_DV = 128
GLA_KEY = GLA_HEADS * GLA_DK
GLA_VAL = GLA_HEADS * GLA_DV
GLA_GATE_RANK = 16
GLA_GATE_NORMALIZER = 16.0
GLA_CHUNK = 64

RWKV_HEADS = 8
RWKV_HEAD = 64
RWKV_W = RWKV_HEADS * RWKV_HEAD
RWKV_DECAY_RANK = 64
RWKV_A_RANK = 64
RWKV_LN_EPS = 64e-5
RWKV_SHIFT = 3 * RWKV_W + RWKV_DECAY_RANK + RWKV_A_RANK

MIX0 = GLA_VAL + RWKV_W
SPLIT0 = [GLA_KEY, 2 * GLA_KEY, 2 * GLA_KEY + GLA_VAL,
          2 * GLA_KEY + GLA_VAL + GLA_GATE_RANK,
          2 * GLA_KEY + GLA_VAL + GLA_GATE_RANK + RWKV_SHIFT]
IN0 = 2 * GLA_KEY + GLA_VAL + GLA_GATE_RANK + RWKV_SHIFT + MIX0
SPLIT_RWKV = [RWKV_W, 2 * RWKV_W, 3 * RWKV_W, 3 * RWKV_W + RWKV_DECAY_RANK]

SWA_Q_HEADS = 16
SWA_KV_HEADS = 4
SWA_GROUP = SWA_Q_HEADS // SWA_KV_HEADS
SWA_HEAD = 64
WINDOW = 128
ROPE_DIMS = SWA_HEAD // 4
ROPE_THETA = 500000.0
MIX1 = SWA_Q_HEADS * SWA_HEAD
SWA_KV = SWA_KV_HEADS * SWA_HEAD
SWA_QKV = MIX1 + 2 * SWA_KV
IN1 = SWA_QKV + MIX1

kernel_name = "hybrid_gla_rwkv7_swa_sink_gated"

def rmsnorm(x, w, eps=NORM_EPS):
    xf = x.astype(jnp.float32)
    y = xf * lax.rsqrt(jnp.mean(xf * xf, axis=-1, keepdims=True) + eps)
    return (y * w.astype(jnp.float32)).astype(x.dtype)

def token_shift(t):
    return jnp.concatenate([jnp.zeros_like(t[:, :1]), t[:, :-1]], axis=1)

def gla_chunked(q, k, v, g):
    f32 = jnp.float32
    B, T, H, dk = q.shape
    dv = v.shape[-1]
    C = GLA_CHUNK
    NC = T // C
    q = (q.astype(f32) * (dk ** -0.5)).reshape(B, NC, C, H, dk)
    k = k.astype(f32).reshape(B, NC, C, H, dk)
    v = v.astype(f32).reshape(B, NC, C, H, dv)
    b = jnp.cumsum(g.astype(f32).reshape(B, NC, C, H, dk), axis=2)
    ref = b[:, :, C // 2:C // 2 + 1]
    att = jnp.einsum('bnihd,bnjhd->bnhij', q * jnp.exp(b - ref), k * jnp.exp(ref - b))
    causal = jnp.tril(jnp.ones((C, C), dtype=bool))
    att = jnp.where(causal, att, 0.0)
    o_intra = jnp.einsum('bnhij,bnjhv->bnihv', att, v)
    b_last = b[:, :, -1:]
    chunk_kv = jnp.einsum('bnjhd,bnjhv->nbhdv', k * jnp.exp(b_last - b), v)
    chunk_decay = jnp.exp(b_last[:, :, 0]).transpose(1, 0, 2, 3)

    def step(S, inp):
        kv, dec = inp
        return S * dec[..., None] + kv, S

    _, S_prev = lax.scan(step, jnp.zeros((B, H, dk, dv), f32), (chunk_kv, chunk_decay))
    o_inter = jnp.einsum('bnihd,nbhdv->bnihv', q * jnp.exp(b), S_prev)
    return (o_intra + o_inter).reshape(B, T, H, dv)

def rwkv7_scan(r, decay, k, v, a_vec, b_vec):
    B, T, H, N = r.shape

    def step(S, inp):
        r_t, w_t, k_t, v_t, a_t, b_t = inp
        sa = jnp.einsum('bhvk,bhk->bhv', S, a_t)
        S = S * w_t[:, :, None, :] + sa[..., None] * b_t[:, :, None, :] + v_t[..., None] * k_t[:, :, None, :]
        return S, jnp.einsum('bhvk,bhk->bhv', S, r_t)

    xs = (jnp.moveaxis(r, 1, 0), jnp.moveaxis(decay, 1, 0), jnp.moveaxis(k, 1, 0),
          jnp.moveaxis(v, 1, 0), jnp.moveaxis(a_vec, 1, 0), jnp.moveaxis(b_vec, 1, 0))
    _, out = lax.scan(step, jnp.zeros((B, H, N, N), jnp.float32), xs)
    return jnp.moveaxis(out, 0, 1)

def gla_rwkv_mixer(h, w_in, gk_up, gk_bias, gla_norm_w, mu, w0, w_up, a0, a_up,
                   k_k, k_a, r_k, ln_w, ln_b, w_out):
    f32 = jnp.float32
    B, T, _ = h.shape
    proj = h @ w_in
    gq, gk, gv, g_low, rw, gate = jnp.split(proj, SPLIT0, axis=-1)

    log_decay = jax.nn.log_sigmoid((g_low @ gk_up + gk_bias).astype(f32)) / GLA_GATE_NORMALIZER
    o_a = gla_chunked(gq.reshape(B, T, GLA_HEADS, GLA_DK), gk.reshape(B, T, GLA_HEADS, GLA_DK),
                      gv.reshape(B, T, GLA_HEADS, GLA_DV), log_decay.reshape(B, T, GLA_HEADS, GLA_DK))
    o_a = o_a * lax.rsqrt(jnp.mean(o_a * o_a, axis=-1, keepdims=True) + NORM_EPS) * gla_norm_w.astype(f32)
    o_a = o_a.reshape(B, T, GLA_VAL)

    rw = rw.astype(f32)
    rw = rw + (token_shift(rw) - rw) * mu.astype(f32)
    r, k, v, xw, xa = jnp.split(rw, SPLIT_RWKV, axis=-1)
    w = -jax.nn.softplus(-(w0.astype(f32) + jnp.tanh(xw) @ w_up.astype(f32))) - 0.5
    decay = jnp.exp(-jnp.exp(w))
    a = jax.nn.sigmoid(a0.astype(f32) + xa @ a_up.astype(f32))
    hs = (B, T, RWKV_HEADS, RWKV_HEAD)
    kk = (k * k_k.astype(f32)).reshape(hs)
    kk = kk / jnp.maximum(jnp.sqrt(jnp.sum(kk * kk, axis=-1, keepdims=True)), 1e-12)
    k = k * (1.0 + (a - 1.0) * k_a.astype(f32))
    r, k, v, decay, a = r.reshape(hs), k.reshape(hs), v.reshape(hs), decay.reshape(hs), a.reshape(hs)
    o_b = rwkv7_scan(r, decay, k, v, -kk, kk * a)
    mean = jnp.mean(o_b, axis=-1, keepdims=True)
    var = jnp.mean((o_b - mean) ** 2, axis=-1, keepdims=True)
    o_b = (o_b - mean) * lax.rsqrt(var + RWKV_LN_EPS) * ln_w.astype(f32).reshape(RWKV_HEADS, RWKV_HEAD) \
        + ln_b.astype(f32).reshape(RWKV_HEADS, RWKV_HEAD)
    o_b = o_b + jnp.sum(r * k * r_k.astype(f32), axis=-1, keepdims=True) * v
    o_b = o_b.reshape(B, T, RWKV_W)

    o = jnp.concatenate([o_a, o_b], axis=-1) * jax.nn.silu(gate.astype(f32))
    return (o.astype(h.dtype) @ w_out).astype(h.dtype)

def partial_rope(x, pos):
    f32 = jnp.float32
    half = ROPE_DIMS // 2
    inv_freq = ROPE_THETA ** (-jnp.arange(half, dtype=f32) / half)
    ang = pos.astype(f32)[:, None] * inv_freq
    cos = jnp.cos(ang)[None, :, None, :]
    sin = jnp.sin(ang)[None, :, None, :]
    xr = x[..., :ROPE_DIMS].astype(f32)
    x1, x2 = xr[..., :half], xr[..., half:]
    rot = jnp.concatenate([x1 * cos - x2 * sin, x2 * cos + x1 * sin], axis=-1)
    return jnp.concatenate([rot.astype(x.dtype), x[..., ROPE_DIMS:]], axis=-1)

def banded_sink_attention(q, k, v, sinks):
    f32 = jnp.float32
    B, T, _, hd = q.shape
    NB = T // WINDOW
    qb = q.astype(f32).reshape(B, NB, WINDOW, SWA_KV_HEADS, SWA_GROUP, hd) * (hd ** -0.5)

    def two_blocks(t):
        tb = t.astype(f32).reshape(B, NB, WINDOW, SWA_KV_HEADS, hd)
        prev = jnp.pad(tb[:, :-1], ((0, 0), (1, 0), (0, 0), (0, 0), (0, 0)))
        return jnp.concatenate([prev, tb], axis=2)

    kb, vb = two_blocks(k), two_blocks(v)
    s = jnp.einsum('bnqhgd,bnkhd->bnhgqk', qb, kb)
    qi = jnp.arange(WINDOW)[:, None]
    kj = jnp.arange(2 * WINDOW)[None, :]
    diff = qi + WINDOW - kj
    band = (diff >= 0) & (diff < WINDOW)
    valid = band[None] & ((jnp.arange(NB)[:, None, None] > 0) | (kj[None] >= WINDOW))
    s = jnp.where(valid[None, :, None, None], s, -jnp.inf)
    sink = sinks.astype(f32).reshape(SWA_KV_HEADS, SWA_GROUP)[None, None, :, :, None, None]
    m = jnp.maximum(jnp.max(s, axis=-1, keepdims=True), sink)
    p = jnp.exp(s - m)
    denom = jnp.sum(p, axis=-1, keepdims=True) + jnp.exp(sink - m)
    o = jnp.einsum('bnhgqk,bnkhd->bnqhgd', p / denom, vb)
    return o.reshape(B, T, SWA_Q_HEADS, hd)

def swa_mixer(h, w_in, b_in, sinks, w_out, b_out):
    f32 = jnp.float32
    B, T, _ = h.shape
    proj = h @ w_in
    qkv = proj[..., :SWA_QKV] + b_in
    gate = proj[..., SWA_QKV:]
    q, k, v = jnp.split(qkv, [MIX1, MIX1 + SWA_KV], axis=-1)
    pos = jnp.arange(T)
    q = partial_rope(q.reshape(B, T, SWA_Q_HEADS, SWA_HEAD), pos)
    k = partial_rope(k.reshape(B, T, SWA_KV_HEADS, SWA_HEAD), pos)
    v = v.reshape(B, T, SWA_KV_HEADS, SWA_HEAD)
    o = banded_sink_attention(q, k, v, sinks).reshape(B, T, MIX1)
    o = o * jax.nn.silu(gate.astype(f32))
    return (o.astype(h.dtype) @ w_out + b_out).astype(h.dtype)

def setup_inputs(seed: int = 0) -> dict:
    key = jax.random.key(seed)
    ks = jax.random.split(key, 24)
    f32 = jnp.float32
    nrm = lambda k, s: jax.random.normal(k, s, f32)
    return {
        "x": nrm(ks[0], (BATCH, SEQ, D_MODEL)),
        "norm_w": 1.0 + 0.02 * nrm(ks[1], (DEPTH, D_MODEL)),
        "w_in0": nrm(ks[2], (N_EVEN, D_MODEL, IN0)) * D_MODEL ** -0.5,
        "gla_gk_up": nrm(ks[3], (N_EVEN, GLA_GATE_RANK, GLA_KEY)) * GLA_GATE_RANK ** -0.5,
        "gla_gk_bias": 0.1 * nrm(ks[4], (N_EVEN, GLA_KEY)),
        "gla_norm_w": 1.0 + 0.02 * nrm(ks[5], (N_EVEN, GLA_DV)),
        "rwkv_mu": jax.random.uniform(ks[6], (N_EVEN, RWKV_SHIFT), f32),
        "rwkv_w0": jax.random.uniform(ks[7], (N_EVEN, RWKV_W), f32, -4.0, 1.0),
        "rwkv_w_up": nrm(ks[8], (N_EVEN, RWKV_DECAY_RANK, RWKV_W)) * 0.5 * RWKV_DECAY_RANK ** -0.5,
        "rwkv_a0": 0.2 * nrm(ks[9], (N_EVEN, RWKV_W)),
        "rwkv_a_up": nrm(ks[10], (N_EVEN, RWKV_A_RANK, RWKV_W)) * 0.5 * RWKV_A_RANK ** -0.5,
        "rwkv_k_k": 0.85 + 0.05 * nrm(ks[11], (N_EVEN, RWKV_W)),
        "rwkv_k_a": 1.0 + 0.05 * nrm(ks[12], (N_EVEN, RWKV_W)),
        "rwkv_r_k": 0.1 * nrm(ks[13], (N_EVEN, RWKV_HEADS, RWKV_HEAD)),
        "rwkv_ln_w": 1.0 + 0.02 * nrm(ks[14], (N_EVEN, RWKV_W)),
        "rwkv_ln_b": 0.02 * nrm(ks[15], (N_EVEN, RWKV_W)),
        "w_out0": nrm(ks[16], (N_EVEN, MIX0, D_MODEL)) * MIX0 ** -0.5,
        "w_in1": nrm(ks[17], (N_ODD, D_MODEL, IN1)) * D_MODEL ** -0.5,
        "b_in1": 0.02 * nrm(ks[18], (N_ODD, SWA_QKV)),
        "attn_sinks": 0.5 * nrm(ks[19], (N_ODD, SWA_Q_HEADS)),
        "w_out1": nrm(ks[20], (N_ODD, MIX1, D_MODEL)) * MIX1 ** -0.5,
        "b_out1": 0.02 * nrm(ks[21], (N_ODD, D_MODEL)),
        "final_norm_w": 1.0 + 0.02 * nrm(ks[22], (D_MODEL,)),
    }

def reference(x, norm_w, w_in0, gla_gk_up, gla_gk_bias, gla_norm_w, rwkv_mu, rwkv_w0, rwkv_w_up,
              rwkv_a0, rwkv_a_up, rwkv_k_k, rwkv_k_a, rwkv_r_k, rwkv_ln_w, rwkv_ln_b, w_out0,
              w_in1, b_in1, attn_sinks, w_out1, b_out1, final_norm_w):
    h = x
    for layer in range(DEPTH):
        i = layer // 2
        hn = rmsnorm(h, norm_w[layer])
        if layer % 2 == 0:
            h = h + gla_rwkv_mixer(hn, w_in0[i], gla_gk_up[i], gla_gk_bias[i], gla_norm_w[i],
                                   rwkv_mu[i], rwkv_w0[i], rwkv_w_up[i], rwkv_a0[i], rwkv_a_up[i],
                                   rwkv_k_k[i], rwkv_k_a[i], rwkv_r_k[i], rwkv_ln_w[i], rwkv_ln_b[i],
                                   w_out0[i])
        else:
            h = h + swa_mixer(hn, w_in1[i], b_in1[i], attn_sinks[i], w_out1[i], b_out1[i])
    return rmsnorm(h, final_norm_w)


_drawn_inputs = setup_inputs


def setup_inputs(seed=0):
    import zlib

    import numpy as np

    out = dict(_drawn_inputs(seed))
    spreads = {}
    factors = {'gla_gk_bias': 3.512,
     'gla_norm_w': 101.02,
     'rwkv_w_up': 3.812,
     'rwkv_k_k': 71.96,
     'rwkv_k_a': 2.891,
     'rwkv_ln_w': 128.466,
     'rwkv_ln_b': 118.995,
     'b_in1': 106.64,
     'attn_sinks': 200.0,
     'b_out1': 47.891,
     'final_norm_w': 22.606,
     'rwkv_r_k': 8.0,
     'w_in1': 4.582,
     'w_out1': 4.341}
    for name, (base, spread) in spreads.items():
        noise = np.random.default_rng([zlib.crc32(name.encode()), seed]).standard_normal(out[name].shape)
        drawn = base * np.exp(spread * noise) if base else spread * noise
        out[name] = __import__('jax').numpy.asarray(drawn.astype(out[name].dtype))
    for name, factor in factors.items():
        out[name] = (out[name] * factor).astype(out[name].dtype)
    return out
```

```python
from contextlib import ExitStack

import concourse.bass as bass
from concourse import mybir

F = mybir.dt.float32
I32 = mybir.dt.int32
ALU = mybir.AluOpType
ACT = mybir.ActivationFunctionType
AX = mybir.AxisListType
ds = bass.ds

P = 128
T = 1024
D = 1024
KT = D // P
TT = T // P
C = 64
NC = T // C
HB = 512
PAIRS = 4
GP = 2
LEVELS = 6
EPS = 1e-5
LN_EPS = 64e-5
DECAY = 0.6065306597126334
NORMALIZER = 16.0
GLA_SCALE = 0.125
Q_TILES = 8
NEG = -1.0e30

_COLS = {}
_at = 0
for _name, _n in (("norm0", 8), ("norm1", 8), ("mu_x", 1), ("mu_k", 4), ("mu_r", 4), ("mu_v", 4), ("w0", 4),
                  ("a0", 4), ("k_k", 4), ("k_a", 4), ("r_k", 4), ("ln_w", 4), ("ln_b", 4), ("gk_bias", 2),
                  ("gla_norm", 1), ("b_q", 8), ("b_k", 2), ("sinks", 16)):
    _COLS[_name] = _at
    _at += _n
NPAR = _at

W0_X = 0
W0_PAIR = 1
W0_GLOW = 13
W0_GLA = 14
W0_GATE = 22
W0_TILES = 30
W1_Q, W1_K, W1_GATE, W1_TILES = 0, 8, 10, 18


def trunk(nc, x, w0t, wup, gkup, wout0, w1t, wv1, bv1, wout1, par, bout1, fnorm, ident_d, istack_d, bdones_d,
          maska_d, scan_d, maskd_d, maskb_d, cos_d, sin_d, band_d, out):
    root = ExitStack()
    with root:
        def sb(name, shape, dt=F, ctx=root):
            return ctx.enter_context(nc.sbuf_tensor(name, shape, dt))

        def sem(name):
            return root.enter_context(nc.semaphore(name))

        PS = [root.enter_context(nc.psum_tensor(f"ps{i}", [P, HB], F)) for i in range(8)]

        par_sb = sb("par", [P, NPAR])
        ident = sb("ident", [P, P])
        istack = sb("istack", [P, C])
        small = sb("small", [P, 64])

        def col(name, i=0, n=1):
            return par_sb[:, _COLS[name] + i:_COLS[name] + i + n]

        const_in = sem("const_in")
        const2_in = sem("const2_in")
        row_in = [sem(f"row_in{t}") for t in range(TT)]
        turns = [0]

        def row_turn():
            turns[0] += 1
            return turns[0]


        def norm_transpose(tag, rows, normed, scratch, dst, norm_name, load=None, extra_load=None, next_loads=None):
            turn = row_turn()
            squared = sem(f"{tag}_squared")
            rooted = sem(f"{tag}_rooted")
            inverted = sem(f"{tag}_inverted")
            scaled = sem(f"{tag}_scaled")
            turned = sem(f"{tag}_turned")
            kept_act = sem(f"{tag}_kept_act")
            kept_dve = sem(f"{tag}_kept_dve")
            eps_set = sem(f"{tag}_eps_set")
            ms, sd, rs, eps = small[:, 0:8], small[:, 8:16], small[:, 16:24], small[:, 24:25]
            with nc.Block() as block:
                @block.sync
                def _(sp):
                    if load is not None:
                        for t in range(TT):
                            sp.dma_start(rows[:, t, :], load[:, t, :]).then_inc(row_in[t], 16)
                    if extra_load:
                        extra_load(sp)

                @block.scalar
                def _(act):
                    act.wait_ge(eps_set, 1)
                    for t in range(TT):
                        if load is not None:
                            act.wait_ge(row_in[t], 16 * turn)
                        if t:
                            act.wait_ge(squared, t)
                        act.activation(scratch, rows[:, t, :], ACT.Square, accum_out=ms[:, t:t + 1]).then_inc(squared, 1)
                        act.wait_ge(squared, t + 1)
                        act.activation(sd[:, t:t + 1], ms[:, t:t + 1], ACT.Sqrt, bias=eps, scale=1.0 / D).then_inc(rooted, 1)
                    act.wait_ge(const_in, 16 * 3)
                    for g in range(1, 16, 2):
                        half, k = divmod(g, KT)
                        act.wait_ge(turned, g + 1)
                        act.activation(dst[:, k, half * HB:(half + 1) * HB], PS[g % 4][:], ACT.Copy,
                                       scale=col(norm_name, k)).then_inc(kept_act, 1)

                @block.vector
                def _(dve):
                    dve.memset(eps, EPS).then_inc(eps_set, 1)
                    for t in range(TT):
                        dve.wait_ge(rooted, t + 1)
                        dve.reciprocal(rs[:, t:t + 1], sd[:, t:t + 1]).then_inc(inverted, 1)
                        dve.wait_ge(inverted, t + 1)
                        dve.tensor_scalar(normed[:, t, :], rows[:, t, :], rs[:, t:t + 1], None, ALU.mult).then_inc(scaled, 1)
                        if t == 3:
                            dve.wait_ge(const_in, 16 * 3)
                    for g in range(0, 16, 2):
                        half, k = divmod(g, KT)
                        dve.wait_ge(turned, g + 1)
                        dve.tensor_scalar(dst[:, k, half * HB:(half + 1) * HB], PS[g % 4][:], col(norm_name, k), None,
                                          ALU.mult).then_inc(kept_dve, 1)

                @block.tensor
                def _(pe):
                    pe.wait_ge(const_in, 16 * 3)
                    for g in range(16):
                        half, k = divmod(g, KT)
                        if g % KT == 0:
                            pe.wait_ge(scaled, 4 * half + 4)
                        if g >= 4:
                            pe.wait_ge(kept_act if g % 2 else kept_dve, (g - 4) // 2 + 1)
                        for j in range(4):
                            last = pe.transpose(PS[g % 4][:, j * P:(j + 1) * P],
                                                normed[:, 4 * half + j, k * P:(k + 1) * P], ident[:])
                        last.then_inc(turned, 1)

        layer0 = ExitStack()
        with layer0:
            AR = sb("AR", [P, 2, PAIRS, T], ctx=layer0)
            BK = sb("BK", [P, 2, PAIRS, T], ctx=layer0)
            VT = sb("VT", [P, PAIRS, T], ctx=layer0)
            QK = sb("QK", [P, 2, GP, T], ctx=layer0)
            GV = sb("GV", [P, 4, T], ctx=layer0)
            SG = sb("SG", [P, KT, T], ctx=layer0)
            bdones = sb("bdones", [P, P], ctx=layer0)
            G = sb("G", [P, PAIRS, NC], ctx=layer0)
            GG = sb("GG", [P, GP, NC], ctx=layer0)
            half1 = ExitStack()
            with half1:
                HN = sb("HN", [P, KT, T], ctx=half1)
                WB = sb("WB", [P, 2, KT, P], ctx=half1)
                scanm = sb("scanm", [P, T], ctx=half1)
                RAW = sb("RAW", [P, 2, T + 1], ctx=half1)
                wup_sb = VT[:, 3, 0:512]
                gk_sb = sb("gk_sb", [16, 256], ctx=half1)

                def const_loads(sp):
                    sp.dma_start(bdones[:], bdones_d).then_inc(const2_in, 16)
                    sp.dma_start(scanm[:], scan_d).then_inc(const2_in, 16)
                    sp.dma_start(gk_sb[:], gkup).then_inc(const2_in, 16)
                    sp.dma_start(wup_sb, wup).then_inc(const2_in, 16)

                with nc.Block() as block:
                    @block.sync
                    def _(sp):
                        sp.dma_start(par_sb[:], par).then_inc(const_in, 16)
                        sp.dma_start(ident[:], ident_d).then_inc(const_in, 16)
                        sp.dma_start(istack[:], istack_d).then_inc(const_in, 16)

                x_rows = AR[:, :, :, :].rearrange("p a b t -> p (a b) t")
                norm_transpose("n0", x_rows, x_rows, BK[:, 0, 0, :], HN, "norm0",
                               load=x.rearrange("(t p) d -> p t d", p=P), extra_load=const_loads)

                project0(nc, sem, PS, HN, WB, wup_sb, gk_sb, RAW, scanm, AR, BK, VT, QK, GV, SG, bdones, G, GG,
                         small, w0t, col, const2_in)
            loop = ExitStack()
            with loop:
                chunks0(nc, sb, sem, loop, PS, AR, BK, VT, QK, GV, G, GG, small, ident, istack, maska_d, maskd_d,
                        maskb_d)
            tail = ExitStack()
            with tail:
                mix0(nc, sb, sem, tail, PS, AR, BK, VT, GV, SG, bdones, col)
            H1 = sb("H1", [P, TT, D], ctx=layer0)
            WO = BK[:, :, :, :].rearrange("p a b t -> p (a b) t")
            XR = AR[:, :, :, :].rearrange("p a b t -> p (a b) t")
            out_project(nc, sem, "o0", PS, SG, WO, XR, H1, wout0, x.rearrange("(t p) d -> p t d", p=P), None,
                        row_in=row_in, turn=row_turn())
            h1_dram = nc.dram_tensor("h1_dram", (P, TT, D), F, kind="Internal").ap()
            h1_out = sem("h1_out")
            with nc.Block() as block:
                @block.sync
                def _(sp):
                    sp.dma_start(h1_dram, H1[:]).then_inc(h1_out, 16)
                    sp.wait_ge(h1_out, 16)

        layer1 = ExitStack()
        with layer1:
            H = sb("H", [P, TT, D], ctx=layer1)
            QT = sb("QT", [P, Q_TILES, T], ctx=layer1)
            KTT = sb("KTT", [P, 2, T + P], ctx=layer1)
            V1 = sb("V1", [P, TT + 1, 256], ctx=layer1)
            SG1 = sb("SG1", [P, KT, T], ctx=layer1)
            HN1 = sb("HN1", [P, KT, T], ctx=layer1)
            proj = ExitStack()
            with proj:
                W1 = sb("W1", [P, 2, KT, P], ctx=proj)
                COS = sb("COS", [P, T], ctx=proj)
                SIN = sb("SIN", [P, T], ctx=proj)
                SW = sb("SW", [P, T], ctx=proj)
                WV = sb("WV", [P, KT, 256], ctx=proj)
                BV = sb("BV", [P, 256], ctx=proj)
                rope_in = sem("rope_in")

                def rope_loads(sp):
                    sp.dma_start(COS[:], cos_d).then_inc(rope_in, 16)
                    sp.dma_start(SIN[:], sin_d).then_inc(rope_in, 16)
                    sp.dma_start(WV[:], wv1).then_inc(rope_in, 16)
                    sp.dma_start(BV[:], bv1).then_inc(rope_in, 16)

                norm_transpose("n1", H, QT, SG1[:, 0, :], HN1, "norm1", load=h1_dram, extra_load=rope_loads)
                project1(nc, sem, PS, HN1, W1, COS, SIN, SW, WV, BV, QT, KTT, V1, SG1, small, w1t,
                         col, rope_in)
            att = ExitStack()
            with att:
                attend(nc, sb, sem, att, PS, QT, KTT, V1, SG1, band_d, small, col, ident)
            outp = ExitStack()
            with outp:
                WO1 = HN1
                BO = sb("BO", [P, D], ctx=outp)
                FN = sb("FN", [P, D], ctx=outp)
                SQ = sb("SQ", [P, D], ctx=outp)
                out_project(nc, sem, "o1", PS, SG1, WO1, H, QT, wout1, None, (BO, bout1),
                            dict(fn=FN, fnorm=fnorm, small=small, scratch=SQ[:],
                                 out=out.rearrange("(t p) d -> p t d", p=P)))


def project0(nc, sem, PS, HN, WB, wup_sb, gk_sb, RAW, scanm, AR, BK, VT, QK, GV, SG, bdones, G, GG, small, w0t,
             col, const_in):
    mixd, kmix, kk, sq = (QK[:, i // 2, i % 2, :] for i in range(4))
    nrm, cum, e2, e1a = (GV[:, i, :] for i in range(4))
    nka, mid = small[:, 32:36], small[:, 40:56]
    tile_bank = [PS[0:2], PS[2:4]]
    w_in = [sem("w_in0"), sem("w_in1")]
    tile_done = sem("tile_done")
    tile_kept = sem("tile_kept")
    mixed = sem("mixed")
    xw_tanh = sem("xw_tanh")
    low_done = sem("low_done")
    low_kept = sem("low_kept")
    kk_raw = sem("kk_raw")
    kk_sq = sem("kk_sq")
    kk_sum = sem("kk_sum")
    kk_nrm = sem("kk_nrm")
    rel_done = sem("rel_done")
    exps = sem("exps")
    pair_done = sem("pair_done")
    step = sem("p0_step")
    chain = sem("p0_chain")
    pad = sem("p0_pad")
    glow_kept = sem("glow_kept")
    gz_done = sem("gz_done")
    gz_kept = sem("gz_kept")
    gz_abs = sem("gz_abs")
    gz_step = sem("gz_step")
    g_rel = sem("g_rel")
    g_exp = sem("g_exp")
    g_scaled = sem("g_scaled")

    with nc.Block() as block:
        @block.sync
        def _(sp):
            for n in range(2):
                sp.dma_start(WB[:, n], w0t[n]).then_inc(w_in[n], 16)
            with sp.Fori(1, W0_TILES // 2) as i:
                for n in range(2):
                    sp.wait_ge(tile_done, 2 * i + (n - 1))
                    sp.sem_inc(step, 1)
                    sp.dma_start(WB[:, n], w0t[ds(2 * i + n, 1)].rearrange("o p k c -> (o p) k c")).then_inc(w_in[n], 16)

        @block.tensor
        def _(pe):
            def tile(n, par, turn=None):
                pe.wait_ge(w_in[par], 16 * (n // 2 if turn is None else turn) + 16)
                if not isinstance(n, int) or n >= 2:
                    pe.wait_ge(tile_kept, n - 1)
                for h in range(2):
                    for k in range(KT):
                        last = pe.matmul(tile_bank[par][h][:], WB[:, par, k, :], HN[:, k, h * HB:(h + 1) * HB],
                                         start=(k == 0), stop=(k == KT - 1))
                last.then_inc(tile_done, 1)

            tile(0, 0)
            pe.wait_ge(const_in, 16 * 4)
            pe.wait_ge(xw_tanh, 1)
            for j in range(8):
                lo = 0 if j < 4 else C
                if j >= 2:
                    pe.wait_ge(low_kept, j - 1)
                for h in range(2):
                    last = pe.matmul(PS[4 + 2 * (j % 2) + h][:], wup_sb[lo:lo + C, (j % 4) * P:(j % 4 + 1) * P],
                                     mixd[lo:lo + C, h * HB:(h + 1) * HB], start=True, stop=True)
                last.then_inc(low_done, 1)
            for p in range(PAIRS):
                for j in range(3):
                    tile(3 * p + j + 1, (3 * p + j + 1) % 2)
                    if j == 1:
                        pe.wait_ge(kk_sq, p + 1)
                        if p:
                            pe.wait_ge(kk_nrm, p)
                        for h in range(2):
                            last = pe.matmul(PS[4 + h][:], bdones[:], sq[:, h * HB:(h + 1) * HB], start=True, stop=True)
                        last.then_inc(kk_sum, 1)
            tile(W0_GLOW, W0_GLOW % 2)
            pe.wait_ge(glow_kept, 1)
            for j in range(GP):
                for h in range(2):
                    last = pe.matmul(PS[4 + 2 * j + h][:], gk_sb[:, j * P:(j + 1) * P], mixd[0:16, h * HB:(h + 1) * HB],
                                     start=True, stop=True)
                last.then_inc(gz_done, 1)
            with pe.Fori(0, (W0_TILES - W0_GLA) // 2) as i:
                for n in range(2):
                    tile(2 * i + (W0_GLA + n), n, i + W0_GLA // 2)

        @block.scalar
        def _(act):
            def keep(n, dst, func, **kw):
                act.wait_ge(tile_done, n + 1)
                for h in range(2):
                    ins = act.activation(dst[:, h * HB:(h + 1) * HB], tile_bank[n % 2][h][:], func, **kw)
                ins.then_inc(tile_kept, 1)

            def keep_raw(n):
                if n >= 2:
                    act.wait_ge(mixed, n - 1)
                keep(n, RAW[:, n % 2, 1:T + 1], ACT.Copy)

            act.wait_ge(pad, 1)
            keep_raw(0)
            act.wait_ge(mixed, 1)
            act.activation(mixd[0:C, :], mixd[0:C, :], ACT.Tanh).then_inc(xw_tanh, 1)
            for j in range(8):
                act.wait_ge(low_done, j + 1)
                for h in range(2):
                    ins = act.activation(SG[:, j, h * HB:(h + 1) * HB], PS[4 + 2 * (j % 2) + h][:], ACT.Sigmoid,
                                         bias=col("w0", j) if j < 4 else col("a0", j - 4))
                ins.then_inc(low_kept, 1)
            for p in range(PAIRS):
                keep_raw(1 + 3 * p)
                act.wait_ge(kk_raw, p + 1)
                act.activation(sq, kk, ACT.Square).then_inc(kk_sq, 1)
                keep_raw(2 + 3 * p)
                act.wait_ge(rel_done, p + 1)
                act.activation(G[:, p, :], G[:, p, :], ACT.Exp, scale=-DECAY)
                act.activation(e2, cum, ACT.Exp, scale=DECAY)
                act.activation(e1a, e1a, ACT.Exp, scale=-DECAY)
                act.activation(cum, cum, ACT.Exp, scale=-DECAY).then_inc(exps, 1)
                act.wait_ge(kk_sum, p + 1)
                for h in range(2):
                    ins = act.activation(nrm[:, h * HB:(h + 1) * HB], PS[4 + h][:], ACT.Sqrt)
                ins.then_inc(kk_nrm, 1)
                keep_raw(3 + 3 * p)
            act.wait_ge(pair_done, PAIRS)
            act.wait_ge(mixed, 3 * PAIRS + 1)
            act.wait_ge(tile_done, W0_GLOW + 1)
            for h in range(2):
                ins = act.activation(mixd[0:16, h * HB:(h + 1) * HB], tile_bank[W0_GLOW % 2][h][0:16, :], ACT.Copy)
            ins.then_inc(glow_kept, 1)
            act.wait_ge(glow_kept, 1)
            act.activation(small[:, 57:58], small[:, 57:58], ACT.Copy).then_inc(tile_kept, 1)
            for j in range(GP):
                z, l = (nrm, cum)[j], (e2, e1a)[j]
                act.wait_ge(gz_done, j + 1)
                for h in range(2):
                    ins = act.activation(z[:, h * HB:(h + 1) * HB], PS[4 + 2 * j + h][:], ACT.Identity, bias=col("gk_bias", j))
                ins.then_inc(gz_kept, 1)
                act.wait_ge(gz_abs, j + 1)
                act.activation(l, l, ACT.Exp, scale=-1.0).then_inc(gz_step, 1)
                act.wait_ge(gz_step, 2 * j + 1)
                act.activation(l, l, ACT.Ln, bias=1.0).then_inc(gz_step, 1)
            for j in range(GP):
                z, l = (nrm, cum)[j], (e2, e1a)[j]
                act.wait_ge(g_rel, j + 1)
                act.activation(l, z, ACT.Exp, scale=-1.0 / NORMALIZER)
                act.activation(GG[:, j, :], GG[:, j, :], ACT.Exp, scale=1.0 / NORMALIZER)
                act.activation(z, z, ACT.Exp, scale=1.0 / NORMALIZER).then_inc(g_exp, 1)
            for j in range(4):
                keep(W0_GLA + j, QK[:, j // 2, j % 2, :], ACT.Copy, scale=GLA_SCALE if j < 2 else 1.0)
            act.wait_ge(g_scaled, 4)
            for j in range(4):
                keep(W0_GLA + 4 + j, GV[:, j, :], ACT.Copy)
            for j in range(KT):
                keep(W0_GATE + j, SG[:, j, :], ACT.Silu)

        @block.vector
        def _(dve):
            count = [0]

            def link(ins):
                count[0] += 1
                ins.then_inc(chain, 1)
                dve.wait_ge(chain, count[0])

            def mix(n, mu, dst, t=mixd):
                raw = RAW[:, n % 2, :]
                dve.wait_ge(tile_kept, n + 1)
                link(dve.tensor_tensor(t, raw[:, 0:T], raw[:, 1:T + 1], ALU.subtract))
                dve.scalar_tensor_tensor(out=dst, in0=t, scalar=mu, in1=raw[:, 1:T + 1],
                                         op0=ALU.mult, op1=ALU.add).then_inc(mixed, 1)
                dve.wait_ge(mixed, n + 1)

            def by_chunk(ap):
                return ap.rearrange("p (c t) -> p c t", t=C)

            def relative(cs, dst, g):
                v = by_chunk(cs)
                link(dve.tensor_copy(mid, v[:, :, C // 2]))
                link(dve.tensor_tensor(g[:, 0:NC - 1], mid[:, 1:NC], mid[:, 0:NC - 1], ALU.subtract))
                link(dve.tensor_tensor(g[:, 0:NC - 1], g[:, 0:NC - 1], v[:, 0:NC - 1, C - 1], ALU.add))
                link(dve.tensor_tensor(by_chunk(dst), v, mid.unsqueeze(2).to_broadcast([P, NC, C]), ALU.subtract))

            dve.memset(small[:, 56:64], 0.0)
            dve.memset(RAW[:, :, 0:1], 0.0).then_inc(pad, 1)
            link(dve.memset(G[:], 0.0))
            link(dve.memset(GG[:], 0.0))
            dve.wait_ge(const_in, 16 * 4)
            link(dve.tensor_scalar(nka, col("k_a", 0, 4), -1.0, 1.0, ALU.mult, ALU.add))
            mix(0, col("mu_x"), mixd, kmix)
            dve.wait_ge(low_kept, 8)
            for p in range(PAIRS):
                sw, sa = SG[:, p, :], SG[:, 4 + p, :]
                link(dve.tensor_tensor_scan(cum, scanm[:], sw, 0.0, ALU.mult, ALU.add))
                relative(cum, cum, G[:, p, :])
                dve.tensor_tensor(e1a, cum, sw, ALU.subtract).then_inc(rel_done, 1)
                mix(1 + 3 * p, col("mu_k", p), kmix)
                dve.tensor_scalar(kk, kmix, col("k_k", p), None, ALU.mult).then_inc(kk_raw, 1)
                link(dve.tensor_scalar(mixd, sa, col("k_a", p), nka[:, p:p + 1], ALU.mult, ALU.add))
                link(dve.tensor_tensor(kmix, kmix, mixd, ALU.mult))
                dve.wait_ge(exps, p + 1)
                link(dve.tensor_tensor(BK[:, 1, p, :], kmix, e2, ALU.mult))
                mix(2 + 3 * p, col("mu_r", p), kmix)
                link(dve.tensor_tensor(AR[:, 1, p, :], kmix, cum, ALU.mult))
                dve.wait_ge(kk_nrm, p + 1)
                link(dve.tensor_scalar(nrm, nrm, 1e-12, None, ALU.max))
                link(dve.reciprocal(nrm, nrm))
                link(dve.tensor_tensor(kk, kk, nrm, ALU.mult))
                link(dve.scalar_tensor_tensor(out=AR[:, 0, p, :], in0=kk, scalar=-1.0, in1=e1a,
                                              op0=ALU.mult, op1=ALU.mult))
                link(dve.tensor_tensor(kk, kk, sa, ALU.mult))
                dve.tensor_tensor(BK[:, 0, p, :], kk, e2, ALU.mult).then_inc(pair_done, 1)
                dve.wait_ge(pair_done, p + 1)
                mix(3 + 3 * p, col("mu_v", p), VT[:, p, :])
            for j in range(GP):
                z, l = (nrm, cum)[j], (e2, e1a)[j]
                dve.wait_ge(gz_kept, j + 1)
                dve.scalar_tensor_tensor(out=l, in0=z, scalar=-1.0, in1=z, op0=ALU.mult, op1=ALU.max).then_inc(gz_abs, 1)
                dve.wait_ge(gz_step, 2 * j + 2)
                link(dve.scalar_tensor_tensor(out=z, in0=z, scalar=0.0, in1=l, op0=ALU.min, op1=ALU.subtract))
                link(dve.tensor_tensor_scan(l, scanm[:], z, 0.0, ALU.mult, ALU.add))
                relative(l, z, GG[:, j, :])
                dve.tensor_copy(mid, mid).then_inc(g_rel, 1)
            for j in range(4):
                dve.wait_ge(tile_kept, W0_GLA + j + 1)
                dve.wait_ge(g_exp, GP)
                e = (nrm, cum)[j % 2] if j < 2 else (e2, e1a)[j % 2]
                qk = QK[:, j // 2, j % 2, :]
                dve.tensor_tensor(qk, qk, e, ALU.mult).then_inc(g_scaled, 1)


def chunks0(nc, sb, sem, ctx, PS, AR, BK, VT, QK, GV, G, GG, small, ident, istack, maska_d, maskd_d, maskb_d):
    def buf(name, shape, dt=F):
        return sb(name, shape, dt, ctx=ctx)

    maska = buf("maska", [P, 2, C])
    maskd = buf("maskd", [P, LEVELS, C], I32)
    maskb = buf("maskb", [P, LEVELS, 2, C], I32)
    RS, AS, BS, KS, VS = (buf(n, [P, PAIRS, 2, C]) for n in ("RS", "AS", "BS", "KS", "VS"))
    AB = buf("AB", [P, 2, PAIRS, 2, C])
    AK = buf("AK", [P, 2, PAIRS, 2, C])
    TM = [buf(f"TM{l}", [P, PAIRS, C]) for l in range(LEVELS)]
    TB = [buf(f"TB{l}", [P, PAIRS, 2, C]) for l in range(LEVELS)]
    X = buf("X", [P, PAIRS, C])
    XT = buf("XT", [P, PAIRS, 2, C])
    RR, U, S, V = (buf(n, [P, PAIRS, C]) for n in ("RR", "U", "S", "V"))
    OB = buf("OB", [P, PAIRS, 2, C])
    OC = buf("OC", [P, PAIRS, C])
    st6, mv = buf("st6", [P, PAIRS, 6]), buf("mv", [P, PAIRS, 2])
    lsd, grs = small[:, 0:4], small[:, 8:10]
    leps, geps = small[:, 12:13], small[:, 13:14]
    gss = small[:, 14:16]
    GQS, GKS = (buf(n, [P, GP, 2, C]) for n in ("GQS", "GKS"))
    GVS = buf("GVS", [P, GP, 2, C])
    GA = buf("GA", [P, GP, 2, C])
    GVT, GS, GO = (buf(n, [P, GP, P]) for n in ("GVT", "GS", "GO"))
    GSQ = buf("GSQ", [P, P])

    names = ("masks_in init staged staged_rv g_staged "
             "b_prod k_prod a_prod v_prod k_turn b_turn t_prod x_prod xt_prod r_prod u_prod o_prod m_prod ot_prod step halves_staged "
             "ab_kept ak_kept x_kept joined xt_kept v_kept kt_kept bt_kept r_kept u_kept s_kept "
             "stats rooted ob_kept out_kept "
             "g_att g_turn g_prod g_ot g_att_kept g_turn_kept g_kept g_rooted g_norm g_out_kept chain act_chain")
    s = {n: sem("c_" + n) for n in names.split()}

    def halves():
        return ((h, slice(h * C, (h + 1) * C)) for h in range(2))

    def after(eng, name, n, plain=False):
        if not isinstance(n, int) or n > 0:
            eng.wait_ge(s[name], n)
            if plain:
                eng.sem_inc(s["step"], 1)

    def over_chunks(eng, body):
        body(0)
        with eng.Fori(1, NC) as c:
            body(c)

    with nc.Block() as block:
        @block.sync
        def _(sp):
            sp.dma_start(maska[:], maska_d).then_inc(s["masks_in"], 16)
            sp.dma_start(maskd[:], maskd_d).then_inc(s["masks_in"], 16)
            sp.dma_start(maskb[:], maskb_d).then_inc(s["masks_in"], 16)

        @block.gpsimd
        def _(pool):
            for b in (RS, AS, BS, KS, VS, OB, GQS, GKS, GA):
                pool.memset(b[:], 0.0)
            for b in (AB, AK):
                pool.memset(b[:], 0.0)
            for b in TB:
                pool.tensor_copy(b[:].rearrange("p q h t -> p q (h t)"), ident[:].unsqueeze(1).to_broadcast([P, PAIRS, P]))
            for b in TM:
                pool.tensor_copy(b[:], istack[:].unsqueeze(1).to_broadcast([P, PAIRS, C]))
            pool.memset(S[:], 0.0)
            pool.memset(GS[:], 0.0)
            pool.memset(leps, LN_EPS)
            pool.memset(geps, EPS).then_inc(s["init"], 1)
            pool.wait_ge(s["init"], 1)

            def body(c):
                at = ds(c * C, C)

                def stage(dst, src, done):
                    for h, rows in halves():
                        ins = pool.tensor_copy(dst[rows, :, h, :], src[rows, :, at])
                    if done:
                        ins.then_inc(s[done], 1)

                after(pool, "m_prod", c)
                stage(BS, BK[:, 0], None)
                stage(AS, AR[:, 0], None)
                stage(KS, BK[:, 1], "staged")
                stage(VS, VT, None)
                stage(RS, AR[:, 1], "staged_rv")
                after(pool, "g_prod", c)
                stage(GQS, QK[:, 0], None)
                stage(GKS, QK[:, 1], "halves_staged")
                pool.wait_ge(s["halves_staged"], c + 1)
                pool.tensor_copy(GVS[:].rearrange("p q h t -> p (q h) t"), GV[:, :, at]).then_inc(s["g_staged"], 1)
                pool.wait_ge(s["g_staged"], c + 1)

            over_chunks(pool, body)

        @block.tensor
        def _(pe):
            def each(pairs, bank, width, base, products, done):
                n = len(products(0))
                for q in pairs:
                    for i, (lhsT, rhs) in enumerate(products(q)):
                        last = pe.matmul(PS[bank][:, base + q * width:base + (q + 1) * width], lhsT, rhs,
                                         start=(i == 0), stop=(i == n - 1))
                if done:
                    last.then_inc(s[done], 1)

            R4, R2 = range(PAIRS), range(GP)

            def body(c):
                at = ds(c * C, C)
                after(pe, "staged", c + 1)
                each(R4, 0, P, 0, lambda q: [(BS[:, q], AR[:, :, q, at])], "b_prod")
                each(R4, 2, C, 0, lambda q: [(AS[:, q], BK[:, 0, q, at])], "a_prod")
                each(R4, 1, P, 0, lambda q: [(KS[:, q], AR[:, :, q, at])], "k_prod")
                after(pe, "staged_rv", c + 1)
                each(R4, 3, C, 0, lambda q: [(VS[:, q], istack[:])], "v_prod")
                for q in R4:
                    last = pe.transpose(PS[5][:, q * P:(q + 1) * P], KS[:, q], ident[:])
                last.then_inc(s["k_turn"], 1)
                after(pe, "out_kept", c)
                for q in R4:
                    last = pe.transpose(PS[6][:, q * P:(q + 1) * P], BS[:, q], ident[:])
                last.then_inc(s["b_turn"], 1)
                after(pe, "g_staged", c + 1)
                after(pe, "g_out_kept", c)
                each(R2, 7, C, 0, lambda q: [(GKS[:, q], QK[:, 0, q, at])], "g_att")
                after(pe, "ab_kept", c + 1)
                for l in range(1, LEVELS):
                    x = TM[0] if l == 1 else X
                    xt = TB[0] if l == 1 else XT
                    after(pe, "x_kept", (LEVELS - 1) * c + l)
                    each(R4, 2, C, 0, lambda q: [(AB[:, 0, q], x[:, q])], "t_prod")
                    if l == 2:
                        after(pe, "g_att_kept", c + 1)
                        for q in R2:
                            pe.transpose(PS[7][:, q * P:(q + 1) * P], GVS[:, q], ident[:])
                        for q in R2:
                            last = pe.transpose(PS[7][:, (GP + q) * P:(GP + q + 1) * P], GKS[:, q], ident[:])
                        last.then_inc(s["g_turn"], 1)
                    if l == 3:
                        after(pe, "ak_kept", c + 1)
                        after(pe, "v_kept", c + 1)
                        after(pe, "kt_kept", c + 1)
                        after(pe, "s_kept", c)
                        each(R4, 5, C, 0, lambda q: [(AK[:, 0, q], V[:, q]), (AS[:, q], S[:, q])], "r_prod")
                    if l == 4:
                        after(pe, "g_turn_kept", c + 1)
                        each(R2, 7, P, 0, lambda q: [(GA[:, q], GVT[:, q]), (GQS[:, q], GS[:, q])], None)
                        each(R2, 7, P, GP * P, lambda q: [(GKS[:, q], GVT[:, q])], "g_prod")
                    after(pe, "joined", (LEVELS - 1) * c + l)
                    if l > 1:
                        after(pe, "xt_kept", (LEVELS - 1) * c + l - 1)
                    else:
                        after(pe, "v_kept", c + 1)
                    if l < LEVELS - 1:
                        each(R4, 3, C, 0, lambda q: [(xt[:, q], TM[l][:, q])], "x_prod")
                    each(R4, 4, P, 0, lambda q: [(TB[l][:, q], xt[:, q])], "xt_prod")
                after(pe, "r_kept", c + 1)
                after(pe, "xt_kept", (LEVELS - 1) * (c + 1))
                each(R4, 5, C, PAIRS * C, lambda q: [(XT[:, q], RR[:, q])], "u_prod")
                after(pe, "g_norm", c + 1)
                for q in R2:
                    last = pe.transpose(PS[7][:, q * P:(q + 1) * P], GO[:, q], ident[:])
                last.then_inc(s["g_ot"], 1)
                after(pe, "u_kept", c + 1)
                each(R4, 1, C, 0, lambda q: [(RS[:, q], S[:, q]), (AB[:, 1, q], U[:, q]), (AK[:, 1, q], V[:, q])],
                     "o_prod")
                after(pe, "bt_kept", c + 1)
                each(R4, 0, C, 0, lambda q: [(KS[:, q], V[:, q]), (BS[:, q], U[:, q])], "m_prod")
                after(pe, "ob_kept", c + 1)
                each(R4, 6, C, 0, lambda q: [(OB[:, q], istack[:])], "ot_prod")

            pe.wait_ge(s["init"], 1)
            over_chunks(pe, body)

        @block.vector
        def _(dve):
            count, base = [0], [0]

            def link(ins):
                count[0] += 1
                ins.then_inc(s["chain"], 1)
                dve.wait_ge(s["chain"], base[0] + count[0])

            def body(c):
                count[0] = 0
                if not isinstance(c, int):
                    base[0] = c * per_chunk[0]
                after(dve, "b_prod", c + 1)
                b = PS[0][:].rearrange("p (q a t) -> p q a t", q=PAIRS, a=2)
                for h, rows in halves():
                    ins = dve.tensor_tensor(AB[rows, :, :, h, :].rearrange("p a q t -> p q a t"), b[rows],
                                            maska[rows].unsqueeze(1).to_broadcast([C, PAIRS, 2, C]), ALU.mult)
                ins.then_inc(s["ab_kept"], 1)
                after(dve, "a_prod", c + 1, plain=True)
                dve.copy_predicated(TM[0][:], maskd[:, 0].unsqueeze(1).to_broadcast([P, PAIRS, C]),
                                    dense(PS[2], PAIRS)).then_inc(s["x_kept"], 1)
                dve.copy_predicated(TB[0][:], maskb[:, 0].unsqueeze(1).to_broadcast([P, PAIRS, 2, C]),
                                    b[:, :, 0:1, :].to_broadcast([P, PAIRS, 2, C]))
                for l in range(1, LEVELS):
                    after(dve, "t_prod", (LEVELS - 1) * c + l, plain=True)
                    t = dense(PS[2], PAIRS)
                    dve.copy_predicated(TM[l][:], maskd[:, l].unsqueeze(1).to_broadcast([P, PAIRS, C]), t)
                    dve.copy_predicated(TB[l][:], maskb[:, l].unsqueeze(1).to_broadcast([P, PAIRS, 2, C]),
                                        t.unsqueeze(2).to_broadcast([P, PAIRS, 2, C])).then_inc(s["joined"], 1)
                    if l == 1:
                        after(dve, "k_prod", c + 1)
                        k = PS[1][:].rearrange("p (q a t) -> p q a t", q=PAIRS, a=2)
                        for h, rows in halves():
                            ins = dve.tensor_tensor(AK[rows, :, :, h, :].rearrange("p a q t -> p q a t"), k[rows],
                                                    maska[rows].unsqueeze(1).to_broadcast([C, PAIRS, 2, C]), ALU.mult)
                        ins.then_inc(s["ak_kept"], 1)
                        after(dve, "g_att", c + 1, plain=True)
                        for h, rows in halves():
                            ins = dve.copy_predicated(
                                GA[rows, :, h, :], maska[rows, 1:2, :].to_broadcast([C, GP, C]).bitcast(I32),
                                PS[7][rows, 0:GP * C].rearrange("p (q t) -> p q t", q=GP))
                        ins.then_inc(s["g_att_kept"], 1)
                    if l < LEVELS - 1:
                        after(dve, "x_prod", (LEVELS - 2) * c + l)
                        dve.tensor_copy(X[:], dense(PS[3], PAIRS)).then_inc(s["x_kept"], 1)
                    if l == 3:
                        after(dve, "r_prod", c + 1)
                        dve.tensor_copy(RR[:], dense(PS[5], PAIRS)).then_inc(s["r_kept"], 1)
                    if l == 4:
                        after(dve, "g_prod", c + 1)
                        g = PS[7][:].rearrange("p (a q v) -> p a q v", a=2, q=GP)
                        dve.tensor_copy(GO[:], g[:, 0])
                        dve.tensor_tensor(GS[:], GS[:], g[:, 1], ALU.add).then_inc(s["g_kept"], 1)
                        dve.wait_ge(s["g_kept"], c + 1)
                        link(dve.tensor_tensor(GS[:], GS[:], GG[:, :, ds(c, 1)].to_broadcast([P, GP, P]), ALU.mult))
                after(dve, "g_rooted", c + 1)
                link(dve.reciprocal(grs, grs))
                for q in range(GP):
                    ins = dve.tensor_scalar(GO[:, q], GO[:, q], grs[:, q:q + 1], None, ALU.mult)
                ins.then_inc(s["g_norm"], 1)
                after(dve, "u_prod", c + 1)
                dve.tensor_copy(U[:], PS[5][:, PAIRS * C:2 * PAIRS * C].rearrange("p (q v) -> p q v", q=PAIRS)
                                ).then_inc(s["u_kept"], 1)
                after(dve, "m_prod", c + 1)
                link(dve.tensor_tensor(S[:], S[:], dense(PS[0], PAIRS), ALU.add))
                dve.tensor_tensor(S[:], S[:], G[:, :, ds(c, 1)].to_broadcast([P, PAIRS, C]), ALU.mult
                                  ).then_inc(s["s_kept"], 1)
                after(dve, "o_prod", c + 1, plain=True)
                o = dense(PS[1], PAIRS)
                for q in range(PAIRS):
                    ins = dve.bn_stats(st6[:, q], o[:, q])
                link(ins)
                dve.sem_inc(s["step"], 1)
                for q in range(PAIRS):
                    ins = dve.bn_aggr(mv[:, q], st6[:, q])
                ins.then_inc(s["stats"], 1)
                dve.wait_ge(s["stats"], c + 1)
                link(dve.tensor_tensor(OC[:], o, mv[:, :, 0:1].to_broadcast([P, PAIRS, C]), ALU.subtract))
                dve.wait_ge(s["rooted"], c + 1)
                link(dve.reciprocal(lsd, lsd))
                for h, rows in halves():
                    ins = dve.tensor_tensor(OB[rows, :, h, :], OC[rows], lsd[rows].unsqueeze(2).to_broadcast([C, PAIRS, C]),
                                            ALU.mult)
                ins.then_inc(s["ob_kept"], 1)

            per_chunk = [0]
            dve.wait_ge(s["init"], 1)
            dve.wait_ge(s["masks_in"], 48)
            body(0)
            per_chunk[0] = count[0]
            with dve.Fori(1, NC) as c:
                body(c)
            assert count[0] == per_chunk[0]

        @block.scalar
        def _(act):
            def body(c):
                at = ds(c * C, C)
                after(act, "v_prod", c + 1)
                act.activation(V[:], dense(PS[3], PAIRS), ACT.Copy).then_inc(s["v_kept"], 1)
                after(act, "k_turn", c + 1)
                act.activation(KS[:].rearrange("p q h t -> p (q h t)"), PS[5][:], ACT.Copy).then_inc(s["kt_kept"], 1)
                after(act, "b_turn", c + 1)
                act.activation(BS[:].rearrange("p q h t -> p (q h t)"), PS[6][:], ACT.Copy).then_inc(s["bt_kept"], 1)
                for l in range(1, LEVELS):
                    after(act, "xt_prod", (LEVELS - 1) * c + l)
                    act.activation(XT[:].rearrange("p q h t -> p (q h t)"), PS[4][:], ACT.Copy).then_inc(s["xt_kept"], 1)
                    if l == 2:
                        after(act, "g_turn", c + 1)
                        act.activation(GVT[:].rearrange("p q v -> p (q v)"), PS[7][:, 0:GP * P], ACT.Copy)
                        act.activation(GKS[:].rearrange("p q h t -> p (q h t)"), PS[7][:, GP * P:2 * GP * P], ACT.Copy
                                       ).then_inc(s["g_turn_kept"], 1)
                after(act, "g_kept", c + 1)
                for q in range(GP):
                    ins = act.activation(GSQ[:], GO[:, q], ACT.Square, accum_out=gss[:, q:q + 1])
                    ins.then_inc(s["act_chain"], 1)
                    act.wait_ge(s["act_chain"], 2 * c + q + 1)
                act.activation(grs, gss, ACT.Sqrt, scale=1.0 / P, bias=geps).then_inc(s["g_rooted"], 1)
                after(act, "g_ot", c + 1)
                act.activation(GV[:, :, at], PS[7][:, 0:GP * P].rearrange("p (q t) -> p q t", t=C), ACT.Copy
                               ).then_inc(s["g_out_kept"], 1)
                after(act, "stats", c + 1)
                act.activation(lsd, mv[:, :, 1], ACT.Sqrt, bias=leps).then_inc(s["rooted"], 1)
                after(act, "ot_prod", c + 1)
                act.activation(AR[:, 0, :, at], dense(PS[6], PAIRS), ACT.Copy).then_inc(s["out_kept"], 1)

            act.wait_ge(s["init"], 1)
            over_chunks(act, body)


def dense(bank, n):
    return bank[:, 0:n * C].rearrange("p (q t) -> p q t", t=C)


def mix0(nc, sb, sem, ctx, PS, AR, BK, VT, GV, SG, bdones, col):
    rk_done = sem("m0_rk")
    summed = sem("m0_sum")
    chain = sem("m0_chain")
    read = sem("m0_read")
    with nc.Block() as block:
        @block.tensor
        def _(pe):
            for p in range(PAIRS):
                pe.wait_ge(rk_done, p + 1)
                if p >= 2:
                    pe.wait_ge(read, p - 1)
                for h in range(2):
                    last = pe.matmul(PS[2 * (p % 2) + h][:], bdones[:], AR[:, 1, p, h * HB:(h + 1) * HB],
                                     start=True, stop=True)
                last.then_inc(summed, 1)

        @block.vector
        def _(dve):
            count = [0]

            def link(ins):
                count[0] += 1
                ins.then_inc(chain, 1)
                dve.wait_ge(chain, count[0])

            for p in range(PAIRS):
                r = AR[:, 1, p, :]
                dve.scalar_tensor_tensor(out=r, in0=r, scalar=col("r_k", p), in1=BK[:, 1, p, :], op0=ALU.mult,
                                         op1=ALU.mult).then_inc(rk_done, 1)
            for j in range(4):
                dve.scalar_tensor_tensor(out=SG[:, j, :], in0=GV[:, j, :], scalar=col("gla_norm"), in1=SG[:, j, :],
                                         op0=ALU.mult, op1=ALU.mult)
            for p in range(PAIRS):
                o = AR[:, 0, p, :]
                link(dve.tensor_scalar(o, o, col("ln_w", p), col("ln_b", p), ALU.mult, ALU.add))
                dve.wait_ge(summed, p + 1)
                for h in range(2):
                    v = VT[:, p, h * HB:(h + 1) * HB]
                    ins = dve.tensor_tensor(v, v, PS[2 * (p % 2) + h][:], ALU.mult)
                ins.then_inc(read, 1)
                dve.wait_ge(read, p + 1)
                link(dve.tensor_tensor(o, o, VT[:, p, :], ALU.add))
                link(dve.tensor_tensor(SG[:, 4 + p, :], SG[:, 4 + p, :], o, ALU.mult))


def out_project(nc, sem, tag, PS, A, W, R, dst, w_dram, r_dram, bias, final=None, row_in=None, turn=0):
    w_in, b_in = sem(f"{tag}_w_in"), sem(f"{tag}_b_in")
    done = sem(f"{tag}_done")
    biased = sem(f"{tag}_biased")
    added = sem(f"{tag}_added")
    squared, rooted = sem(f"{tag}_squared"), sem(f"{tag}_rooted")
    chain, normed, stored = sem(f"{tag}_chain"), sem(f"{tag}_normed"), sem(f"{tag}_stored")
    with nc.Block() as block:
        @block.sync
        def _(sp):
            for k in range(KT):
                sp.dma_start(W[:, k, :], w_dram[:, k, :]).then_inc(w_in, 16)
            if bias:
                sp.dma_start(bias[0][:], bias[1]).then_inc(b_in, 16)
            if final:
                sp.dma_start(final["fn"][:], final["fnorm"]).then_inc(b_in, 16)
            if r_dram is not None:
                for t in range(TT):
                    sp.dma_start(R[:, t, :], r_dram[:, t, :]).then_inc(row_in[t], 16)
            if final:
                for t in range(TT):
                    sp.wait_ge(normed, t + 1)
                    sp.dma_start(final["out"][:, t, :], dst[:, t, :]).then_inc(stored, 16)
                sp.wait_ge(stored, 16 * TT)

        @block.tensor
        def _(pe):
            pe.wait_ge(w_in, 16 * KT)
            for t in range(TT):
                if t >= 4:
                    pe.wait_ge(added, t - 3)
                for h in range(2):
                    for k in range(KT):
                        last = pe.matmul(PS[2 * (t % 4) + h][:], A[:, k, t * P:(t + 1) * P], W[:, k, h * HB:(h + 1) * HB],
                                         start=(k == 0), stop=(k == KT - 1))
                last.then_inc(done, 1)

        @block.gpsimd
        def _(pool):
            if bias:
                pool.wait_ge(b_in, 32)
                for t in range(TT):
                    pool.tensor_tensor(R[:, t, :], R[:, t, :], bias[0][:], ALU.add).then_inc(biased, 1)

        @block.scalar
        def _(act):
            if final:
                ms, sd, eps = (final["small"][:, i:j] for i, j in ((0, 8), (8, 16), (24, 25)))
                for t in range(TT):
                    act.wait_ge(added, t + 1)
                    act.activation(final["scratch"], dst[:, t, :], ACT.Square, accum_out=ms[:, t:t + 1]).then_inc(squared, 1)
                    act.wait_ge(squared, t + 1)
                    act.activation(sd[:, t:t + 1], ms[:, t:t + 1], ACT.Sqrt, bias=eps, scale=1.0 / D).then_inc(rooted, 1)

        @block.vector
        def _(dve):
            def finish(t):
                sd = final["small"][:, 8 + t:9 + t]
                dve.wait_ge(rooted, t + 1)
                dve.reciprocal(sd, sd).then_inc(chain, 1)
                dve.wait_ge(chain, t + 1)
                dve.scalar_tensor_tensor(out=dst[:, t, :], in0=dst[:, t, :], scalar=sd, in1=final["fn"][:], op0=ALU.mult,
                                         op1=ALU.mult).then_inc(normed, 1)

            if final:
                dve.wait_ge(b_in, 32)
            for t in range(TT):
                if bias:
                    dve.wait_ge(biased, t + 1)
                if r_dram is not None:
                    dve.wait_ge(row_in[t], 16 * turn)
                dve.wait_ge(done, t + 1)
                for h in range(2):
                    ins = dve.tensor_tensor(dst[:, t, h * HB:(h + 1) * HB], PS[2 * (t % 4) + h][:],
                                            R[:, t, h * HB:(h + 1) * HB], ALU.add)
                ins.then_inc(added, 1)
                if final and t:
                    finish(t - 1)
            if final:
                finish(TT - 1)


def project1(nc, sem, PS, HN, W1, COS, SIN, SW, WV, BV, QT, KTT, V1, SG1, small, w1t, col, rope_in):
    w_in = [sem("p1_w_in0"), sem("p1_w_in1")]
    tile_done, tile_kept = sem("p1_tile_done"), sem("p1_tile_kept")
    v_done, v_kept = sem("p1_v_done"), sem("p1_v_kept")
    bq = sem("p1_bq")
    chain = sem("p1_chain")
    step = sem("p1_step")
    bqs = small[:, 32:40]
    swap = [8 + i for i in range(8)] + list(range(8)) + list(range(16, 32))
    with nc.Block() as block:
        @block.sync
        def _(sp):
            for n in range(2):
                sp.dma_start(W1[:, n], w1t[n]).then_inc(w_in[n], 16)
            with sp.Fori(1, W1_TILES // 2) as i:
                for n in range(2):
                    sp.wait_ge(tile_done, 2 * i + (n - 1))
                    sp.sem_inc(step, 1)
                    sp.dma_start(W1[:, n], w1t[ds(2 * i + n, 1)].rearrange("o p k c -> (o p) k c")).then_inc(w_in[n], 16)

        @block.tensor
        def _(pe):
            pe.wait_ge(rope_in, 64)
            for t in range(TT):
                if t >= 2:
                    pe.wait_ge(v_kept, t - 1)
                for k in range(KT):
                    last = pe.matmul(PS[4 + t % 2][:, 0:256], HN[:, k, t * P:(t + 1) * P], WV[:, k, :],
                                     start=(k == 0), stop=(k == KT - 1))
                last.then_inc(v_done, 1)

            def tile(n, par, turn):
                pe.wait_ge(w_in[par], 16 * turn + 16)
                if not isinstance(n, int):
                    pe.wait_ge(tile_kept, n - 1)
                for h in range(2):
                    for k in range(KT):
                        last = pe.matmul(PS[2 * par + h][:], W1[:, par, k, :], HN[:, k, h * HB:(h + 1) * HB],
                                         start=(k == 0), stop=(k == KT - 1))
                last.then_inc(tile_done, 1)

            for n in range(2):
                tile(n, n, 0)
            with pe.Fori(1, W1_TILES // 2) as i:
                for n in range(2):
                    tile(2 * i + n, n, i)

        @block.scalar
        def _(act):
            def keep(n, dst, func, **kw):
                act.wait_ge(tile_done, n + 1)
                for h in range(2):
                    ins = act.activation(dst[:, h * HB:(h + 1) * HB], PS[2 * (n % 2) + h][:], func, **kw)
                ins.then_inc(tile_kept, 1)

            act.wait_ge(bq, 1)
            for j in range(Q_TILES):
                keep(W1_Q + j, QT[:, j, :], ACT.Identity, scale=GLA_SCALE, bias=bqs[:, j:j + 1])
            for j in range(2):
                keep(W1_K + j, KTT[:, j, P:], ACT.Identity, bias=col("b_k", j))
            for j in range(KT):
                keep(W1_GATE + j, SG1[:, j, :], ACT.Silu)

        @block.vector
        def _(dve):
            count = [0]

            def link(ins):
                count[0] += 1
                ins.then_inc(chain, 1)
                dve.wait_ge(chain, count[0])

            dve.tensor_scalar(bqs, col("b_q", 0, 8), GLA_SCALE, None, ALU.mult).then_inc(bq, 1)
            dve.memset(KTT[:, :, 0:P], 0.0)
            dve.memset(V1[:, 0, :], 0.0)
            dve.wait_ge(rope_in, 64)
            for t in range(TT):
                dve.wait_ge(v_done, t + 1)
                dve.tensor_tensor(V1[:, t + 1, :], PS[4 + t % 2][:, 0:256], BV[:], ALU.add).then_inc(v_kept, 1)
            for j in range(Q_TILES + 2):
                x = QT[:, j, :] if j < Q_TILES else KTT[:, j - Q_TILES, P:]
                dve.wait_ge(tile_kept, j + 1)
                link(dve.stream_shuffle(SW[:], x, swap))
                link(dve.tensor_tensor(SW[:], SW[:], SIN[:], ALU.mult))
                link(dve.tensor_tensor(x, x, COS[:], ALU.mult))
                link(dve.tensor_tensor(x, x, SW[:], ALU.add))


def attend(nc, sb, sem, ctx, PS, QT, KTT, V1, SG1, band_d, small, col, ident):
    def buf(name, shape, dt=F):
        return sb(name, shape, dt, ctx=ctx)

    NB = T // P
    band = buf("band", [P, 2, 2 * P])
    QS = buf("QS", [P, 2, Q_TILES, P])
    KS2 = buf("KS2", [P, 2, 2, 2 * P])
    SC = buf("SC", [P, 2, 2, 2 * P])
    PR = buf("PR", [P, 2, 2, 2 * P])
    PT = buf("PT", [P, 2, 2, 2 * P])
    OS = buf("OS", [P, Q_TILES, P])
    nm, rs, es = buf("nm", [P, 16]), buf("rs_", [P, 16]), buf("es", [P, 16])
    nsink = buf("nsink", [P, 16])
    names = ("band_in q_in0 q_in1 s_prod scored exped turned pt_kept pv_done o_kept o_turned gated es_in es_exp "
             "step chain setup")
    s = {n: sem("a_" + n) for n in names.split()}
    with nc.Block() as block:
        def after(eng, name, n):
            if not isinstance(n, int) or n > 0:
                eng.wait_ge(s[name], n)

        def over_blocks(eng, body):
            for n in range(2):
                body(n, n, 0)
            with eng.Fori(1, NB // 2) as i:
                for n in range(2):
                    body(2 * i + n, n, i)

        @block.sync
        def _(sp):
            sp.dma_start(band[:], band_d).then_inc(s["band_in"], 16)

            def body(n, u, turn):
                if not isinstance(n, int):
                    sp.wait_ge(s["pv_done"], Q_TILES * (n - 1))
                    sp.sem_inc(s["step"], 1)
                sp.dma_start(QS[:, u], QT[:, :, ds(n * P, P)]).then_inc(s[f"q_in{u}"], 16)
                sp.dma_start(KS2[:, u], KTT[:, :, ds(n * P, 2 * P)]).then_inc(s[f"q_in{u}"], 16)

            over_blocks(sp, body)

        @block.tensor
        def _(pe):
            def body(n, u, turn):
                after(pe, f"q_in{u}", 32 * turn + 32)
                for i in range(Q_TILES + 2):
                    if i < Q_TILES:
                        j = i
                        if i >= 2 or not (isinstance(n, int) and n == 0):
                            after(pe, "scored", Q_TILES * n + (j - 1))
                        for a in range(2):
                            rows = slice(a * C, (a + 1) * C)
                            last = pe.matmul(PS[2 * (j % 2) + a][:, 0:2 * P], QS[rows, u, j, :], KS2[rows, u, j // 4, :],
                                             start=True, stop=True)
                        last.then_inc(s["s_prod"], 1)
                    if 1 <= i <= Q_TILES:
                        j = i - 1
                        after(pe, "exped", Q_TILES * n + j + 1)
                        if j == 0:
                            after(pe, "gated", n)
                        after(pe, "pt_kept", Q_TILES * n + (j - 1))
                        for a in range(2):
                            for b in range(2):
                                last = pe.transpose(PS[4 + j % 2][:, (2 * a + b) * P:(2 * a + b + 1) * P],
                                                    PR[:, j % 2, a, b * P:(b + 1) * P], ident[:])
                        last.then_inc(s["turned"], 1)
                    if i >= 2:
                        j = i - 2
                        after(pe, "pt_kept", Q_TILES * n + j + 1)
                        if j == 0:
                            after(pe, "o_kept", n)
                        for a in range(2):
                            g = 2 * (j // 4) + a
                            for b in range(2):
                                last = pe.matmul(PS[6 + j // 4][:, (j % 4) * P + a * C:(j % 4) * P + (a + 1) * C],
                                                 PT[:, j % 2, a, b * P:(b + 1) * P],
                                                 V1[:, ds(n + b, 1), g * C:(g + 1) * C].rearrange("p o v -> p (o v)"),
                                                 start=(b == 0), stop=(b == 1))
                        last.then_inc(s["pv_done"], 1)
                after(pe, "o_kept", n + 1)
                for j in range(Q_TILES):
                    last = pe.transpose(PS[4 + j // 4][:, (j % 4) * P:(j % 4 + 1) * P], OS[:, j, :], ident[:])
                last.then_inc(s["o_turned"], 1)

            over_blocks(pe, body)

        @block.scalar
        def _(act):
            def body(n, u, turn):
                for j in range(Q_TILES):
                    after(act, "scored", Q_TILES * n + j + 1)
                    after(act, "turned", Q_TILES * n + (j - 1))
                    for a in range(2):
                        h = 2 * j + a
                        ins = act.activation(PR[:, j % 2, a, :], SC[:, j % 2, a, :], ACT.Exp, scale=-1.0, bias=nm[:, h:h + 1],
                                             accum_out=rs[:, h:h + 1])
                    ins.then_inc(s["exped"], 1)
                after(act, "es_in", n + 1)
                act.activation(es[:], es[:], ACT.Exp).then_inc(s["es_exp"], 1)

            over_blocks(act, body)

        @block.vector
        def _(dve):
            count, base = [0], [0]

            def link(ins):
                count[0] += 1
                ins.then_inc(s["chain"], 1)
                dve.wait_ge(s["chain"], base[0] + count[0])

            def body(n, u, turn):
                first = isinstance(n, int) and n == 0
                mask = band[:, 0 if first else 1, :]
                for i in range(Q_TILES + 1):
                    if i < Q_TILES:
                        j = i
                        after(dve, "s_prod", Q_TILES * n + j + 1)
                        dve.sem_inc(s["step"], 1)
                        after(dve, "exped", Q_TILES * n + (j - 1))
                        dve.sem_inc(s["step"], 1)
                        for a in range(2):
                            h = 2 * j + a
                            ins = dve.tensor_tensor_reduce(SC[:, j % 2, a, :], PS[2 * (j % 2) + a][:, 0:2 * P], mask,
                                                           -1.0, nsink[:, h:h + 1], ALU.add, ALU.min, nm[:, h:h + 1])
                        ins.then_inc(s["scored"], 1)
                    if i >= 1:
                        j = i - 1
                        after(dve, "turned", Q_TILES * n + j + 1)
                        after(dve, "pv_done", Q_TILES * n + (j - 1))
                        dve.tensor_copy(PT[:, j % 2].rearrange("p a k -> p (a k)"), PS[4 + j % 2][:]).then_inc(s["pt_kept"], 1)
                dve.wait_ge(s["scored"], Q_TILES * n + Q_TILES)
                dve.tensor_tensor(es[:], nm[:], nsink[:], ALU.subtract).then_inc(s["es_in"], 1)
                after(dve, "es_exp", n + 1)
                link(dve.tensor_tensor(es[:], es[:], rs[:], ALU.add))
                link(dve.reciprocal(es[:], es[:]))
                after(dve, "pv_done", Q_TILES * n + Q_TILES)
                after(dve, "o_turned", n)
                for b in range(2):
                    ins = dve.tensor_tensor(OS[:, 4 * b:4 * b + 4, :].rearrange("p j (a v) -> p (j a) v", a=2),
                                            PS[6 + b][:].rearrange("p (h v) -> p h v", v=C),
                                            es[:, 8 * b:8 * b + 8].unsqueeze(2).to_broadcast([P, 8, C]), ALU.mult)
                ins.then_inc(s["o_kept"], 1)
                after(dve, "o_turned", n + 1)
                for b in range(2):
                    sg = SG1[:, 4 * b:4 * b + 4, ds(n * P, P)]
                    ins = dve.tensor_tensor(sg, sg, PS[4 + b][:].rearrange("p (j q) -> p j q", j=4), ALU.mult)
                ins.then_inc(s["gated"], 1)

            link_setup = dve.tensor_scalar(nsink[:], col("sinks", 0, 16), -1.0, None, ALU.mult)
            link_setup.then_inc(s["setup"], 1)
            dve.wait_ge(s["setup"], 1)
            dve.wait_ge(s["band_in"], 16)
            body(0, 0, 0)
            per = count[0]
            count[0], base[0] = 0, per
            body(1, 1, 0)
            with dve.Fori(1, NB // 2) as i:
                for n in range(2):
                    count[0], base[0] = 0, per * (2 * i + n)
                    body(2 * i + n, n, i)


def _layout(inputs):
    import numpy as np

    f = {k: np.ascontiguousarray(v) for k, v in inputs.items()}

    def tiles(w, cols):
        out = np.zeros((len(cols), P, KT, P), np.float32)
        for i, c in enumerate(cols):
            out[i, :, :, :len(c)] = w[:, c].reshape(KT, P, len(c)).transpose(1, 0, 2)
        return out

    def run(a, n=P):
        return list(range(a, a + n))

    gq, gk, gv, gl, r, k, v, xx, gate = 0, 256, 512, 1024, 1040, 1552, 2064, 2576, 2704
    cols = [run(xx)]
    for p in range(PAIRS):
        cols += [run(k + p * P), run(r + p * P), run(v + p * P)]
    cols += [run(gl, 16)] + [run(gq + i * P) for i in range(8)] + [run(gate + i * P) for i in range(8)]
    w0t = tiles(f["w_in0"][0], cols)

    order = []
    for j in range(Q_TILES):
        a = 8 * (j // 4) + j % 4
        order += run(a * C, C) + run((a + 4) * C, C)
    heads = [order[i * C] // C for i in range(16)]
    w1 = f["w_in1"][0]
    kq, vq, gq1 = 1024, 1280, 1536
    w1t = tiles(w1, [order[i * P:(i + 1) * P] for i in range(8)] + [run(kq + i * P) for i in range(2)]
                + [[gq1 + o for o in order[i * P:(i + 1) * P]] for i in range(8)])
    wv1 = np.ascontiguousarray(w1[:, vq:vq + 256].reshape(KT, P, 256).transpose(1, 0, 2))
    wout0 = np.ascontiguousarray(f["w_out0"][0].reshape(KT, P, D).transpose(1, 0, 2))
    wout1 = np.ascontiguousarray(f["w_out1"][0][order].reshape(KT, P, D).transpose(1, 0, 2))

    b_in = f["b_in1"][0]
    mu = f["rwkv_mu"][0]
    vectors = {
        "norm0": f["norm_w"][0], "norm1": f["norm_w"][1], "mu_x": mu[1536:1664], "mu_k": mu[512:1024], "mu_r": mu[:512],
        "mu_v": mu[1024:1536], "w0": f["rwkv_w0"][0], "a0": f["rwkv_a0"][0], "k_k": f["rwkv_k_k"][0],
        "k_a": f["rwkv_k_a"][0], "r_k": f["rwkv_r_k"][0].reshape(-1), "ln_w": f["rwkv_ln_w"][0], "ln_b": f["rwkv_ln_b"][0],
        "gk_bias": f["gla_gk_bias"][0], "gla_norm": f["gla_norm_w"][0], "b_q": b_in[order], "b_k": b_in[1024:1280],
    }
    par = np.zeros((P, NPAR), np.float32)
    for name, vec in vectors.items():
        n = vec.size // P
        par[:, _COLS[name]:_COLS[name] + n] = vec.reshape(n, P).T
    par[:, _COLS["sinks"]:_COLS["sinks"] + 16] = f["attn_sinks"][0][heads]

    one = np.arange(P)
    h, t = one // C, one % C
    ident = np.eye(P, dtype=np.float32)
    istack = (t[:, None] == np.arange(C)).astype(np.float32)
    bdones = (h[:, None] == h[None, :]).astype(np.float32)
    cc = np.arange(C)
    maska = np.stack([t[:, None] < cc, t[:, None] <= cc], 1).astype(np.float32)
    scanm = np.broadcast_to((np.arange(T) % C != 0).astype(np.float32), (P, T)).copy()
    maskd = np.zeros((P, LEVELS, C), np.int32)
    maskb = np.zeros((P, LEVELS, 2, C), np.int32)
    for l in range(LEVELS):
        b = 1 << l

        def joint(row, c):
            return (row // (2 * b) == c // (2 * b)) & ((row // b) % 2 == 1) & ((c // b) % 2 == 0)

        maskd[:, l] = joint(t[:, None], cc[None])
        m = joint(cc[None], t[:, None]) if l == 0 else joint(t[:, None], cc[None])
        for hh in range(2):
            maskb[:, l, hh] = m & (h[:, None] == hh)
    half = 8
    inv_freq = (np.float32(500000.0) ** (-np.arange(half, dtype=np.float32) / np.float32(half))).astype(np.float32)
    ang = (np.arange(T, dtype=np.float32)[None, :] * inv_freq[:, None]).astype(np.float32).astype(np.float64)
    cos, sin = np.ones((P, T), np.float32), np.zeros((P, T), np.float32)
    for base in (0, C):
        for i in range(16):
            cos[base + i] = np.cos(ang[i % 8])
            sin[base + i] = np.sin(ang[i % 8]) * (-1.0 if i < 8 else 1.0)
    i, j = np.arange(P)[:, None], np.arange(2 * P)[None, :]
    inside = (i + P - j >= 0) & (i + P - j < P)
    band = np.stack([np.where(inside & (j >= P), 0.0, NEG), np.where(inside, 0.0, NEG)], 1).astype(np.float32)

    return {
        "x": f["x"][0], "w0t": w0t, "wup": np.concatenate([f["rwkv_w_up"][0], f["rwkv_a_up"][0]], 0),
        "gkup": f["gla_gk_up"][0], "wout0": wout0, "w1t": w1t, "wv1": wv1,
        "bv1": np.broadcast_to(b_in[1280:1536], (P, 256)).copy(), "wout1": wout1, "par": par,
        "bout1": np.broadcast_to(f["b_out1"][0], (P, D)).copy(), "fnorm": np.broadcast_to(f["final_norm_w"], (P, D)).copy(),
        "ident_d": ident, "istack_d": istack, "bdones_d": bdones, "maska_d": maska, "scan_d": scanm, "maskd_d": maskd,
        "maskb_d": maskb, "cos_d": cos, "sin_d": sin, "band_d": band,
    }


def kernel(**inputs):
    import concourse.bacc as bacc
    import numpy as np
    from concourse.bass_utils import run_bass_kernel_spmd

    nc = bacc.Bacc("TRN2", target_bir_lowering=False, num_devices=1)
    arrays = {"in_" + k: np.ascontiguousarray(v) for k, v in _layout(inputs).items()}
    args = {k[3:]: nc.dram_tensor(k, a.shape, mybir.dt.from_np(a.dtype), kind="ExternalInput").ap()
            for k, a in arrays.items()}
    out = nc.dram_tensor("out", (T, D), F, kind="ExternalOutput").ap()
    trunk(nc, **args, out=out)
    got = run_bass_kernel_spmd(nc, [arrays], core_ids=[0])
    return got.results[0]["out"].reshape(1, T, D)
```

```python
from contextlib import ExitStack

import concourse.bass as bass
from concourse import mybir

F = mybir.dt.float32
I32 = mybir.dt.int32
ALU = mybir.AluOpType
ACT = mybir.ActivationFunctionType
AX = mybir.AxisListType
ds = bass.ds

P = 128
T = 1024
D = 1024
KT = D // P
TT = T // P
C = 64
NC = T // C
HB = 512
PAIRS = 4
GP = 2
LEVELS = 6
EPS = 1e-5
LN_EPS = 64e-5
DECAY = 0.6065306597126334
NORMALIZER = 16.0
GLA_SCALE = 0.125
Q_TILES = 8
NEG = -1.0e30

_COLS = {}
_at = 0
for _name, _n in (("norm0", 8), ("norm1", 8), ("mu_x", 1), ("mu_k", 4), ("mu_r", 4), ("mu_v", 4), ("w0", 4),
                  ("a0", 4), ("k_k", 4), ("k_a", 4), ("r_k", 4), ("ln_w", 4), ("ln_b", 4), ("gk_bias", 2),
                  ("gla_norm", 1), ("b_q", 8), ("b_k", 2), ("sinks", 16)):
    _COLS[_name] = _at
    _at += _n
NPAR = _at

W0_X = 0
W0_PAIR = 1
W0_GLOW = 13
W0_GLA = 14
W0_GATE = 22
W0_TILES = 30
W1_Q, W1_K, W1_GATE, W1_TILES = 0, 8, 10, 18


def trunk(nc, x, w0t, wup, gkup, wout0, w1t, wv1, bv1, wout1, par, bout1, fnorm, ident_d, istack_d, bdones_d,
          maska_d, scan_d, maskd_d, maskb_d, cos_d, sin_d, band_d, out):
    root = ExitStack()
    with root:
        def sb(name, shape, dt=F, ctx=root):
            return ctx.enter_context(nc.sbuf_tensor(name, shape, dt))

        def sem(name):
            return root.enter_context(nc.semaphore(name))

        PS = [root.enter_context(nc.psum_tensor(f"ps{i}", [P, HB], F)) for i in range(8)]

        par_sb = sb("par", [P, NPAR])
        ident = sb("ident", [P, P])
        istack = sb("istack", [P, C])
        small = sb("small", [P, 64])

        def col(name, i=0, n=1):
            return par_sb[:, _COLS[name] + i:_COLS[name] + i + n]

        const_in = sem("const_in")
        const2_in = sem("const2_in")
        row_in = [sem(f"row_in{t}") for t in range(TT)]
        turns = [0]

        norms, norm_sems = [0], {}

        def row_turn():
            turns[0] += 1
            return turns[0]


        def norm_transpose(rows, normed, scratch, dst, norm_name, load=None, extra_load=None, next_loads=None):
            turn = row_turn()
            again = norms[0]
            norms[0] += 1
            if not again:
                norm_sems.update((n, sem("norm_" + n)) for n in
                                 "squared rooted inverted scaled turned kept_act kept_dve eps_set".split())
            squared, rooted, inverted, scaled, turned, kept_act, kept_dve, eps_set = norm_sems.values()
            r, g0 = TT * again, 2 * TT * again
            ms, sd, rs, eps = small[:, 0:8], small[:, 8:16], small[:, 16:24], small[:, 24:25]
            with nc.Block() as block:
                @block.sync
                def _(sp):
                    if load is not None:
                        for t in range(TT):
                            sp.dma_start(rows[:, t, :], load[:, t, :]).then_inc(row_in[t], 16)
                    if extra_load:
                        extra_load(sp)

                @block.scalar
                def _(act):
                    act.wait_ge(eps_set, again + 1)
                    for t in range(TT):
                        if load is not None:
                            act.wait_ge(row_in[t], 16 * turn)
                        if t:
                            act.wait_ge(squared, r + t)
                        act.activation(scratch, rows[:, t, :], ACT.Square, accum_out=ms[:, t:t + 1]).then_inc(squared, 1)
                        act.wait_ge(squared, r + t + 1)
                        act.activation(sd[:, t:t + 1], ms[:, t:t + 1], ACT.Sqrt, bias=eps, scale=1.0 / D).then_inc(rooted, 1)
                    act.wait_ge(const_in, 16 * 3)
                    for g in range(1, 16, 2):
                        half, k = divmod(g, KT)
                        act.wait_ge(turned, g0 + g + 1)
                        act.activation(dst[:, k, half * HB:(half + 1) * HB], PS[g % 4][:], ACT.Copy,
                                       scale=col(norm_name, k)).then_inc(kept_act, 1)

                @block.vector
                def _(dve):
                    dve.memset(eps, EPS).then_inc(eps_set, 1)
                    for t in range(TT):
                        dve.wait_ge(rooted, r + t + 1)
                        dve.reciprocal(rs[:, t:t + 1], sd[:, t:t + 1]).then_inc(inverted, 1)
                        dve.wait_ge(inverted, r + t + 1)
                        dve.tensor_scalar(normed[:, t, :], rows[:, t, :], rs[:, t:t + 1], None, ALU.mult).then_inc(scaled, 1)
                        if t == 3:
                            dve.wait_ge(const_in, 16 * 3)
                    for g in range(0, 16, 2):
                        half, k = divmod(g, KT)
                        dve.wait_ge(turned, g0 + g + 1)
                        dve.tensor_scalar(dst[:, k, half * HB:(half + 1) * HB], PS[g % 4][:], col(norm_name, k), None,
                                          ALU.mult).then_inc(kept_dve, 1)

                @block.tensor
                def _(pe):
                    pe.wait_ge(const_in, 16 * 3)
                    for g in range(16):
                        half, k = divmod(g, KT)
                        if g % KT == 0:
                            pe.wait_ge(scaled, r + 4 * half + 4)
                        if g >= 4:
                            pe.wait_ge(kept_act if g % 2 else kept_dve, r + (g - 4) // 2 + 1)
                        for j in range(4):
                            last = pe.transpose(PS[g % 4][:, j * P:(j + 1) * P],
                                                normed[:, 4 * half + j, k * P:(k + 1) * P], ident[:])
                        last.then_inc(turned, 1)

        layer0 = ExitStack()
        with layer0:
            AR = sb("AR", [P, 2, PAIRS, T], ctx=layer0)
            BK = sb("BK", [P, 2, PAIRS, T], ctx=layer0)
            VT = sb("VT", [P, PAIRS, T], ctx=layer0)
            QK = sb("QK", [P, 2, GP, T], ctx=layer0)
            GV = sb("GV", [P, 4, T], ctx=layer0)
            SG = sb("SG", [P, KT, T], ctx=layer0)
            bdones = sb("bdones", [P, P], ctx=layer0)
            G = sb("G", [P, PAIRS, NC], ctx=layer0)
            GG = sb("GG", [P, GP, NC], ctx=layer0)
            half1 = ExitStack()
            with half1:
                HN = sb("HN", [P, KT, T], ctx=half1)
                WB = sb("WB", [P, 2, KT, P], ctx=half1)
                scanm = sb("scanm", [P, T], ctx=half1)
                RAW = sb("RAW", [P, 2, T + 1], ctx=half1)
                wup_sb = VT[:, 3, 0:512]
                gk_sb = sb("gk_sb", [16, 256], ctx=half1)

                def const_loads(sp):
                    sp.dma_start(bdones[:], bdones_d).then_inc(const2_in, 16)
                    sp.dma_start(scanm[:], scan_d).then_inc(const2_in, 16)
                    sp.dma_start(gk_sb[:], gkup).then_inc(const2_in, 16)
                    sp.dma_start(wup_sb, wup).then_inc(const2_in, 16)

                with nc.Block() as block:
                    @block.sync
                    def _(sp):
                        sp.dma_start(par_sb[:], par).then_inc(const_in, 16)
                        sp.dma_start(ident[:], ident_d).then_inc(const_in, 16)
                        sp.dma_start(istack[:], istack_d).then_inc(const_in, 16)

                x_rows = AR[:, :, :, :].rearrange("p a b t -> p (a b) t")
                norm_transpose(x_rows, x_rows, BK[:, 0, 0, :], HN, "norm0",
                               load=x.rearrange("(t p) d -> p t d", p=P), extra_load=const_loads)

                project0(nc, sem, PS, HN, WB, wup_sb, gk_sb, RAW, scanm, AR, BK, VT, QK, GV, SG, bdones, G, GG,
                         small, w0t, col, const2_in)
            loop = ExitStack()
            with loop:
                chunks0(nc, sb, sem, loop, PS, AR, BK, VT, QK, GV, G, GG, small, ident, istack, maska_d, maskd_d,
                        maskb_d)
            tail = ExitStack()
            with tail:
                mix0(nc, sb, sem, tail, PS, AR, BK, VT, GV, SG, bdones, col)
            H1 = sb("H1", [P, TT, D], ctx=layer0)
            WO = BK[:, :, :, :].rearrange("p a b t -> p (a b) t")
            XR = AR[:, :, :, :].rearrange("p a b t -> p (a b) t")
            out_project(nc, sem, "o0", PS, SG, WO, XR, H1, wout0, x.rearrange("(t p) d -> p t d", p=P), None,
                        row_in=row_in, turn=row_turn())
            h1_dram = nc.dram_tensor("h1_dram", (P, TT, D), F, kind="Internal").ap()
            h1_out = sem("h1_out")
            with nc.Block() as block:
                @block.sync
                def _(sp):
                    sp.dma_start(h1_dram, H1[:]).then_inc(h1_out, 16)
                    sp.wait_ge(h1_out, 16)

        layer1 = ExitStack()
        with layer1:
            H = sb("H", [P, TT, D], ctx=layer1)
            QT = sb("QT", [P, Q_TILES, T], ctx=layer1)
            KTT = sb("KTT", [P, 2, T + P], ctx=layer1)
            V1 = sb("V1", [P, TT + 1, 256], ctx=layer1)
            SG1 = sb("SG1", [P, KT, T], ctx=layer1)
            HN1 = sb("HN1", [P, KT, T], ctx=layer1)
            proj = ExitStack()
            with proj:
                W1 = sb("W1", [P, 2, KT, P], ctx=proj)
                COS = sb("COS", [P, T], ctx=proj)
                SIN = sb("SIN", [P, T], ctx=proj)
                SW = sb("SW", [P, T], ctx=proj)
                WV = sb("WV", [P, KT, 256], ctx=proj)
                BV = sb("BV", [P, 256], ctx=proj)
                rope_in = sem("rope_in")

                def rope_loads(sp):
                    sp.dma_start(COS[:], cos_d).then_inc(rope_in, 16)
                    sp.dma_start(SIN[:], sin_d).then_inc(rope_in, 16)
                    sp.dma_start(WV[:], wv1).then_inc(rope_in, 16)
                    sp.dma_start(BV[:], bv1).then_inc(rope_in, 16)

                norm_transpose(H, QT, SG1[:, 0, :], HN1, "norm1", load=h1_dram, extra_load=rope_loads)
                project1(nc, sem, PS, HN1, W1, COS, SIN, SW, WV, BV, QT, KTT, V1, SG1, small, w1t,
                         col, rope_in)
            att = ExitStack()
            with att:
                attend(nc, sb, sem, att, PS, QT, KTT, V1, SG1, band_d, small, col, ident)
            outp = ExitStack()
            with outp:
                WO1 = HN1
                BO = sb("BO", [P, D], ctx=outp)
                FN = sb("FN", [P, D], ctx=outp)
                SQ = sb("SQ", [P, D], ctx=outp)
                out_project(nc, sem, "o1", PS, SG1, WO1, H, QT, wout1, None, (BO, bout1),
                            dict(fn=FN, fnorm=fnorm, small=small, scratch=SQ[:],
                                 out=out.rearrange("(t p) d -> p t d", p=P)))


def project0(nc, sem, PS, HN, WB, wup_sb, gk_sb, RAW, scanm, AR, BK, VT, QK, GV, SG, bdones, G, GG, small, w0t,
             col, const_in):
    mixd, kmix, kk, sq = (QK[:, i // 2, i % 2, :] for i in range(4))
    nrm, cum, e2, e1a = (GV[:, i, :] for i in range(4))
    nka, mid = small[:, 32:36], small[:, 40:56]
    tile_bank = [PS[0:2], PS[2:4]]
    w_in = [sem("w_in0"), sem("w_in1")]
    tile_done = sem("tile_done")
    tile_kept = sem("tile_kept")
    mixed = sem("mixed")
    xw_tanh = sem("xw_tanh")
    low_done = sem("low_done")
    low_kept = sem("low_kept")
    kk_raw = sem("kk_raw")
    kk_sq = sem("kk_sq")
    kk_sum = sem("kk_sum")
    kk_nrm = sem("kk_nrm")
    rel_done = sem("rel_done")
    exps = sem("exps")
    pair_done = sem("pair_done")
    step = sem("p0_step")
    chain = sem("p0_chain")
    pad = sem("p0_pad")
    glow_kept = sem("glow_kept")
    gz_done = sem("gz_done")
    gz_kept = sem("gz_kept")
    gz_abs = sem("gz_abs")
    gz_step = sem("gz_step")
    g_rel = sem("g_rel")
    g_exp = sem("g_exp")
    g_scaled = sem("g_scaled")

    with nc.Block() as block:
        @block.sync
        def _(sp):
            for n in range(2):
                sp.dma_start(WB[:, n], w0t[n]).then_inc(w_in[n], 16)
            with sp.Fori(1, W0_TILES // 2) as i:
                for n in range(2):
                    sp.wait_ge(tile_done, 2 * i + (n - 1))
                    sp.sem_inc(step, 1)
                    sp.dma_start(WB[:, n], w0t[ds(2 * i + n, 1)].rearrange("o p k c -> (o p) k c")).then_inc(w_in[n], 16)

        @block.tensor
        def _(pe):
            def tile(n, par, turn=None):
                pe.wait_ge(w_in[par], 16 * (n // 2 if turn is None else turn) + 16)
                if not isinstance(n, int) or n >= 2:
                    pe.wait_ge(tile_kept, n - 1)
                for h in range(2):
                    for k in range(KT):
                        last = pe.matmul(tile_bank[par][h][:], WB[:, par, k, :], HN[:, k, h * HB:(h + 1) * HB],
                                         start=(k == 0), stop=(k == KT - 1))
                last.then_inc(tile_done, 1)

            tile(0, 0)
            pe.wait_ge(const_in, 16 * 4)
            pe.wait_ge(xw_tanh, 1)
            for j in range(8):
                lo = 0 if j < 4 else C
                if j >= 2:
                    pe.wait_ge(low_kept, j - 1)
                for h in range(2):
                    last = pe.matmul(PS[4 + 2 * (j % 2) + h][:], wup_sb[lo:lo + C, (j % 4) * P:(j % 4 + 1) * P],
                                     mixd[lo:lo + C, h * HB:(h + 1) * HB], start=True, stop=True)
                last.then_inc(low_done, 1)
            for p in range(PAIRS):
                for j in range(3):
                    tile(3 * p + j + 1, (3 * p + j + 1) % 2)
                    if j == 1:
                        pe.wait_ge(kk_sq, p + 1)
                        if p:
                            pe.wait_ge(kk_nrm, p)
                        for h in range(2):
                            last = pe.matmul(PS[4 + h][:], bdones[:], sq[:, h * HB:(h + 1) * HB], start=True, stop=True)
                        last.then_inc(kk_sum, 1)
            tile(W0_GLOW, W0_GLOW % 2)
            pe.wait_ge(glow_kept, 1)
            for j in range(GP):
                for h in range(2):
                    last = pe.matmul(PS[4 + 2 * j + h][:], gk_sb[:, j * P:(j + 1) * P], mixd[0:16, h * HB:(h + 1) * HB],
                                     start=True, stop=True)
                last.then_inc(gz_done, 1)
            with pe.Fori(0, (W0_TILES - W0_GLA) // 2) as i:
                for n in range(2):
                    tile(2 * i + (W0_GLA + n), n, i + W0_GLA // 2)

        @block.scalar
        def _(act):
            def keep(n, dst, func, **kw):
                act.wait_ge(tile_done, n + 1)
                for h in range(2):
                    ins = act.activation(dst[:, h * HB:(h + 1) * HB], tile_bank[n % 2][h][:], func, **kw)
                ins.then_inc(tile_kept, 1)

            def keep_raw(n):
                if n >= 2:
                    act.wait_ge(mixed, n - 1)
                keep(n, RAW[:, n % 2, 1:T + 1], ACT.Copy)

            act.wait_ge(pad, 1)
            keep_raw(0)
            act.wait_ge(mixed, 1)
            act.activation(mixd[0:C, :], mixd[0:C, :], ACT.Tanh).then_inc(xw_tanh, 1)
            for j in range(8):
                act.wait_ge(low_done, j + 1)
                for h in range(2):
                    ins = act.activation(SG[:, j, h * HB:(h + 1) * HB], PS[4 + 2 * (j % 2) + h][:], ACT.Sigmoid,
                                         bias=col("w0", j) if j < 4 else col("a0", j - 4))
                ins.then_inc(low_kept, 1)
            for p in range(PAIRS):
                keep_raw(1 + 3 * p)
                act.wait_ge(kk_raw, p + 1)
                act.activation(sq, kk, ACT.Square).then_inc(kk_sq, 1)
                keep_raw(2 + 3 * p)
                act.wait_ge(rel_done, p + 1)
                act.activation(G[:, p, :], G[:, p, :], ACT.Exp, scale=-DECAY)
                act.activation(e2, cum, ACT.Exp, scale=DECAY)
                act.activation(e1a, e1a, ACT.Exp, scale=-DECAY)
                act.activation(cum, cum, ACT.Exp, scale=-DECAY).then_inc(exps, 1)
                act.wait_ge(kk_sum, p + 1)
                for h in range(2):
                    ins = act.activation(nrm[:, h * HB:(h + 1) * HB], PS[4 + h][:], ACT.Sqrt)
                ins.then_inc(kk_nrm, 1)
                keep_raw(3 + 3 * p)
            act.wait_ge(pair_done, PAIRS)
            act.wait_ge(mixed, 3 * PAIRS + 1)
            act.wait_ge(tile_done, W0_GLOW + 1)
            for h in range(2):
                ins = act.activation(mixd[0:16, h * HB:(h + 1) * HB], tile_bank[W0_GLOW % 2][h][0:16, :], ACT.Copy)
            ins.then_inc(glow_kept, 1)
            act.wait_ge(glow_kept, 1)
            act.activation(small[:, 57:58], small[:, 57:58], ACT.Copy).then_inc(tile_kept, 1)
            for j in range(GP):
                z, l = (nrm, cum)[j], (e2, e1a)[j]
                act.wait_ge(gz_done, j + 1)
                for h in range(2):
                    ins = act.activation(z[:, h * HB:(h + 1) * HB], PS[4 + 2 * j + h][:], ACT.Identity, bias=col("gk_bias", j))
                ins.then_inc(gz_kept, 1)
                act.wait_ge(gz_abs, j + 1)
                act.activation(l, l, ACT.Exp, scale=-1.0).then_inc(gz_step, 1)
                act.wait_ge(gz_step, 2 * j + 1)
                act.activation(l, l, ACT.Ln, bias=1.0).then_inc(gz_step, 1)
            for j in range(GP):
                z, l = (nrm, cum)[j], (e2, e1a)[j]
                act.wait_ge(g_rel, j + 1)
                act.activation(l, z, ACT.Exp, scale=-1.0 / NORMALIZER)
                act.activation(GG[:, j, :], GG[:, j, :], ACT.Exp, scale=1.0 / NORMALIZER)
                act.activation(z, z, ACT.Exp, scale=1.0 / NORMALIZER).then_inc(g_exp, 1)
            for j in range(4):
                keep(W0_GLA + j, QK[:, j // 2, j % 2, :], ACT.Copy, scale=GLA_SCALE if j < 2 else 1.0)
            act.wait_ge(g_scaled, 4)
            for j in range(4):
                keep(W0_GLA + 4 + j, GV[:, j, :], ACT.Copy)
            for j in range(KT):
                keep(W0_GATE + j, SG[:, j, :], ACT.Silu)

        @block.vector
        def _(dve):
            count = [0]

            def link(ins):
                count[0] += 1
                ins.then_inc(chain, 1)
                dve.wait_ge(chain, count[0])

            def mix(n, mu, dst, t=mixd):
                raw = RAW[:, n % 2, :]
                dve.wait_ge(tile_kept, n + 1)
                link(dve.tensor_tensor(t, raw[:, 0:T], raw[:, 1:T + 1], ALU.subtract))
                dve.scalar_tensor_tensor(out=dst, in0=t, scalar=mu, in1=raw[:, 1:T + 1],
                                         op0=ALU.mult, op1=ALU.add).then_inc(mixed, 1)
                dve.wait_ge(mixed, n + 1)

            def by_chunk(ap):
                return ap.rearrange("p (c t) -> p c t", t=C)

            def relative(cs, dst, g):
                v = by_chunk(cs)
                link(dve.tensor_copy(mid, v[:, :, C // 2]))
                link(dve.tensor_tensor(g[:, 0:NC - 1], mid[:, 1:NC], mid[:, 0:NC - 1], ALU.subtract))
                link(dve.tensor_tensor(g[:, 0:NC - 1], g[:, 0:NC - 1], v[:, 0:NC - 1, C - 1], ALU.add))
                link(dve.tensor_tensor(by_chunk(dst), v, mid.unsqueeze(2).to_broadcast([P, NC, C]), ALU.subtract))

            dve.memset(small[:, 56:64], 0.0)
            dve.memset(RAW[:, :, 0:1], 0.0).then_inc(pad, 1)
            link(dve.memset(G[:], 0.0))
            link(dve.memset(GG[:], 0.0))
            dve.wait_ge(const_in, 16 * 4)
            link(dve.tensor_scalar(nka, col("k_a", 0, 4), -1.0, 1.0, ALU.mult, ALU.add))
            mix(0, col("mu_x"), mixd, kmix)
            dve.wait_ge(low_kept, 8)
            for p in range(PAIRS):
                sw, sa = SG[:, p, :], SG[:, 4 + p, :]
                link(dve.tensor_tensor_scan(cum, scanm[:], sw, 0.0, ALU.mult, ALU.add))
                relative(cum, cum, G[:, p, :])
                dve.tensor_tensor(e1a, cum, sw, ALU.subtract).then_inc(rel_done, 1)
                mix(1 + 3 * p, col("mu_k", p), kmix)
                dve.tensor_scalar(kk, kmix, col("k_k", p), None, ALU.mult).then_inc(kk_raw, 1)
                link(dve.tensor_scalar(mixd, sa, col("k_a", p), nka[:, p:p + 1], ALU.mult, ALU.add))
                link(dve.tensor_tensor(kmix, kmix, mixd, ALU.mult))
                dve.wait_ge(exps, p + 1)
                link(dve.tensor_tensor(BK[:, 1, p, :], kmix, e2, ALU.mult))
                mix(2 + 3 * p, col("mu_r", p), kmix)
                link(dve.tensor_tensor(AR[:, 1, p, :], kmix, cum, ALU.mult))
                dve.wait_ge(kk_nrm, p + 1)
                link(dve.tensor_scalar(nrm, nrm, 1e-12, None, ALU.max))
                link(dve.reciprocal(nrm, nrm))
                link(dve.tensor_tensor(kk, kk, nrm, ALU.mult))
                link(dve.scalar_tensor_tensor(out=AR[:, 0, p, :], in0=kk, scalar=-1.0, in1=e1a,
                                              op0=ALU.mult, op1=ALU.mult))
                link(dve.tensor_tensor(kk, kk, sa, ALU.mult))
                dve.tensor_tensor(BK[:, 0, p, :], kk, e2, ALU.mult).then_inc(pair_done, 1)
                dve.wait_ge(pair_done, p + 1)
                mix(3 + 3 * p, col("mu_v", p), VT[:, p, :])
            for j in range(GP):
                z, l = (nrm, cum)[j], (e2, e1a)[j]
                dve.wait_ge(gz_kept, j + 1)
                dve.scalar_tensor_tensor(out=l, in0=z, scalar=-1.0, in1=z, op0=ALU.mult, op1=ALU.max).then_inc(gz_abs, 1)
                dve.wait_ge(gz_step, 2 * j + 2)
                link(dve.scalar_tensor_tensor(out=z, in0=z, scalar=0.0, in1=l, op0=ALU.min, op1=ALU.subtract))
                link(dve.tensor_tensor_scan(l, scanm[:], z, 0.0, ALU.mult, ALU.add))
                relative(l, z, GG[:, j, :])
                dve.tensor_copy(mid, mid).then_inc(g_rel, 1)
            for j in range(4):
                dve.wait_ge(tile_kept, W0_GLA + j + 1)
                dve.wait_ge(g_exp, GP)
                e = (nrm, cum)[j % 2] if j < 2 else (e2, e1a)[j % 2]
                qk = QK[:, j // 2, j % 2, :]
                dve.tensor_tensor(qk, qk, e, ALU.mult).then_inc(g_scaled, 1)


def chunks0(nc, sb, sem, ctx, PS, AR, BK, VT, QK, GV, G, GG, small, ident, istack, maska_d, maskd_d, maskb_d):
    def buf(name, shape, dt=F):
        return sb(name, shape, dt, ctx=ctx)

    maska = buf("maska", [P, 2, C])
    maskd = buf("maskd", [P, LEVELS, C], I32)
    maskb = buf("maskb", [P, LEVELS, 2, C], I32)
    RS, AS, BS, KS, VS = (buf(n, [P, PAIRS, 2, C]) for n in ("RS", "AS", "BS", "KS", "VS"))
    AB = buf("AB", [P, 2, PAIRS, 2, C])
    AK = buf("AK", [P, 2, PAIRS, 2, C])
    TM = [buf(f"TM{l}", [P, PAIRS, C]) for l in range(LEVELS - 1)]
    TB = [buf(f"TB{l}", [P, PAIRS, 2, C]) for l in range(LEVELS)]
    X = buf("X", [P, PAIRS, C])
    XT = buf("XT", [P, PAIRS, 2, C])
    RR, U, S, V = (buf(n, [P, PAIRS, C]) for n in ("RR", "U", "S", "V"))
    OB = buf("OB", [P, PAIRS, 2, C])
    BT, KTB = buf("BT", [P, PAIRS, 2, C]), buf("KTB", [P, PAIRS, 2, C])
    st6, mv = buf("st6", [P, PAIRS, 6]), buf("mv", [P, PAIRS, 2])
    lsd, grs = small[:, 0:4], small[:, 8:10]
    leps, geps = small[:, 12:13], small[:, 13:14]
    gss = small[:, 14:16]
    LX, LJ = LEVELS - 2, LEVELS - 1
    GQS, GKS = (buf(n, [P, GP, 2, C]) for n in ("GQS", "GKS"))
    GVS = buf("GVS", [P, GP, 2, C])
    GA = buf("GA", [P, GP, 2, C])
    GVT, GS, GO = (buf(n, [P, GP, P]) for n in ("GVT", "GS", "GO"))

    names = ("masks_in staged_zero joints_set staged_a staged_b staged_k staged_v staged_r g_split g_staged "
             "b_prod k_prod a_prod v_prod k_turn b_turn t_prod x_prod xt_prod r_prod u_prod o_prod m_prod ot_prod step "
             "ab_kept arb_kept ak_kept x_kept tm_kept joined xt_kept v_kept kt_kept bt_kept r_kept u_kept s_added s_kept "
             "stats inverted rooted ob_kept out_kept "
             "g_att g_turn g_prod g_ot g_att_kept g_turn_kept g_kept g_decayed g_squared g_rooted g_inverted g_norm g_out_kept")
    s = {n: sem("c_" + n) for n in names.split()}

    def halves():
        return ((h, slice(h * C, (h + 1) * C)) for h in range(2))

    def after(eng, name, n, plain=False):
        if not isinstance(n, int) or n > 0:
            eng.wait_ge(s[name], n)
            if plain:
                eng.sem_inc(s["step"], 1)

    def flat(b):
        return b[:].rearrange("p q h t -> p (q h t)")

    with nc.Block() as block:
        @block.sync
        def _(sp):
            sp.dma_start(maska[:], maska_d).then_inc(s["masks_in"], 16)
            sp.dma_start(maskd[:], maskd_d).then_inc(s["masks_in"], 16)
            sp.dma_start(maskb[:], maskb_d).then_inc(s["masks_in"], 16)

        @block.gpsimd
        def _(pool):
            def stage(c, dst, src, done):
                at = ds(c * C, C)
                for h, rows in halves():
                    ins = pool.tensor_copy(dst[rows, :, h, :], src[rows, :, at])
                ins.then_inc(s[done], 1)

            def body(c):
                after(pool, "b_turn", c)
                stage(c, BS, BK[:, 0], "staged_b")
                after(pool, "g_prod", c)
                stage(c, GQS, QK[:, 0], "g_split")
                stage(c, GKS, QK[:, 1], "g_split")
                pool.wait_ge(s["g_split"], 2 * c + 2)
                pool.tensor_copy(GVS[:].rearrange("p q h t -> p (q h) t"), GV[:, :, ds(c * C, C)]
                                 ).then_inc(s["g_staged"], 1)
                pool.wait_ge(s["g_staged"], c + 1)
                after(pool, "k_prod", c)
                stage(c, KS, BK[:, 1], "staged_k")
                after(pool, "v_prod", c)
                stage(c, VS, VT, "staged_v")
                after(pool, "o_prod", c)
                stage(c, RS, AR[:, 1], "staged_r")

            for b in (BS, AS, GQS, GKS, KS, VS, RS):
                last = pool.memset(b[:], 0.0)
            last.then_inc(s["staged_zero"], 1)
            pool.wait_ge(s["staged_zero"], 1)
            body(0)
            with pool.Fori(1, NC) as c:
                body(c)

        @block.tensor
        def _(pe):
            def each(pairs, bank, width, base, products, done):
                n = len(products(0))
                for q in pairs:
                    for i, (lhsT, rhs) in enumerate(products(q)):
                        last = pe.matmul(PS[bank][:, base + q * width:base + (q + 1) * width], lhsT, rhs,
                                         start=(i == 0), stop=(i == n - 1))
                if done:
                    last.then_inc(s[done], 1)

            R4, R2 = range(PAIRS), range(GP)

            def solve(n):
                after(pe, "r_kept", n)
                after(pe, "xt_kept", LJ * n)
                each(R4, 5, C, PAIRS * C, lambda q: [(XT[:, q], RR[:, q])], "u_prod")

            def output(n):
                after(pe, "u_kept", n)
                after(pe, "staged_r", n)
                each(R4, 1, C, 0, lambda q: [(RS[:, q], S[:, q]), (AB[:, 1, q], U[:, q]), (AK[:, 1, q], V[:, q])],
                     "o_prod")
                after(pe, "bt_kept", n)
                each(R4, 6, C, 0, lambda q: [(KTB[:, q], V[:, q]), (BT[:, q], U[:, q])], "m_prod")

            def turn_output(n):
                after(pe, "ob_kept", n)
                after(pe, "s_added", n)
                each(R4, 6, C, 0, lambda q: [(OB[:, q], istack[:])], "ot_prod")

            def body(c, apply=True):
                at = ds(c * C, C)
                after(pe, "staged_b", c + 1)
                each(R4, 0, P, 0, lambda q: [(BS[:, q], AR[:, :, q, at])], "b_prod")
                after(pe, "staged_a", c + 1)
                each(R4, 2, C, 0, lambda q: [(AS[:, q], BK[:, 0, q, at])], "a_prod")
                if apply:
                    solve(c)
                after(pe, "g_staged", c + 1)
                after(pe, "g_out_kept", c)
                each(R2, 7, C, 0, lambda q: [(GKS[:, q], QK[:, 0, q, at])], "g_att")
                after(pe, "ab_kept", c + 1)
                for l in range(1, LEVELS):
                    x = TM[0] if l == 1 else X
                    xt = TB[0] if l == 1 else XT
                    after(pe, "x_kept", LJ * c + l)
                    each(R4, 2, C, 0, lambda q: [(AB[:, 0, q], x[:, q])], "t_prod")
                    if l == 1:
                        if apply:
                            output(c)
                    if l == 2:
                        after(pe, "g_att_kept", c + 1)
                        for q in R2:
                            pe.transpose(PS[7][:, q * P:(q + 1) * P], GVS[:, q], ident[:])
                        for q in R2:
                            last = pe.transpose(PS[7][:, (GP + q) * P:(GP + q + 1) * P], GKS[:, q], ident[:])
                        last.then_inc(s["g_turn"], 1)
                        after(pe, "staged_k", c + 1)
                        for q in R4:
                            last = pe.transpose(PS[5][:, q * P:(q + 1) * P], KS[:, q], ident[:])
                        last.then_inc(s["k_turn"], 1)
                    if l == 3:
                        if apply:
                            turn_output(c)
                        each(R4, 1, P, 0, lambda q: [(KS[:, q], AR[:, :, q, at])], "k_prod")
                        after(pe, "staged_v", c + 1)
                        after(pe, "arb_kept", c + 1)
                        each(R4, 0, C, 0, lambda q: [(VS[:, q], istack[:])], "v_prod")
                    if l == 4:
                        after(pe, "g_turn_kept", c + 1)
                        each(R2, 7, P, 0, lambda q: [(GA[:, q], GVT[:, q]), (GQS[:, q], GS[:, q])], None)
                        each(R2, 7, P, GP * P, lambda q: [(GKS[:, q], GVT[:, q])], "g_prod")
                        if apply:
                            after(pe, "out_kept", c)
                        for q in R4:
                            last = pe.transpose(PS[6][:, q * P:(q + 1) * P], BS[:, q], ident[:])
                        last.then_inc(s["b_turn"], 1)
                    if l == LJ:
                        after(pe, "ak_kept", c + 1)
                        after(pe, "v_kept", c + 1)
                        after(pe, "kt_kept", c + 1)
                        after(pe, "s_kept", c)
                        each(R4, 5, C, 0, lambda q: [(AK[:, 0, q], V[:, q]), (AS[:, q], S[:, q])], "r_prod")
                    if l > 1:
                        after(pe, "xt_kept", LJ * c + l - 1)
                    if l < LJ:
                        after(pe, "tm_kept", LX * c + l)
                        each(R4, 3, C, 0, lambda q: [(xt[:, q], TM[l][:, q])], "x_prod")
                    after(pe, "joined", LJ * c + l)
                    each(R4, 4, P, 0, lambda q: [(TB[l][:, q], xt[:, q])], "xt_prod")
                after(pe, "g_norm", c + 1)
                for q in R2:
                    last = pe.transpose(PS[7][:, q * P:(q + 1) * P], GO[:, q], ident[:])
                last.then_inc(s["g_ot"], 1)

            pe.wait_ge(s["joints_set"], 1)
            body(0, apply=False)
            with pe.Fori(1, NC) as c:
                body(c)
            solve(NC)
            output(NC)
            turn_output(NC)

        @block.vector
        def _(dve):
            def state(n):
                after(dve, "m_prod", n)
                dve.tensor_tensor(S[:], S[:], dense(PS[6], PAIRS), ALU.add).then_inc(s["s_added"], 1)
                dve.wait_ge(s["s_added"], n)
                dve.tensor_tensor(S[:], S[:], G[:, :, ds(n - 1, 1)].to_broadcast([P, PAIRS, C]), ALU.mult
                                  ).then_inc(s["s_kept"], 1)

            def statistics(n):
                after(dve, "o_prod", n, plain=True)
                o = dense(PS[1], PAIRS)
                for q in range(PAIRS):
                    ins = dve.bn_stats(st6[:, q], o[:, q])
                ins.then_inc(s["stats"], 1)
                dve.wait_ge(s["stats"], 2 * n - 1)
                dve.sem_inc(s["step"], 1)
                for q in range(PAIRS):
                    ins = dve.bn_aggr(mv[:, q], st6[:, q])
                ins.then_inc(s["stats"], 1)

            def normalise(n):
                dve.wait_ge(s["rooted"], n)
                dve.reciprocal(lsd, lsd).then_inc(s["inverted"], 1)
                dve.wait_ge(s["inverted"], n)
                for q in range(PAIRS):
                    for h, rows in halves():
                        ins = dve.tensor_scalar(OB[rows, q, h, :], dense(PS[1], PAIRS)[rows, q], mv[rows, q, 0:1],
                                                lsd[rows, q:q + 1], ALU.subtract, ALU.mult)
                ins.then_inc(s["ob_kept"], 1)

            def body(c, apply=True):
                b = PS[0][:].rearrange("p (q a t) -> p q a t", q=PAIRS, a=2)

                def mask_to(dst, src, kind, done):
                    for h, rows in halves():
                        ins = dve.tensor_tensor(dst[rows, kind, :, h, :], src[rows, :, kind],
                                                maska[rows, kind:kind + 1].to_broadcast([C, PAIRS, C]), ALU.mult)
                    if done:
                        ins.then_inc(s[done], 1)

                after(dve, "b_prod", c + 1)
                mask_to(AB, b, 0, "ab_kept")
                after(dve, "a_prod", c + 1, plain=True)
                dve.copy_predicated(TM[0][:], maskd[:, 0].unsqueeze(1).to_broadcast([P, PAIRS, C]),
                                    dense(PS[2], PAIRS)).then_inc(s["x_kept"], 1)
                dve.copy_predicated(TB[0][:], maskb[:, 0].unsqueeze(1).to_broadcast([P, PAIRS, 2, C]),
                                    b[:, :, 0:1, :].to_broadcast([P, PAIRS, 2, C]))
                for l in range(1, LEVELS):
                    after(dve, "t_prod", LJ * c + l, plain=True)
                    t = dense(PS[2], PAIRS)
                    if l < LJ:
                        dve.copy_predicated(TM[l][:], maskd[:, l].unsqueeze(1).to_broadcast([P, PAIRS, C]), t
                                            ).then_inc(s["tm_kept"], 1)
                    dve.copy_predicated(TB[l][:], maskb[:, l].unsqueeze(1).to_broadcast([P, PAIRS, 2, C]),
                                        t.unsqueeze(2).to_broadcast([P, PAIRS, 2, C])).then_inc(s["joined"], 1)
                    if l < LJ:
                        after(dve, "x_prod", LX * c + l)
                        dve.tensor_copy(X[:], dense(PS[3], PAIRS)).then_inc(s["x_kept"], 1)
                    if l == 1:
                        after(dve, "g_att", c + 1, plain=True)
                        for h, rows in halves():
                            ins = dve.copy_predicated(
                                GA[rows, :, h, :], maska[rows, 1:2, :].to_broadcast([C, GP, C]).bitcast(I32),
                                PS[7][rows, 0:GP * C].rearrange("p (q t) -> p q t", q=GP))
                        ins.then_inc(s["g_att_kept"], 1)
                        if apply:
                            statistics(c)
                    if l == 2:
                        if apply:
                            normalise(c)
                            state(c)
                        mask_to(AB, b, 1, "arb_kept")
                    if l == 3:
                        after(dve, "k_prod", c + 1)
                        k = PS[1][:].rearrange("p (q a t) -> p q a t", q=PAIRS, a=2)
                        mask_to(AK, k, 0, None)
                        mask_to(AK, k, 1, "ak_kept")
                    if l == 4:
                        after(dve, "g_prod", c + 1)
                        g = PS[7][:].rearrange("p (a q v) -> p a q v", a=2, q=GP)
                        dve.tensor_copy(GO[:], g[:, 0])
                        dve.tensor_tensor(GS[:], GS[:], g[:, 1], ALU.add).then_inc(s["g_kept"], 1)
                        dve.wait_ge(s["g_kept"], c + 1)
                        dve.tensor_tensor(GS[:], GS[:], GG[:, :, ds(c, 1)].to_broadcast([P, GP, P]), ALU.mult
                                          ).then_inc(s["g_decayed"], 1)
                        dve.wait_ge(s["g_decayed"], c + 1)
                after(dve, "g_rooted", c + 1)
                dve.reciprocal(grs, grs).then_inc(s["g_inverted"], 1)
                dve.wait_ge(s["g_inverted"], c + 1)
                for q in range(GP):
                    ins = dve.tensor_scalar(GO[:, q], GO[:, q], grs[:, q:q + 1], None, ALU.mult)
                ins.then_inc(s["g_norm"], 1)

            for b in TB:
                dve.tensor_copy(b[:].rearrange("p q h t -> p q (h t)"), ident[:].unsqueeze(1).to_broadcast([P, PAIRS, P]))
            for b in TM:
                dve.tensor_copy(b[:], istack[:].unsqueeze(1).to_broadcast([P, PAIRS, C]))
            for b in (AB, AK, OB, S, GS, GA):
                dve.memset(b[:], 0.0)
            dve.memset(leps, LN_EPS)
            dve.memset(geps, EPS).then_inc(s["joints_set"], 1)
            dve.wait_ge(s["joints_set"], 1)
            dve.wait_ge(s["masks_in"], 48)
            body(0, apply=False)
            with dve.Fori(1, NC) as c:
                body(c)
            statistics(NC)
            normalise(NC)
            state(NC)

        @block.scalar
        def _(act):
            def keep(dst, src, done):
                act.activation(dst, src, ACT.Copy).then_inc(s[done], 1)

            def keep_u(n):
                after(act, "u_prod", n)
                keep(U[:], PS[5][:, PAIRS * C:2 * PAIRS * C].rearrange("p (q v) -> p q v", q=PAIRS), "u_kept")

            def root(n):
                after(act, "stats", 2 * n)
                act.activation(lsd, mv[:, :, 1], ACT.Sqrt, bias=leps).then_inc(s["rooted"], 1)

            def keep_output(n):
                after(act, "ot_prod", n)
                keep(AR[:, 0, :, ds((n - 1) * C, C)], dense(PS[6], PAIRS), "out_kept")

            def stage_a(c):
                for h, rows in halves():
                    ins = act.activation(AS[rows, :, h, :], AR[rows, 0, :, ds(c * C, C)], ACT.Copy)
                ins.then_inc(s["staged_a"], 1)

            def body(c, apply=True, last=False):
                if apply:
                    keep_u(c)
                for l in range(1, LEVELS):
                    if l == LJ:
                        after(act, "r_prod", c + 1)
                        keep(RR[:], dense(PS[5], PAIRS), "r_kept")
                        if not last:
                            stage_a(c + 1)
                    after(act, "xt_prod", LJ * c + l)
                    keep(flat(XT), PS[4][:], "xt_kept")
                    if l == 1 and apply:
                        root(c)
                    if l == 2:
                        after(act, "g_turn", c + 1)
                        act.activation(GVT[:].rearrange("p q v -> p (q v)"), PS[7][:, 0:GP * P], ACT.Copy)
                        keep(flat(GKS), PS[7][:, GP * P:2 * GP * P], "g_turn_kept")
                        after(act, "k_turn", c + 1)
                        keep(flat(KTB), PS[5][:], "kt_kept")
                    if l == 3:
                        if apply:
                            keep_output(c)
                        after(act, "v_prod", c + 1)
                        keep(V[:], dense(PS[0], PAIRS), "v_kept")
                    if l == 4:
                        after(act, "b_turn", c + 1)
                        keep(flat(BT), PS[6][:], "bt_kept")
                        after(act, "g_kept", c + 1)
                        for q in range(GP):
                            ins = act.activation(GVT[:, q], GO[:, q], ACT.Square, accum_out=gss[:, q:q + 1])
                        ins.then_inc(s["g_squared"], 1)
                        act.wait_ge(s["g_squared"], c + 1)
                        act.activation(grs, gss, ACT.Sqrt, scale=1.0 / P, bias=geps).then_inc(s["g_rooted"], 1)
                after(act, "g_ot", c + 1)
                keep(GV[:, :, ds(c * C, C)], PS[7][:, 0:GP * P].rearrange("p (q t) -> p q t", t=C), "g_out_kept")

            act.wait_ge(s["joints_set"], 1)
            act.wait_ge(s["staged_zero"], 1)
            stage_a(0)
            body(0, apply=False)
            with act.Fori(1, NC - 1) as c:
                body(c)
            body(NC - 1, last=True)
            keep_u(NC)
            root(NC)
            keep_output(NC)


def dense(bank, n):
    return bank[:, 0:n * C].rearrange("p (q t) -> p q t", t=C)


def mix0(nc, sb, sem, ctx, PS, AR, BK, VT, GV, SG, bdones, col):
    rk_done = sem("m0_rk")
    summed = sem("m0_sum")
    chain = sem("m0_chain")
    read = sem("m0_read")
    with nc.Block() as block:
        @block.tensor
        def _(pe):
            for p in range(PAIRS):
                pe.wait_ge(rk_done, p + 1)
                if p >= 2:
                    pe.wait_ge(read, p - 1)
                for h in range(2):
                    last = pe.matmul(PS[2 * (p % 2) + h][:], bdones[:], AR[:, 1, p, h * HB:(h + 1) * HB],
                                     start=True, stop=True)
                last.then_inc(summed, 1)

        @block.vector
        def _(dve):
            count = [0]

            def link(ins):
                count[0] += 1
                ins.then_inc(chain, 1)
                dve.wait_ge(chain, count[0])

            for p in range(PAIRS):
                r = AR[:, 1, p, :]
                dve.scalar_tensor_tensor(out=r, in0=r, scalar=col("r_k", p), in1=BK[:, 1, p, :], op0=ALU.mult,
                                         op1=ALU.mult).then_inc(rk_done, 1)
            for j in range(4):
                dve.scalar_tensor_tensor(out=SG[:, j, :], in0=GV[:, j, :], scalar=col("gla_norm"), in1=SG[:, j, :],
                                         op0=ALU.mult, op1=ALU.mult)
            for p in range(PAIRS):
                o = AR[:, 0, p, :]
                link(dve.tensor_scalar(o, o, col("ln_w", p), col("ln_b", p), ALU.mult, ALU.add))
                dve.wait_ge(summed, p + 1)
                for h in range(2):
                    v = VT[:, p, h * HB:(h + 1) * HB]
                    ins = dve.tensor_tensor(v, v, PS[2 * (p % 2) + h][:], ALU.mult)
                ins.then_inc(read, 1)
                dve.wait_ge(read, p + 1)
                link(dve.tensor_tensor(o, o, VT[:, p, :], ALU.add))
                link(dve.tensor_tensor(SG[:, 4 + p, :], SG[:, 4 + p, :], o, ALU.mult))


def out_project(nc, sem, tag, PS, A, W, R, dst, w_dram, r_dram, bias, final=None, row_in=None, turn=0):
    w_in, b_in = sem(f"{tag}_w_in"), sem(f"{tag}_b_in")
    done = sem(f"{tag}_done")
    biased = sem(f"{tag}_biased")
    added = sem(f"{tag}_added")
    squared, rooted = sem(f"{tag}_squared"), sem(f"{tag}_rooted")
    chain, normed, stored = sem(f"{tag}_chain"), sem(f"{tag}_normed"), sem(f"{tag}_stored")
    with nc.Block() as block:
        @block.sync
        def _(sp):
            for k in range(KT):
                sp.dma_start(W[:, k, :], w_dram[:, k, :]).then_inc(w_in, 16)
            if bias:
                sp.dma_start(bias[0][:], bias[1]).then_inc(b_in, 16)
            if final:
                sp.dma_start(final["fn"][:], final["fnorm"]).then_inc(b_in, 16)
            if r_dram is not None:
                for t in range(TT):
                    sp.dma_start(R[:, t, :], r_dram[:, t, :]).then_inc(row_in[t], 16)
            if final:
                for t in range(TT):
                    sp.wait_ge(normed, t + 1)
                    sp.dma_start(final["out"][:, t, :], dst[:, t, :]).then_inc(stored, 16)
                sp.wait_ge(stored, 16 * TT)

        @block.tensor
        def _(pe):
            pe.wait_ge(w_in, 16 * KT)
            for t in range(TT):
                if t >= 4:
                    pe.wait_ge(added, t - 3)
                for h in range(2):
                    for k in range(KT):
                        last = pe.matmul(PS[2 * (t % 4) + h][:], A[:, k, t * P:(t + 1) * P], W[:, k, h * HB:(h + 1) * HB],
                                         start=(k == 0), stop=(k == KT - 1))
                last.then_inc(done, 1)

        @block.gpsimd
        def _(pool):
            if bias:
                pool.wait_ge(b_in, 32)
                for t in range(TT):
                    pool.tensor_tensor(R[:, t, :], R[:, t, :], bias[0][:], ALU.add).then_inc(biased, 1)

        @block.scalar
        def _(act):
            if final:
                ms, sd, eps = (final["small"][:, i:j] for i, j in ((0, 8), (8, 16), (24, 25)))
                for t in range(TT):
                    act.wait_ge(added, t + 1)
                    act.activation(final["scratch"], dst[:, t, :], ACT.Square, accum_out=ms[:, t:t + 1]).then_inc(squared, 1)
                    act.wait_ge(squared, t + 1)
                    act.activation(sd[:, t:t + 1], ms[:, t:t + 1], ACT.Sqrt, bias=eps, scale=1.0 / D).then_inc(rooted, 1)

        @block.vector
        def _(dve):
            def finish(t):
                sd = final["small"][:, 8 + t:9 + t]
                dve.wait_ge(rooted, t + 1)
                dve.reciprocal(sd, sd).then_inc(chain, 1)
                dve.wait_ge(chain, t + 1)
                dve.scalar_tensor_tensor(out=dst[:, t, :], in0=dst[:, t, :], scalar=sd, in1=final["fn"][:], op0=ALU.mult,
                                         op1=ALU.mult).then_inc(normed, 1)

            if final:
                dve.wait_ge(b_in, 32)
            for t in range(TT):
                if bias:
                    dve.wait_ge(biased, t + 1)
                if r_dram is not None:
                    dve.wait_ge(row_in[t], 16 * turn)
                dve.wait_ge(done, t + 1)
                for h in range(2):
                    ins = dve.tensor_tensor(dst[:, t, h * HB:(h + 1) * HB], PS[2 * (t % 4) + h][:],
                                            R[:, t, h * HB:(h + 1) * HB], ALU.add)
                ins.then_inc(added, 1)
                if final and t:
                    finish(t - 1)
            if final:
                finish(TT - 1)


def project1(nc, sem, PS, HN, W1, COS, SIN, SW, WV, BV, QT, KTT, V1, SG1, small, w1t, col, rope_in):
    w_in = [sem("p1_w_in0"), sem("p1_w_in1")]
    tile_done, tile_kept = sem("p1_tile_done"), sem("p1_tile_kept")
    v_done, v_kept = sem("p1_v_done"), sem("p1_v_kept")
    bq = sem("p1_bq")
    chain = sem("p1_chain")
    step = sem("p1_step")
    bqs = small[:, 32:40]
    swap = [8 + i for i in range(8)] + list(range(8)) + list(range(16, 32))
    with nc.Block() as block:
        @block.sync
        def _(sp):
            for n in range(2):
                sp.dma_start(W1[:, n], w1t[n]).then_inc(w_in[n], 16)
            with sp.Fori(1, W1_TILES // 2) as i:
                for n in range(2):
                    sp.wait_ge(tile_done, 2 * i + (n - 1))
                    sp.sem_inc(step, 1)
                    sp.dma_start(W1[:, n], w1t[ds(2 * i + n, 1)].rearrange("o p k c -> (o p) k c")).then_inc(w_in[n], 16)

        @block.tensor
        def _(pe):
            pe.wait_ge(rope_in, 64)
            for t in range(TT):
                if t >= 2:
                    pe.wait_ge(v_kept, t - 1)
                for k in range(KT):
                    last = pe.matmul(PS[4 + t % 2][:, 0:256], HN[:, k, t * P:(t + 1) * P], WV[:, k, :],
                                     start=(k == 0), stop=(k == KT - 1))
                last.then_inc(v_done, 1)

            def tile(n, par, turn):
                pe.wait_ge(w_in[par], 16 * turn + 16)
                if not isinstance(n, int):
                    pe.wait_ge(tile_kept, n - 1)
                for h in range(2):
                    for k in range(KT):
                        last = pe.matmul(PS[2 * par + h][:], W1[:, par, k, :], HN[:, k, h * HB:(h + 1) * HB],
                                         start=(k == 0), stop=(k == KT - 1))
                last.then_inc(tile_done, 1)

            for n in range(2):
                tile(n, n, 0)
            with pe.Fori(1, W1_TILES // 2) as i:
                for n in range(2):
                    tile(2 * i + n, n, i)

        @block.scalar
        def _(act):
            def keep(n, dst, func, **kw):
                act.wait_ge(tile_done, n + 1)
                for h in range(2):
                    ins = act.activation(dst[:, h * HB:(h + 1) * HB], PS[2 * (n % 2) + h][:], func, **kw)
                ins.then_inc(tile_kept, 1)

            act.wait_ge(bq, 1)
            for j in range(Q_TILES):
                keep(W1_Q + j, QT[:, j, :], ACT.Identity, scale=GLA_SCALE, bias=bqs[:, j:j + 1])
            for j in range(2):
                keep(W1_K + j, KTT[:, j, P:], ACT.Identity, bias=col("b_k", j))
            for j in range(KT):
                keep(W1_GATE + j, SG1[:, j, :], ACT.Silu)

        @block.vector
        def _(dve):
            count = [0]

            def link(ins):
                count[0] += 1
                ins.then_inc(chain, 1)
                dve.wait_ge(chain, count[0])

            dve.tensor_scalar(bqs, col("b_q", 0, 8), GLA_SCALE, None, ALU.mult).then_inc(bq, 1)
            dve.memset(KTT[:, :, 0:P], 0.0)
            dve.memset(V1[:, 0, :], 0.0)
            dve.wait_ge(rope_in, 64)
            for t in range(TT):
                dve.wait_ge(v_done, t + 1)
                dve.tensor_tensor(V1[:, t + 1, :], PS[4 + t % 2][:, 0:256], BV[:], ALU.add).then_inc(v_kept, 1)
            for j in range(Q_TILES + 2):
                x = QT[:, j, :] if j < Q_TILES else KTT[:, j - Q_TILES, P:]
                dve.wait_ge(tile_kept, j + 1)
                link(dve.stream_shuffle(SW[:], x, swap))
                link(dve.tensor_tensor(SW[:], SW[:], SIN[:], ALU.mult))
                link(dve.tensor_tensor(x, x, COS[:], ALU.mult))
                link(dve.tensor_tensor(x, x, SW[:], ALU.add))


def attend(nc, sb, sem, ctx, PS, QT, KTT, V1, SG1, band_d, small, col, ident):
    def buf(name, shape, dt=F):
        return sb(name, shape, dt, ctx=ctx)

    NB = T // P
    band = buf("band", [P, 2, 2 * P])
    QS = buf("QS", [P, 2, Q_TILES, P])
    KS2 = buf("KS2", [P, 2, 2, 2 * P])
    SC = buf("SC", [P, 2, 2, 2 * P])
    PR = buf("PR", [P, 2, 2, 2 * P])
    PT = buf("PT", [P, 2, 2, 2 * P])
    OS = buf("OS", [P, Q_TILES, P])
    nm, rs, es = buf("nm", [P, 16]), buf("rs_", [P, 16]), buf("es", [P, 16])
    nsink = buf("nsink", [P, 16])
    names = ("band_in q_in0 q_in1 s_prod scored exped turned pt_kept pv_done o_kept o_turned gated es_in es_exp "
             "es_added es_ready step setup")
    s = {n: sem("a_" + n) for n in names.split()}
    HT = Q_TILES // 2
    STEPS = Q_TILES * NB
    with nc.Block() as block:
        def after(eng, name, n, plain=False):
            if not isinstance(n, int) or n > 0:
                eng.wait_ge(s[name], n)
                if plain:
                    eng.sem_inc(s["step"], 1)

        def there(i, count):
            return not isinstance(i, int) or 0 <= i < count

        def over_blocks(eng, body, drain=True):
            for n in range(2):
                body(n, n, 0, range(Q_TILES))
            with eng.Fori(1, NB // 2) as i:
                for n in range(2):
                    body(2 * i + n, n, i, range(Q_TILES))
            if drain:
                body(NB, 0, 0, range(HT + 2))

        @block.sync
        def _(sp):
            sp.dma_start(band[:], band_d).then_inc(s["band_in"], 16)

            def body(n, u, turn, steps):
                after(sp, "s_prod", Q_TILES * (n - 1), plain=True)
                sp.dma_start(QS[:, u], QT[:, :, ds(n * P, P)]).then_inc(s[f"q_in{u}"], 16)
                sp.dma_start(KS2[:, u], KTT[:, :, ds(n * P, 2 * P)]).then_inc(s[f"q_in{u}"], 16)

            over_blocks(sp, body, drain=False)

        @block.tensor
        def _(pe):
            def scores(g, j, u):
                after(pe, "scored", g - 1)
                for a in range(2):
                    rows = slice(a * C, (a + 1) * C)
                    last = pe.matmul(PS[2 * (j % 2) + a][:, 0:2 * P], QS[rows, u, j, :], KS2[rows, u, j // 4, :],
                                     start=True, stop=True)
                last.then_inc(s["s_prod"], 1)

            def turn_probs(t, j):
                after(pe, "exped", t + 1)
                after(pe, "pt_kept", t - 1)
                for a in range(2):
                    for b in range(2):
                        last = pe.transpose(PS[4 + j % 2][:, (2 * a + b) * P:(2 * a + b + 1) * P],
                                            PR[:, j % 2, a, b * P:(b + 1) * P], ident[:])
                last.then_inc(s["turned"], 1)

            def values(t, j, n, half):
                after(pe, "pt_kept", t + 1)
                if j % HT == 0:
                    after(pe, "gated", half - 1)
                for a in range(2):
                    kv = 2 * (j // 4) + a
                    for b in range(2):
                        last = pe.matmul(PS[6 + j // HT][:, (j % HT) * P + a * C:(j % HT) * P + (a + 1) * C],
                                         PT[:, j % 2, a, b * P:(b + 1) * P],
                                         V1[:, ds(n + b, 1), kv * C:(kv + 1) * C].rearrange("p o v -> p (o v)"),
                                         start=(b == 0), stop=(b == 1))
                last.then_inc(s["pv_done"], 1)

            def turn_output(half, b):
                after(pe, "o_kept", half + 1)
                for j in range(HT):
                    last = pe.transpose(PS[6 + b][:, j * P:(j + 1) * P], OS[:, HT * b + j, :], ident[:])
                last.then_inc(s["o_turned"], 1)

            def body(n, u, turn, steps):
                for j in steps:
                    g, half = Q_TILES * n + j, 2 * n + j // HT
                    if there(g, STEPS):
                        if j == 0:
                            after(pe, f"q_in{u}", 32 * turn + 32)
                        scores(g, j, u)
                    if there(g - 2, STEPS):
                        turn_probs(g - 2, (j - 2) % Q_TILES)
                    if there(g - 3, STEPS):
                        before = j < 3
                        values(g - 3, (j - 3) % Q_TILES, n - before, 2 * (n - before) + (j - 3) % Q_TILES // HT)
                    if j % HT == 0 and there(half - 2, 2 * NB):
                        turn_output(half - 2, j // HT)

            over_blocks(pe, body)

        @block.scalar
        def _(act):
            def body(n, u, turn, steps):
                for j in steps:
                    g = Q_TILES * n + j
                    if not there(g, STEPS):
                        continue
                    after(act, "scored", g + 1)
                    after(act, "turned", g - 1)
                    for a in range(2):
                        h = 2 * j + a
                        ins = act.activation(PR[:, j % 2, a, :], SC[:, j % 2, a, :], ACT.Exp, scale=-1.0, bias=nm[:, h:h + 1],
                                             accum_out=rs[:, h:h + 1])
                    ins.then_inc(s["exped"], 1)
                    if j % HT == HT - 1:
                        half, hs = 2 * n + j // HT, slice(2 * (j + 1 - HT), 2 * (j + 1))
                        after(act, "es_in", half + 1)
                        act.activation(es[:, hs], es[:, hs], ACT.Exp).then_inc(s["es_exp"], 1)

            over_blocks(act, body)

        @block.vector
        def _(dve):
            def heads(b):
                return slice(2 * HT * b, 2 * HT * (b + 1))

            def mask_and_max(g, j, first):
                after(dve, "s_prod", g + 1, plain=True)
                after(dve, "exped", g - 1, plain=True)
                for a in range(2):
                    h = 2 * j + a
                    ins = dve.tensor_tensor_reduce(SC[:, j % 2, a, :], PS[2 * (j % 2) + a][:, 0:2 * P],
                                                   band[:, 0 if first else 1, :], -1.0, nsink[:, h:h + 1],
                                                   ALU.add, ALU.min, nm[:, h:h + 1])
                ins.then_inc(s["scored"], 1)

            def sink_logits(half, b):
                after(dve, "scored", HT * (half + 1))
                dve.tensor_tensor(es[:, heads(b)], nm[:, heads(b)], nsink[:, heads(b)], ALU.subtract
                                  ).then_inc(s["es_in"], 1)

            def keep_probs(t, j):
                after(dve, "turned", t + 1)
                after(dve, "pv_done", t - 1)
                dve.tensor_copy(PT[:, j % 2].rearrange("p a k -> p (a k)"), PS[4 + j % 2][:]).then_inc(s["pt_kept"], 1)

            def denominators(half, b):
                after(dve, "es_exp", half + 1)
                dve.tensor_tensor(es[:, heads(b)], es[:, heads(b)], rs[:, heads(b)], ALU.add).then_inc(s["es_added"], 1)
                dve.wait_ge(s["es_added"], half + 1)
                dve.reciprocal(es[:, heads(b)], es[:, heads(b)]).then_inc(s["es_ready"], 1)

            def divide(half, b):
                after(dve, "es_ready", half + 1)
                after(dve, "pv_done", HT * (half + 1))
                dve.tensor_tensor(OS[:, HT * b:HT * (b + 1), :].rearrange("p j (a v) -> p (j a) v", a=2),
                                  PS[6 + b][:].rearrange("p (h v) -> p h v", v=C),
                                  es[:, heads(b)].unsqueeze(2).to_broadcast([P, 2 * HT, C]), ALU.mult
                                  ).then_inc(s["o_kept"], 1)

            def gate(half, b, n):
                after(dve, "o_turned", half + 1)
                sg = SG1[:, HT * b:HT * (b + 1), ds(n * P, P)]
                dve.tensor_tensor(sg, sg, PS[6 + b][:].rearrange("p (j q) -> p j q", j=HT), ALU.mult
                                  ).then_inc(s["gated"], 1)

            def body(n, u, turn, steps):
                for j in steps:
                    g, half = Q_TILES * n + j, 2 * n + j // HT
                    if there(g, STEPS):
                        mask_and_max(g, j, isinstance(n, int) and n == 0)
                        if j % HT == HT - 1:
                            sink_logits(half, j // HT)
                    if there(g - 2, STEPS):
                        keep_probs(g - 2, (j - 2) % Q_TILES)
                    if j % HT == 1 and there(half - 1, 2 * NB):
                        denominators(half - 1, 1 - j // HT)
                    if j % HT == HT - 1 and there(half - 1, 2 * NB):
                        divide(half - 1, 1 - j // HT)
                    if j % HT == 1 and there(half - 2, 2 * NB):
                        gate(half - 2, j // HT, n - 1)

            dve.tensor_scalar(nsink[:], col("sinks", 0, 16), -1.0, None, ALU.mult).then_inc(s["setup"], 1)
            dve.wait_ge(s["setup"], 1)
            dve.wait_ge(s["band_in"], 16)
            over_blocks(dve, body)


def _layout(inputs):
    import numpy as np

    f = {k: np.ascontiguousarray(v) for k, v in inputs.items()}

    def tiles(w, cols):
        out = np.zeros((len(cols), P, KT, P), np.float32)
        for i, c in enumerate(cols):
            out[i, :, :, :len(c)] = w[:, c].reshape(KT, P, len(c)).transpose(1, 0, 2)
        return out

    def run(a, n=P):
        return list(range(a, a + n))

    gq, gk, gv, gl, r, k, v, xx, gate = 0, 256, 512, 1024, 1040, 1552, 2064, 2576, 2704
    cols = [run(xx)]
    for p in range(PAIRS):
        cols += [run(k + p * P), run(r + p * P), run(v + p * P)]
    cols += [run(gl, 16)] + [run(gq + i * P) for i in range(8)] + [run(gate + i * P) for i in range(8)]
    w0t = tiles(f["w_in0"][0], cols)

    order = []
    for j in range(Q_TILES):
        a = 8 * (j // 4) + j % 4
        order += run(a * C, C) + run((a + 4) * C, C)
    heads = [order[i * C] // C for i in range(16)]
    w1 = f["w_in1"][0]
    kq, vq, gq1 = 1024, 1280, 1536
    w1t = tiles(w1, [order[i * P:(i + 1) * P] for i in range(8)] + [run(kq + i * P) for i in range(2)]
                + [[gq1 + o for o in order[i * P:(i + 1) * P]] for i in range(8)])
    wv1 = np.ascontiguousarray(w1[:, vq:vq + 256].reshape(KT, P, 256).transpose(1, 0, 2))
    wout0 = np.ascontiguousarray(f["w_out0"][0].reshape(KT, P, D).transpose(1, 0, 2))
    wout1 = np.ascontiguousarray(f["w_out1"][0][order].reshape(KT, P, D).transpose(1, 0, 2))

    b_in = f["b_in1"][0]
    mu = f["rwkv_mu"][0]
    vectors = {
        "norm0": f["norm_w"][0], "norm1": f["norm_w"][1], "mu_x": mu[1536:1664], "mu_k": mu[512:1024], "mu_r": mu[:512],
        "mu_v": mu[1024:1536], "w0": f["rwkv_w0"][0], "a0": f["rwkv_a0"][0], "k_k": f["rwkv_k_k"][0],
        "k_a": f["rwkv_k_a"][0], "r_k": f["rwkv_r_k"][0].reshape(-1), "ln_w": f["rwkv_ln_w"][0], "ln_b": f["rwkv_ln_b"][0],
        "gk_bias": f["gla_gk_bias"][0], "gla_norm": f["gla_norm_w"][0], "b_q": b_in[order], "b_k": b_in[1024:1280],
    }
    par = np.zeros((P, NPAR), np.float32)
    for name, vec in vectors.items():
        n = vec.size // P
        par[:, _COLS[name]:_COLS[name] + n] = vec.reshape(n, P).T
    par[:, _COLS["sinks"]:_COLS["sinks"] + 16] = f["attn_sinks"][0][heads]

    one = np.arange(P)
    h, t = one // C, one % C
    ident = np.eye(P, dtype=np.float32)
    istack = (t[:, None] == np.arange(C)).astype(np.float32)
    bdones = (h[:, None] == h[None, :]).astype(np.float32)
    cc = np.arange(C)
    maska = np.stack([t[:, None] < cc, t[:, None] <= cc], 1).astype(np.float32)
    scanm = np.broadcast_to((np.arange(T) % C != 0).astype(np.float32), (P, T)).copy()
    maskd = np.zeros((P, LEVELS, C), np.int32)
    maskb = np.zeros((P, LEVELS, 2, C), np.int32)
    for l in range(LEVELS):
        b = 1 << l

        def joint(row, c):
            return (row // (2 * b) == c // (2 * b)) & ((row // b) % 2 == 1) & ((c // b) % 2 == 0)

        maskd[:, l] = joint(t[:, None], cc[None])
        m = joint(cc[None], t[:, None]) if l == 0 else joint(t[:, None], cc[None])
        for hh in range(2):
            maskb[:, l, hh] = m & (h[:, None] == hh)
    half = 8
    inv_freq = (np.float32(500000.0) ** (-np.arange(half, dtype=np.float32) / np.float32(half))).astype(np.float32)
    ang = (np.arange(T, dtype=np.float32)[None, :] * inv_freq[:, None]).astype(np.float32).astype(np.float64)
    cos, sin = np.ones((P, T), np.float32), np.zeros((P, T), np.float32)
    for base in (0, C):
        for i in range(16):
            cos[base + i] = np.cos(ang[i % 8])
            sin[base + i] = np.sin(ang[i % 8]) * (-1.0 if i < 8 else 1.0)
    i, j = np.arange(P)[:, None], np.arange(2 * P)[None, :]
    inside = (i + P - j >= 0) & (i + P - j < P)
    band = np.stack([np.where(inside & (j >= P), 0.0, NEG), np.where(inside, 0.0, NEG)], 1).astype(np.float32)

    return {
        "x": f["x"][0], "w0t": w0t, "wup": np.concatenate([f["rwkv_w_up"][0], f["rwkv_a_up"][0]], 0),
        "gkup": f["gla_gk_up"][0], "wout0": wout0, "w1t": w1t, "wv1": wv1,
        "bv1": np.broadcast_to(b_in[1280:1536], (P, 256)).copy(), "wout1": wout1, "par": par,
        "bout1": np.broadcast_to(f["b_out1"][0], (P, D)).copy(), "fnorm": np.broadcast_to(f["final_norm_w"], (P, D)).copy(),
        "ident_d": ident, "istack_d": istack, "bdones_d": bdones, "maska_d": maska, "scan_d": scanm, "maskd_d": maskd,
        "maskb_d": maskb, "cos_d": cos, "sin_d": sin, "band_d": band,
    }


def kernel(**inputs):
    import concourse.bacc as bacc
    import numpy as np
    from concourse.bass_utils import run_bass_kernel_spmd

    nc = bacc.Bacc("TRN2", target_bir_lowering=False, num_devices=1)
    arrays = {"in_" + k: np.ascontiguousarray(v) for k, v in _layout(inputs).items()}
    args = {k[3:]: nc.dram_tensor(k, a.shape, mybir.dt.from_np(a.dtype), kind="ExternalInput").ap()
            for k, a in arrays.items()}
    out = nc.dram_tensor("out", (T, D), F, kind="ExternalOutput").ap()
    trunk(nc, **args, out=out)
    got = run_bass_kernel_spmd(nc, [arrays], core_ids=[0])
    return got.results[0]["out"].reshape(1, T, D)
```

```python
from contextlib import ExitStack

import concourse.bass as bass
from concourse import mybir

F = mybir.dt.float32
FR = mybir.dt.float32r
I32 = mybir.dt.int32
ALU = mybir.AluOpType
ACT = mybir.ActivationFunctionType
AX = mybir.AxisListType
ds = bass.ds

P = 128
T = 1024
D = 1024
KT = D // P
TT = T // P
C = 64
NC = T // C
HB = 512
PAIRS = 4
GP = 2
LEVELS = 6
EPS = 1e-5
LN_EPS = 64e-5
DECAY = 0.6065306597126334
NORMALIZER = 16.0
GLA_SCALE = 0.125
Q_TILES = 8
NEG = -1.0e30

_COLS = {}
_at = 0
for _name, _n in (("norm0", 8), ("norm1", 8), ("mu_x", 1), ("mu_k", 4), ("mu_r", 4), ("mu_v", 4), ("w0", 4),
                  ("a0", 4), ("k_k", 4), ("k_a", 4), ("r_k", 4), ("ln_w", 4), ("ln_b", 4), ("gk_bias", 2),
                  ("gla_norm", 1), ("b_q", 8), ("b_k", 2), ("sinks", 16)):
    _COLS[_name] = _at
    _at += _n
NPAR = _at

W0_X = 0
W0_PAIR = 1
W0_GLOW = 13
W0_GLA = 14
W0_GATE = 22
W0_TILES = 30
W1_Q, W1_K, W1_GATE, W1_TILES = 0, 8, 10, 18


def trunk(nc, x, w0t, wup, gkup, wout0, w1t, wv1, bv1, wout1, par, bout1, fnorm, ident_d, istack_d, bdones_d,
          maska_d, scan_d, maskd_d, maskb_d, cos_d, sin_d, band_d, out):
    root = ExitStack()
    with root:
        def sb(name, shape, dt=F, ctx=root):
            return ctx.enter_context(nc.sbuf_tensor(name, shape, dt))

        def sem(name):
            return step if name == "step" else root.enter_context(nc.semaphore(name))

        step = sem("steps")

        PS = [root.enter_context(nc.psum_tensor(f"ps{i}", [P, HB], F)) for i in range(8)]

        par_sb = sb("par", [P, NPAR])
        ident = sb("ident", [P, P])
        istack = sb("istack", [P, C])
        small = sb("small", [P, 64])

        def col(name, i=0, n=1):
            return par_sb[:, _COLS[name] + i:_COLS[name] + i + n]

        const_in = sem("const_in")
        const2_in = sem("const2_in")
        row_in = [sem(f"row_in{t}") for t in range(TT)]
        turns = [0]

        norms, norm_sems = [0], {}
        rms = {n: sem("rms_" + n) for n in ("squared", "rooted", "inverted")}
        rows = {n: sem("rows_" + n) for n in ("done", "added", "normed")}

        def row_turn():
            turns[0] += 1
            return turns[0]

        def norm_transpose(rows, normed, scratch, high, low, norm_name, load=None, extra_load=None,
                           extra_pool=None):
            turn = row_turn() if load is not None else 0
            again = norms[0]
            norms[0] += 1
            if not again:
                norm_sems.update((n, sem("norm_" + n)) for n in
                                 "scaled turned kept_act kept_dve eps_set".split())
            scaled, turned, kept_act, kept_dve, eps_set = norm_sems.values()
            squared, rooted, inverted = rms.values()
            r, g0 = TT * again, 2 * TT * again
            ms, sd, rs, eps = small[:, 0:8], small[:, 8:16], small[:, 16:24], small[:, 24:25]
            with nc.Block() as block:
                @block.sync
                def _(sp):
                    if rows is not None:
                        for t in range(TT):
                            sp.dma_start(rows[:, t, :], load[:, t, :]).then_inc(row_in[t], 16)
                    if extra_load:
                        extra_load(sp)

                @block.gpsimd
                def _(pool):
                    if extra_pool:
                        extra_pool(pool)

                @block.scalar
                def _(act):
                    act.wait_ge(eps_set, again + 1)
                    for t in range(TT if rows is not None else 0):
                        act.wait_ge(row_in[t], 16 * turn)
                        if t:
                            act.wait_ge(squared, r + t)
                        act.activation(scratch, rows[:, t, :], ACT.Square, accum_out=ms[:, t:t + 1]).then_inc(squared, 1)
                        act.wait_ge(squared, r + t + 1)
                        act.activation(sd[:, t:t + 1], ms[:, t:t + 1], ACT.Sqrt, bias=eps, scale=1.0 / D).then_inc(rooted, 1)
                    act.wait_ge(const_in, 16 * 3)
                    for g in range(2 * TT):
                        half, k = divmod(g, KT)
                        act.wait_ge(turned, g0 + g + 1)
                        act.activation(high[:, k, half * HB:(half + 1) * HB], PS[g % 4][:], ACT.Copy,
                                       scale=col(norm_name, k)).then_inc(kept_act, 1)

                @block.vector
                def _(dve):
                    dve.memset(eps, EPS).then_inc(eps_set, 1)
                    for t in range(TT if rows is not None else 0):
                        dve.wait_ge(rooted, r + t + 1)
                        dve.reciprocal(rs[:, t:t + 1], sd[:, t:t + 1]).then_inc(inverted, 1)
                        dve.wait_ge(inverted, r + t + 1)
                        dve.tensor_scalar(normed[:, t, :], rows[:, t, :], rs[:, t:t + 1], None, ALU.mult).then_inc(scaled, 1)
                        if t == 3:
                            dve.wait_ge(const_in, 16 * 3)
                    for g in range(2 * TT):
                        half, k = divmod(g, KT)
                        cols = slice(half * HB, (half + 1) * HB)
                        dve.wait_ge(kept_act, g0 + g + 1)
                        dve.scalar_tensor_tensor(out=low[:, k, cols], in0=PS[g % 4][:], scalar=col(norm_name, k),
                                                 in1=high[:, k, cols].bitcast(F), op0=ALU.mult, op1=ALU.subtract
                                                 ).then_inc(kept_dve, 1)

                @block.tensor
                def _(pe):
                    pe.wait_ge(const_in, 16 * 3)
                    for g in range(16):
                        half, k = divmod(g, KT)
                        if g % KT == 0 and rows is not None:
                            pe.wait_ge(scaled, r + 4 * half + 4)
                        if g >= 4:
                            pe.wait_ge(kept_dve, g0 + g - 3)
                        for j in range(4):
                            last = pe.transpose(PS[g % 4][:, j * P:(j + 1) * P],
                                                normed[:, 4 * half + j, k * P:(k + 1) * P], ident[:])
                        last.then_inc(turned, 1)

        VQ = sb("VQ", [P, KT, T])
        GV = sb("GV", [P, 4, T])
        w_in = [sem("w_in0"), sem("w_in1")]
        parts = sem("parts")
        wv_in, h1_out = sem("wv_in"), sem("h1_out")
        h1_dram = nc.dram_tensor("h1_dram", (P, TT, D), F, kind="Internal").ap()
        W1 = GV[:, 0:2, :].rearrange("p n (k c) -> p n k c", k=KT)
        WV = GV[:, 2:4, :].rearrange("p a (k c) -> p (a k) c", c=256)
        layer0 = ExitStack()
        with layer0:
            AR = sb("AR", [P, 2, PAIRS, T], ctx=layer0)
            BK = sb("BK", [P, 2, PAIRS, T], ctx=layer0)
            VT = VQ[:, 0:PAIRS, :]
            QK = VQ[:, PAIRS:, :].rearrange("p (a q) t -> p a q t", a=2)
            bdones = sb("bdones", [P, P], ctx=layer0)
            G = sb("G", [P, PAIRS, NC], ctx=layer0)
            GG = sb("GG", [P, GP, NC], ctx=layer0)
            ar_tiles, bk_tiles = (b[:, :, :, :].rearrange("p a b t -> p (a b) t") for b in (AR, BK))

            gate_dram = nc.dram_tensor("gate_dram", (KT, P, T), F, kind="Internal").ap()
            gate_out = sem("gate_out")
            half1 = ExitStack()
            with half1:
                HNH, HNL = (sb(n, [P, KT, T], FR, ctx=half1) for n in ("HNH0", "HNL0"))
                WH, WL = (sb(n, [P, 2, KT, P], FR, ctx=half1) for n in ("WH0", "WL0"))
                WA = sb("WA", [P, KT, P], ctx=half1)
                RAW = sb("RAW", [P, 2, T + 1], ctx=half1)
                WBK = BK[:, 0, 3, :].rearrange("p (k c) -> p k c", k=KT)
                xw, wup_sb, scanm = AR[:, 1, 3, :], VT[:, 3, :], AR[:, 0, 3, :]
                WRAW = RAW[:, 0, 0:T].rearrange("p (k c) -> p k c", k=KT)
                gk_sb, gate_row = RAW[0:16, 1, 0:256], RAW[:, 1, 0:T]

                def const_loads(sp):
                    for n, slot in enumerate((WA[:], WBK)):
                        sp.dma_start(slot, w0t[n]).then_inc(w_in[n], 16)
                    sp.dma_start(bdones[:], bdones_d).then_inc(const2_in, 16)
                    sp.dma_start(wup_sb, wup).then_inc(const2_in, 16)

                def first_tiles(pool):
                    for n, slot in enumerate((WA[:], WBK)):
                        pool.wait_ge(w_in[n], 16)
                        split_parts(pool, slot, WH[:, n], WL[:, n], 2 * n, parts)

                with nc.Block() as block:
                    @block.sync
                    def _(sp):
                        sp.dma_start(par_sb[:], par).then_inc(const_in, 16)
                        sp.dma_start(ident[:], ident_d).then_inc(const_in, 16)
                        sp.dma_start(istack[:], istack_d).then_inc(const_in, 16)

                norm_transpose(ar_tiles, ar_tiles, BK[:, 0, 0, :], HNH, HNL, "norm0",
                               load=x.rearrange("(t p) d -> p t d", p=P), extra_load=const_loads,
                               extra_pool=first_tiles)
                project0(nc, sem, PS, HNH, HNL, WA, WBK, WRAW, WH, WL, parts, wup_sb, xw, gk_sb, gkup, gate_row,
                         gate_dram, gate_out, RAW, scanm, scan_d, AR, BK, VT, QK, GV, bdones, G, GG, small, w0t, col, const2_in,
                         w_in)
            SG = sb("SG", [P, KT, T], ctx=layer0)
            wo_in = [sem(f"wo_in{i}") for i in range(4)]
            loop = ExitStack()
            with loop:
                chunks0(nc, sb, sem, loop, PS, AR, BK, VT, QK, GV, G, GG, small, ident, istack, maska_d, maskd_d,
                        maskb_d, SG, col("gla_norm"), bk_tiles, wout0, wo_in, gate_dram, gate_out)

            H1 = sb("H1", [P, TT, D], ctx=layer0)
            SQ = sb("SQ", [P, D], ctx=layer0)

            def next_loads(sp):
                sp.dma_start(WV, wv1).then_inc(wv_in, 16)
                for n in range(2):
                    sp.dma_start(W1[:, n], w1t[n]).then_inc(w_in[n], 16)

            mix_and_out_project(nc, sem, PS, AR, VT, SG, bdones, col, small,
                                x.rearrange("(t p) d -> p t d", p=P), ar_tiles, bk_tiles, H1, VQ, SQ, wo_in, row_in,
                                row_turn(), next_loads, rms, TT, rows, h1_dram, h1_out)

        layer1 = ExitStack()
        with layer1:
            HNH, HNL = (sb(n, [P, KT, T], FR, ctx=layer1) for n in ("HNH", "HNL"))
            WH, WL = (sb(n, [P, 2, KT, P], FR, ctx=layer1) for n in ("WH", "WL"))
            KTT = sb("KTT", [P, 2, T + P], ctx=layer1)
            V1 = sb("V1", [P, TT + 1, 256], ctx=layer1)
            KH, KL = (sb(n, [P, 2, 2, 2 * P], FR, ctx=layer1) for n in ("KH", "KL"))
            BV = sb("BV", [P, 256], ctx=layer1)
            COS, SIN, SW = (sb(n, [P, T], ctx=layer1) for n in ("COS", "SIN", "SW"))
            SG1 = VQ
            band = GV[:, 3, 0:4 * P].rearrange("p (b k) -> p b k", b=2)
            rope_in, band_in = sem("rope_in"), sem("band_in")
            staged = sem("staged")
            w0_turns, w1_turns = W0_TILES // 2, (W0_TILES + W1_TILES) // 2
            values = ExitStack()
            with values:
                WVH, WVL = (sb(n, [P, KT, 256], FR, ctx=values) for n in ("WVH", "WVL"))

                def rope_loads(sp):
                    sp.wait_ge(h1_out, 16 * TT)
                    for dst, src in ((BV, bv1), (COS, cos_d), (SIN, sin_d)):
                        sp.dma_start(dst[:], src).then_inc(rope_in, 16)

                def first_parts(pool):
                    pool.wait_ge(h1_out, 16 * TT)
                    pool.wait_ge(wv_in, 16)
                    split_parts(pool, WV, WVH[:], WVL[:], 2 * W0_TILES, parts)

                def tile_parts(pool):
                    for n in range(2):
                        pool.wait_ge(w_in[n], 16 * w0_turns + 16)
                        split_parts(pool, W1[:, n], WH[:, n], WL[:, n], 2 * (W0_TILES + 1 + n), parts)

                norm_transpose(None, VQ, None, HNH, HNL, "norm1", extra_load=rope_loads, extra_pool=first_parts)
                project_values(nc, sem, PS, HNH, HNL, WVH, WVL, BV, KTT, V1, band, band_d, band_in, rope_in,
                               tile_parts)
            QT = sb("QT", [P, Q_TILES, T], ctx=layer1)
            project1(nc, sem, PS, HNH, HNL, W1, WH, WL, COS, SIN, SW, QT, KTT, SG1, small, w1t, col, w_in, w0_turns,
                     parts, KH, KL, staged)
            WOH, WOL = HNH, HNL
            split = sem("wo1_split")
            turn = row_turn()
            attend(nc, sb, sem, layer1, staged, WH, WL, KH, KL, PS, QT, KTT, V1, SG1, band, band_in, small, col, ident,
                   [GV[:, i, :] for i in range(3)] + [COS[:]], h1_dram, row_in, WOH, WOL, (SIN, SW), w_in, w1_turns,
                   wout1, split)
            BO, FN = KTT[:, :, :].rearrange("p j t -> p (j t)")[:, 0:D], V1[:, 0:4, :].rearrange("p t v -> p (t v)")
            out_project(nc, sem, PS, SG1, WH, WL, WOH, WOL, QT, (BO, FN), (bout1, fnorm), small, SIN[:],
                        out.rearrange("(t p) d -> p t d", p=P), split, rms, 2 * TT, rows, row_in, turn)


def project0(nc, sem, PS, HNH, HNL, WA, WBK, WRAW, WH, WL, parts, wup_sb, xw, gk_sb, gkup, gate_row, gate_dram,
             gate_out, RAW, scanm, scan_d, AR, BK, VT, QK, GV, bdones, G, GG, small, w0t, col, const_in, w_in):
    mixd, kmix, kk, sa = (QK[:, i // 2, i % 2, :] for i in range(4))
    nrm, cum, e2, sw = (GV[:, i, :] for i in range(4))
    e1a, sq, scan_again = sw, nrm, kk
    PAIRED = 3 * PAIRS + 1

    def arrival(n):
        return WA[:] if n % 2 == 0 or n == PAIRED else WBK if n < PAIRED else WRAW

    nka, mid = small[:, 32:36], small[:, 40:56]
    tile_bank = [PS[0:2], PS[2:4]]
    tile_done = sem("tile_done")
    tile_kept = sem("tile_kept")
    mixed = sem("mixed")
    xw_tanh = sem("xw_tanh")
    low_done = sem("low_done")
    low_kept = sem("low_kept")
    kk_raw = sem("kk_raw")
    kk_sq = sem("kk_sq")
    kk_sum = sem("kk_sum")
    kk_nrm = sem("kk_nrm")
    rel_done = sem("rel_done")
    exps = sem("exps")
    pair_done = sem("pair_done")
    scan_in = sem("scan_in")
    gk_in = sem("gk_in")
    step = sem("step")
    chain = sem("p0_chain")
    pad = sem("p0_pad")
    glow_kept = sem("glow_kept")
    gz_done = sem("gz_done")
    gz_kept = sem("gz_kept")
    gz_abs = sem("gz_abs")
    gz_step = sem("gz_step")
    g_rel = sem("g_rel")
    g_exp = sem("g_exp")
    g_scaled = sem("g_scaled")

    with nc.Block() as block:
        @block.sync
        def _(sp):
            sp.dma_start(scanm, scan_d).then_inc(scan_in, 16)
            for n in range(2, W0_GLA + 2):
                if n == W0_GLA + 1:
                    sp.wait_ge(mixed, PAIRED)
                    sp.dma_start(gk_sb, gkup).then_inc(gk_in, 16)
                    sp.dma_start(scan_again, scan_d).then_inc(gk_in, 16)
                else:
                    sp.wait_ge(parts, 2 * n if n in (PAIRED, PAIRED + 1) else 2 * n - 2)
                sp.dma_start(arrival(n), w0t[n]).then_inc(w_in[n % 2], 16)
            with sp.Fori(W0_GLA // 2 + 1, W0_TILES // 2) as i:
                for n in range(2):
                    sp.wait_ge(parts, 4 * i + (2 * n - 2))
                    sp.sem_inc(step, 1)
                    sp.dma_start((WA[:], WRAW)[n], w0t[ds(2 * i + n, 1)].rearrange("o p k c -> (o p) k c")
                                 ).then_inc(w_in[n], 16)

        @block.gpsimd
        def _(pool):
            for n in range(2, W0_GLA):
                pool.wait_ge(w_in[n % 2], 16 * (n // 2) + 16)
                pool.wait_ge(tile_done, n - 1)
                split_parts(pool, arrival(n), WH[:, n % 2], WL[:, n % 2], 2 * n, parts)
            with pool.Fori(W0_GLA // 2, W0_TILES // 2) as i:
                for n in range(2):
                    pool.wait_ge(w_in[n], 16 * i + 16)
                    pool.sem_inc(step, 1)
                    pool.wait_ge(tile_done, 2 * i + (n - 1))
                    pool.sem_inc(step, 1)
                    split_parts(pool, (WA[:], WRAW)[n], WH[:, n], WL[:, n], 4 * i + 2 * n, parts, carry=step)

        @block.tensor
        def _(pe):
            def tile(n, par):
                pe.wait_ge(parts, 2 * n + 2)
                if not isinstance(n, int) or n >= 2:
                    pe.wait_ge(tile_kept, n - 1)
                for h in range(2):
                    cols = slice(h * HB, (h + 1) * HB)
                    last = products3(pe, tile_bank[par][h][:], lambda k: (WH[:, par, k, :], HNH[:, k, cols]),
                                     lambda k: (WL[:, par, k, :], HNL[:, k, cols]), KT)
                last.then_inc(tile_done, 1)

            def low_rank(p):
                if p:
                    pe.wait_ge(low_kept, 2 * p)
                    pe.wait_ge(kk_nrm, p)
                for j in range(2):
                    for h in range(2):
                        last = pe.matmul(PS[4 + 2 * j + h][:], wup_sb[:, (PAIRS * j + p) * P:(PAIRS * j + p + 1) * P],
                                         xw[:, h * HB:(h + 1) * HB], start=True, stop=True)
                    last.then_inc(low_done, 1)

            tile(0, 0)
            tile(1, 1)
            pe.wait_ge(const_in, 16 * 2)
            pe.wait_ge(xw_tanh, 1)
            low_rank(0)
            for p in range(PAIRS):
                for j in range(3):
                    if p or j:
                        tile(3 * p + j + 1, (3 * p + j + 1) % 2)
                    if j == 1:
                        pe.wait_ge(kk_sq, p + 1)
                        pe.wait_ge(low_kept, 2 * p + 1)
                        for h in range(2):
                            last = pe.matmul(PS[4 + h][:], bdones[:], sq[:, h * HB:(h + 1) * HB], start=True, stop=True)
                        last.then_inc(kk_sum, 1)
                if p + 1 < PAIRS:
                    low_rank(p + 1)
            tile(W0_GLOW, W0_GLOW % 2)
            tile(W0_GLA, 0)
            pe.wait_ge(glow_kept, 1)
            pe.wait_ge(gk_in, 32)
            for j in range(GP):
                for h in range(2):
                    last = pe.matmul(PS[4 + 2 * j + h][:], gk_sb[:, j * P:(j + 1) * P], mixd[0:16, h * HB:(h + 1) * HB],
                                     start=True, stop=True)
                last.then_inc(gz_done, 1)
            tile(W0_GLA + 1, 1)
            with pe.Fori(1, (W0_TILES - W0_GLA) // 2) as i:
                for n in range(2):
                    tile(2 * i + (W0_GLA + n), n)

        @block.scalar
        def _(act):
            def keep(n, dst, func, **kw):
                act.wait_ge(tile_done, n + 1)
                for h in range(2):
                    ins = act.activation(dst[:, h * HB:(h + 1) * HB], tile_bank[n % 2][h][:], func, **kw)
                ins.then_inc(tile_kept, 1)

            def keep_raw(n):
                if n >= 2:
                    act.wait_ge(mixed, n - 1)
                keep(n, RAW[:, n % 2, 1:T + 1], ACT.Copy)

            act.wait_ge(pad, 1)
            keep_raw(0)
            act.wait_ge(mixed, 1)
            act.activation(xw[0:C, :], xw[0:C, :], ACT.Tanh).then_inc(xw_tanh, 1)
            for p in range(PAIRS):
                if p == 0:
                    keep_raw(1)
                if p:
                    act.wait_ge(pair_done, p)
                for j, bias in enumerate(("w0", "a0")):
                    act.wait_ge(low_done, 2 * p + j + 1)
                    for h in range(2):
                        ins = act.activation((sw, sa)[j][:, h * HB:(h + 1) * HB], PS[4 + 2 * j + h][:], ACT.Sigmoid,
                                             bias=col(bias, p))
                    ins.then_inc(low_kept, 1)
                if p:
                    keep_raw(1 + 3 * p)
                act.wait_ge(kk_raw, p + 1)
                act.activation(sq, kk, ACT.Square).then_inc(kk_sq, 1)
                keep_raw(2 + 3 * p)
                act.wait_ge(rel_done, p + 1)
                act.activation(G[:, p, :], G[:, p, :], ACT.Exp, scale=-DECAY)
                act.activation(e2, cum, ACT.Exp, scale=DECAY)
                act.activation(e1a, e1a, ACT.Exp, scale=-DECAY)
                act.activation(cum, cum, ACT.Exp, scale=-DECAY).then_inc(exps, 1)
                act.wait_ge(kk_sum, p + 1)
                for h in range(2):
                    ins = act.activation(nrm[:, h * HB:(h + 1) * HB], PS[4 + h][:], ACT.Sqrt)
                ins.then_inc(kk_nrm, 1)
                keep_raw(3 + 3 * p)
            act.wait_ge(pair_done, PAIRS)
            act.wait_ge(mixed, 3 * PAIRS + 1)
            act.wait_ge(tile_done, W0_GLOW + 1)
            for h in range(2):
                ins = act.activation(mixd[0:16, h * HB:(h + 1) * HB], tile_bank[W0_GLOW % 2][h][0:16, :], ACT.Copy)
            ins.then_inc(glow_kept, 1)
            act.wait_ge(glow_kept, 1)
            act.activation(small[:, 57:58], small[:, 57:58], ACT.Copy).then_inc(tile_kept, 1)
            for j in range(GP):
                z = (nrm, cum)[j]
                act.wait_ge(gz_done, j + 1)
                for h in range(2):
                    ins = act.activation(z[:, h * HB:(h + 1) * HB], PS[4 + 2 * j + h][:], ACT.Identity, bias=col("gk_bias", j))
                ins.then_inc(gz_kept, 1)
            for j in range(GP):
                l = (e2, sw)[j]
                keep(W0_GLA + j, QK[:, 0, j, :], ACT.Copy, scale=GLA_SCALE)
                act.wait_ge(gz_abs, j + 1)
                act.activation(l, l, ACT.Exp, scale=-1.0).then_inc(gz_step, 1)
                act.wait_ge(gz_step, 2 * j + 1)
                act.activation(l, l, ACT.Ln, bias=1.0).then_inc(gz_step, 1)
            for j in range(GP):
                z, l = (nrm, cum)[j], (e2, sw)[j]
                act.wait_ge(g_rel, j + 1)
                act.activation(l, z, ACT.Exp, scale=-1.0 / NORMALIZER)
                act.activation(GG[:, j, :], GG[:, j, :], ACT.Exp, scale=1.0 / NORMALIZER)
                act.activation(z, z, ACT.Exp, scale=1.0 / NORMALIZER).then_inc(g_exp, 1)
            for j in range(2, 4):
                keep(W0_GLA + j, QK[:, 1, j % 2, :], ACT.Copy)
            act.wait_ge(g_scaled, 4)
            for j in range(4):
                keep(W0_GLA + 4 + j, GV[:, j, :], ACT.Copy)
            for j in range(KT):
                if j:
                    act.wait_ge(gate_out, 16 * j)
                keep(W0_GATE + j, gate_row, ACT.Silu)
                act.wait_ge(tile_kept, W0_GATE + j + 1)
                act.dma_start(gate_dram[j], gate_row).then_inc(gate_out, 16)

        @block.vector
        def _(dve):
            count = [0]

            def link(ins):
                count[0] += 1
                ins.then_inc(chain, 1)
                dve.wait_ge(chain, count[0])

            def mix(n, mu, dst, t=mixd):
                raw = RAW[:, n % 2, :]
                dve.wait_ge(tile_kept, n + 1)
                link(dve.tensor_tensor(t, raw[:, 0:T], raw[:, 1:T + 1], ALU.subtract))
                dve.scalar_tensor_tensor(out=dst, in0=t, scalar=mu, in1=raw[:, 1:T + 1],
                                         op0=ALU.mult, op1=ALU.add).then_inc(mixed, 1)
                dve.wait_ge(mixed, n + 1)

            def by_chunk(ap):
                return ap.rearrange("p (c t) -> p c t", t=C)

            def relative(cs, dst, g):
                v = by_chunk(cs)
                link(dve.tensor_copy(mid, v[:, :, C // 2]))
                link(dve.tensor_tensor(g[:, 0:NC - 1], mid[:, 1:NC], mid[:, 0:NC - 1], ALU.subtract))
                link(dve.tensor_tensor(g[:, 0:NC - 1], g[:, 0:NC - 1], v[:, 0:NC - 1, C - 1], ALU.add))
                link(dve.tensor_tensor(by_chunk(dst), v, mid.unsqueeze(2).to_broadcast([P, NC, C]), ALU.subtract))

            dve.memset(small[:, 56:64], 0.0)
            dve.memset(RAW[:, :, 0:1], 0.0).then_inc(pad, 1)
            link(dve.memset(G[:], 0.0))
            link(dve.memset(GG[:], 0.0))
            dve.wait_ge(const_in, 16 * 2)
            link(dve.tensor_scalar(nka, col("k_a", 0, 4), -1.0, 1.0, ALU.mult, ALU.add))
            mix(0, col("mu_x"), xw, kmix)
            dve.wait_ge(scan_in, 16)
            for p in range(PAIRS):
                dve.wait_ge(low_kept, 2 * p + 2)
                link(dve.tensor_tensor_scan(cum, scanm, sw, 0.0, ALU.mult, ALU.add))
                relative(cum, cum, G[:, p, :])
                dve.tensor_tensor(e1a, cum, sw, ALU.subtract).then_inc(rel_done, 1)
                mix(1 + 3 * p, col("mu_k", p), kmix)
                dve.tensor_scalar(kk, kmix, col("k_k", p), None, ALU.mult).then_inc(kk_raw, 1)
                link(dve.tensor_scalar(mixd, sa, col("k_a", p), nka[:, p:p + 1], ALU.mult, ALU.add))
                link(dve.tensor_tensor(kmix, kmix, mixd, ALU.mult))
                dve.wait_ge(exps, p + 1)
                link(dve.tensor_tensor(BK[:, 1, p, :], kmix, e2, ALU.mult))
                mix(2 + 3 * p, col("mu_r", p), kmix)
                link(dve.tensor_tensor(AR[:, 1, p, :], kmix, cum, ALU.mult))
                dve.wait_ge(kk_nrm, p + 1)
                link(dve.tensor_scalar(nrm, nrm, 1e-12, None, ALU.max))
                link(dve.reciprocal(nrm, nrm))
                link(dve.tensor_tensor(kk, kk, nrm, ALU.mult))
                link(dve.scalar_tensor_tensor(out=AR[:, 0, p, :], in0=kk, scalar=-1.0, in1=e1a,
                                              op0=ALU.mult, op1=ALU.mult))
                link(dve.tensor_tensor(kk, kk, sa, ALU.mult))
                if p == PAIRS - 1:
                    dve.wait_ge(parts, 2 * PAIRED - 2)
                dve.tensor_tensor(BK[:, 0, p, :], kk, e2, ALU.mult).then_inc(pair_done, 1)
                dve.wait_ge(pair_done, p + 1)
                mix(3 + 3 * p, col("mu_v", p), VT[:, p, :])
            dve.wait_ge(gk_in, 32)
            for j in range(GP):
                z, l = (nrm, cum)[j], (e2, sw)[j]
                dve.wait_ge(gz_kept, j + 1)
                dve.scalar_tensor_tensor(out=l, in0=z, scalar=-1.0, in1=z, op0=ALU.mult, op1=ALU.max).then_inc(gz_abs, 1)
                dve.wait_ge(gz_step, 2 * j + 2)
                link(dve.scalar_tensor_tensor(out=z, in0=z, scalar=0.0, in1=l, op0=ALU.min, op1=ALU.subtract))
                link(dve.tensor_tensor_scan(l, scan_again, z, 0.0, ALU.mult, ALU.add))
                relative(l, z, GG[:, j, :])
                dve.tensor_copy(mid, mid).then_inc(g_rel, 1)
            for j in range(4):
                dve.wait_ge(tile_kept, W0_GLA + j + 1)
                dve.wait_ge(g_exp, GP)
                e = (nrm, cum)[j % 2] if j < 2 else (e2, sw)[j % 2]
                qk = QK[:, j // 2, j % 2, :]
                dve.tensor_tensor(qk, qk, e, ALU.mult).then_inc(g_scaled, 1)


def chunks0(nc, sb, sem, ctx, PS, AR, BK, VT, QK, GV, G, GG, small, ident, istack, maska_d, maskd_d, maskb_d,
            SG, gla_norm, next_w, w_dram, w_in, gate_dram, gate_out):
    def buf(name, shape, dt=F):
        return sb(name, shape, dt, ctx=ctx)

    maska = buf("maska", [P, 2, C])
    maskd = buf("maskd", [P, LEVELS, C], I32)
    maskb = buf("maskb", [P, LEVELS, 2, C], I32)
    RS, AS, BS, KS, VS = (buf(n, [P, PAIRS, 2, C]) for n in ("RS", "AS", "BS", "KS", "VS"))
    AB = buf("AB", [P, 2, PAIRS, 2, C])
    AK = buf("AK", [P, 2, PAIRS, 2, C])
    TM = [buf(f"TM{l}", [P, PAIRS, C]) for l in range(LEVELS - 1)]
    TB = [buf(f"TB{l}", [P, PAIRS, 2, C]) for l in range(LEVELS)]
    X = buf("X", [P, PAIRS, C])
    XT = buf("XT", [P, PAIRS, 2, C])
    RR, U, S, V = (buf(n, [P, PAIRS, C]) for n in ("RR", "U", "S", "V"))
    OB = buf("OB", [P, PAIRS, 2, C])
    BT, KTB = buf("BT", [P, PAIRS, 2, C]), buf("KTB", [P, PAIRS, 2, C])
    OC = buf("OC", [P, PAIRS, C])
    st6, mv = buf("st6", [P, PAIRS, 6]), buf("mv", [P, PAIRS, 2])
    lsd, grs = small[:, 0:4], small[:, 8:10]
    leps, geps = small[:, 12:13], small[:, 13:14]
    gss = small[:, 14:16]
    LX, LJ = LEVELS - 2, LEVELS - 1
    GQS, GKS = (buf(n, [P, GP, 2, C]) for n in ("GQS", "GKS"))
    GVS = buf("GVS", [P, GP, 2, C])
    GA = buf("GA", [P, GP, 2, C])
    GVT, GS, GO = (buf(n, [P, GP, P]) for n in ("GVT", "GS", "GO"))

    names = ("gate_in masks_in rk zero_b staged_zero joints_set zeroed staged_a staged_b staged_k staged_v "
             "staged_r g_split g_staged "
             "b_prod k_prod a_prod v_prod k_turn b_turn t_prod x_prod xt_prod r_prod u_prod o_prod m_prod ot_prod "
             "ab_kept arb_kept ak_kept x_kept tm_kept joined xt_kept v_kept kt_kept bt_kept r_kept u_kept s_added s_kept "
             "stats centred inverted rooted ob_kept out_kept "
             "g_att g_turn g_prod g_ot g_att_kept g_turn_kept g_kept g_decayed g_squared g_rooted g_inverted g_norm g_gated")
    s = {n: sem("c_" + n) for n in names.split()}
    s["step"] = sem("step")

    def halves():
        return ((h, slice(h * C, (h + 1) * C)) for h in range(2))

    def after(eng, name, n, plain=False):
        if not isinstance(n, int) or n > 0:
            eng.wait_ge(s[name], n)
            if plain:
                eng.sem_inc(s["step"], 1)

    def flat(b):
        return b[:].rearrange("p q h t -> p (q h t)")

    with nc.Block() as block:
        @block.sync
        def _(sp):
            sp.dma_start(maska[:], maska_d).then_inc(s["masks_in"], 16)
            sp.dma_start(maskd[:], maskd_d).then_inc(s["masks_in"], 16)
            sp.dma_start(maskb[:], maskb_d).then_inc(s["masks_in"], 16)
            sp.wait_ge(gate_out, 16 * KT)
            sp.dma_start(SG[:], gate_dram.rearrange("k p t -> p k t")).then_inc(s["gate_in"], 16)
            for h in range(2):
                n, cols = (h + 1) * NC // 2, slice(h * HB, (h + 1) * HB)
                sp.wait_ge(s["a_prod"], n)
                sp.wait_ge(s["staged_b"], n)
                sp.dma_start(next_w[:, 0:4, cols], w_dram[:, 0:4, cols]).then_inc(w_in[2 * h], 16)
                sp.wait_ge(s["staged_k"], n)
                sp.wait_ge(s["rk"], n)
                sp.dma_start(next_w[:, 4:8, cols], w_dram[:, 4:8, cols]).then_inc(w_in[2 * h + 1], 16)

        @block.gpsimd
        def _(pool):
            def stage(c, dst, src, done):
                at = ds(c * C, C)
                for h, rows in halves():
                    ins = pool.tensor_copy(dst[rows, :, h, :], src[rows, :, at])
                ins.then_inc(s[done], 1)

            def body(c, first=False):
                if not first:
                    after(pool, "b_turn", c)
                    stage(c, BS, BK[:, 0], "staged_b")
                after(pool, "g_prod", c)
                stage(c, GQS, QK[:, 0], "g_split")
                stage(c, GKS, QK[:, 1], "g_split")
                pool.wait_ge(s["g_split"], 2 * c + 2)
                pool.tensor_copy(GVS[:].rearrange("p q h t -> p (q h) t"), GV[:, :, ds(c * C, C)]
                                 ).then_inc(s["g_staged"], 1)
                pool.wait_ge(s["g_staged"], c + 1)
                after(pool, "k_prod", c)
                stage(c, KS, BK[:, 1], "staged_k")
                after(pool, "v_prod", c)
                stage(c, VS, VT, "staged_v")
                after(pool, "o_prod", c)
                stage(c, RS, AR[:, 1], "staged_r")
                after(pool, "k_prod", c + 1, plain=True)
                after(pool, "staged_r", c + 1, plain=True)
                for h, rows in halves():
                    r = AR[rows, 1, :, ds(c * C, C)]
                    ins = pool.tensor_tensor(r, r, BK[rows, 1, :, ds(c * C, C)], ALU.mult)
                ins.then_inc(s["rk"], 1)

            pool.wait_ge(gate_out, 16 * KT)
            for b in (GQS, GKS, KS, VS, RS):
                last = pool.memset(b[:], 0.0)
            last.then_inc(s["staged_zero"], 1)
            pool.wait_ge(s["staged_zero"], 1)
            body(0, first=True)
            with pool.Fori(1, NC) as c:
                body(c)

        @block.tensor
        def _(pe):
            def each(pairs, bank, width, base, products, done):
                n = len(products(0))
                for q in pairs:
                    for i, (lhsT, rhs) in enumerate(products(q)):
                        last = pe.matmul(PS[bank][:, base + q * width:base + (q + 1) * width], lhsT, rhs,
                                         start=(i == 0), stop=(i == n - 1))
                if done:
                    last.then_inc(s[done], 1)

            def turn(bank, src, done):
                for q in range(PAIRS):
                    last = pe.transpose(PS[bank][:, q * P:(q + 1) * P], src[:, q], ident[:])
                last.then_inc(s[done], 1)

            R4, R2 = range(PAIRS), range(GP)

            def solve(n):
                after(pe, "r_kept", n)
                after(pe, "xt_kept", LJ * n)
                each(R4, 5, C, PAIRS * C, lambda q: [(XT[:, q], RR[:, q])], "u_prod")

            def output(n):
                after(pe, "u_kept", n)
                after(pe, "staged_r", n)
                each(R4, 1, C, 0, lambda q: [(RS[:, q], S[:, q]), (AB[:, 1, q], U[:, q]), (AK[:, 1, q], V[:, q])],
                     "o_prod")
                after(pe, "bt_kept", n)
                each(R4, 6, C, 0, lambda q: [(KTB[:, q], V[:, q]), (BT[:, q], U[:, q])], "m_prod")

            def body(c, apply=True):
                at = ds(c * C, C)
                after(pe, "staged_b", c + 1)
                each(R4, 0, P, 0, lambda q: [(BS[:, q], AR[:, :, q, at])], "b_prod")
                after(pe, "staged_a", c + 1)
                each(R4, 2, C, 0, lambda q: [(AS[:, q], BK[:, 0, q, at])], "a_prod")
                if apply:
                    solve(c)
                after(pe, "ab_kept", c + 1)
                for l in range(1, LEVELS):
                    x = TM[0] if l == 1 else X
                    xt = TB[0] if l == 1 else XT
                    after(pe, "x_kept", LJ * c + l)
                    each(R4, 2, C, 0, lambda q: [(AB[:, 0, q], x[:, q])], "t_prod")
                    if l == 1:
                        if apply:
                            output(c)
                        after(pe, "g_staged", c + 1)
                        after(pe, "g_gated", c)
                        each(R2, 7, C, 0, lambda q: [(GKS[:, q], QK[:, 0, q, at])], "g_att")
                    if l == 2:
                        after(pe, "g_att_kept", c + 1)
                        for q in R2:
                            pe.transpose(PS[7][:, q * P:(q + 1) * P], GVS[:, q], ident[:])
                        for q in R2:
                            last = pe.transpose(PS[7][:, (GP + q) * P:(GP + q + 1) * P], GKS[:, q], ident[:])
                        last.then_inc(s["g_turn"], 1)
                        after(pe, "staged_k", c + 1)
                        turn(5, KS, "k_turn")
                    if l == 3:
                        after(pe, "staged_v", c + 1)
                        after(pe, "arb_kept", c + 1)
                        turn(0, VS, "v_prod")
                        if apply:
                            after(pe, "ob_kept", c)
                        each(R4, 1, P, 0, lambda q: [(KS[:, q], AR[:, :, q, at])], "k_prod")
                    if l == 4:
                        after(pe, "g_turn_kept", c + 1)
                        each(R2, 7, P, 0, lambda q: [(GA[:, q], GVT[:, q]), (GQS[:, q], GS[:, q])], None)
                        each(R2, 7, P, GP * P, lambda q: [(GKS[:, q], GVT[:, q])], "g_prod")
                        after(pe, "s_added", c)
                        turn(6, BS, "b_turn")
                        after(pe, "v_kept", c + 1)
                        if apply:
                            turn(0, OB, "ot_prod")
                    if l == LJ:
                        after(pe, "ak_kept", c + 1)
                        after(pe, "kt_kept", c + 1)
                        after(pe, "s_kept", c)
                        each(R4, 5, C, 0, lambda q: [(AK[:, 0, q], V[:, q]), (AS[:, q], S[:, q])], "r_prod")
                    if l > 1:
                        after(pe, "xt_kept", LJ * c + l - 1)
                    if l < LJ:
                        after(pe, "tm_kept", LX * c + l)
                        each(R4, 3, C, 0, lambda q: [(xt[:, q], TM[l][:, q])], "x_prod")
                    after(pe, "joined", LJ * c + l)
                    each(R4, 4, P, 0, lambda q: [(TB[l][:, q], xt[:, q])], "xt_prod")
                after(pe, "out_kept", c)
                after(pe, "g_norm", c + 1)
                for q in R2:
                    last = pe.transpose(PS[7][:, q * P:(q + 1) * P], GO[:, q], ident[:])
                last.then_inc(s["g_ot"], 1)

            body(0, apply=False)
            with pe.Fori(1, NC) as c:
                body(c)
            solve(NC)
            output(NC)
            pe.wait_ge(s["ob_kept"], NC)
            turn(0, OB, "ot_prod")

        @block.vector
        def _(dve):
            def state(n):
                after(dve, "m_prod", n)
                dve.tensor_tensor(S[:], S[:], dense(PS[6], PAIRS), ALU.add).then_inc(s["s_added"], 1)
                dve.wait_ge(s["s_added"], n)
                dve.tensor_tensor(S[:], S[:], G[:, :, ds(n - 1, 1)].to_broadcast([P, PAIRS, C]), ALU.mult
                                  ).then_inc(s["s_kept"], 1)

            def statistics(n):
                after(dve, "o_prod", n, plain=True)
                o = dense(PS[1], PAIRS)
                for q in range(PAIRS):
                    ins = dve.bn_stats(st6[:, q], o[:, q])
                ins.then_inc(s["stats"], 1)
                dve.wait_ge(s["stats"], 2 * n - 1)
                dve.sem_inc(s["step"], 1)
                for q in range(PAIRS):
                    ins = dve.bn_aggr(mv[:, q], st6[:, q])
                ins.then_inc(s["stats"], 1)

            def normalise(n):
                dve.wait_ge(s["stats"], 2 * n)
                dve.tensor_tensor(OC[:], dense(PS[1], PAIRS), mv[:, :, 0:1].to_broadcast([P, PAIRS, C]), ALU.subtract
                                  ).then_inc(s["centred"], 1)
                dve.wait_ge(s["rooted"], n)
                dve.reciprocal(lsd, lsd).then_inc(s["inverted"], 1)
                dve.wait_ge(s["centred"], n)
                dve.wait_ge(s["inverted"], n)
                for h, rows in halves():
                    ins = dve.tensor_tensor(OB[rows, :, h, :], OC[rows], lsd[rows].unsqueeze(2).to_broadcast([C, PAIRS, C]),
                                            ALU.mult)
                ins.then_inc(s["ob_kept"], 1)

            def gate_gla(n):
                after(dve, "g_ot", n, plain=True)
                sg = SG[:, 0:4, ds((n - 1) * C, C)]
                dve.scalar_tensor_tensor(out=sg, in0=PS[7][:, 0:GP * P].rearrange("p (q t) -> p q t", t=C),
                                         scalar=gla_norm, in1=sg, op0=ALU.mult, op1=ALU.mult).then_inc(s["g_gated"], 1)

            def body(c, apply=True):
                b = PS[0][:].rearrange("p (q a t) -> p q a t", q=PAIRS, a=2)

                def mask_to(dst, src, kind, done):
                    for h, rows in halves():
                        ins = dve.tensor_tensor(dst[rows, kind, :, h, :], src[rows, :, kind],
                                                maska[rows, kind:kind + 1].to_broadcast([C, PAIRS, C]), ALU.mult)
                    if done:
                        ins.then_inc(s[done], 1)

                after(dve, "b_prod", c + 1)
                mask_to(AB, b, 0, "ab_kept")
                after(dve, "a_prod", c + 1, plain=True)
                dve.copy_predicated(TM[0][:], maskd[:, 0].unsqueeze(1).to_broadcast([P, PAIRS, C]),
                                    dense(PS[2], PAIRS)).then_inc(s["x_kept"], 1)
                dve.copy_predicated(TB[0][:], maskb[:, 0].unsqueeze(1).to_broadcast([P, PAIRS, 2, C]),
                                    b[:, :, 0:1, :].to_broadcast([P, PAIRS, 2, C]))
                if apply:
                    gate_gla(c)
                for l in range(1, LEVELS):
                    after(dve, "t_prod", LJ * c + l, plain=True)
                    t = dense(PS[2], PAIRS)
                    if l < LJ:
                        dve.copy_predicated(TM[l][:], maskd[:, l].unsqueeze(1).to_broadcast([P, PAIRS, C]), t
                                            ).then_inc(s["tm_kept"], 1)
                    dve.copy_predicated(TB[l][:], maskb[:, l].unsqueeze(1).to_broadcast([P, PAIRS, 2, C]),
                                        t.unsqueeze(2).to_broadcast([P, PAIRS, 2, C])).then_inc(s["joined"], 1)
                    if l == 1:
                        if apply:
                            statistics(c)
                        mask_to(AB, b, 1, "arb_kept")
                        after(dve, "g_att", c + 1, plain=True)
                        for h, rows in halves():
                            ins = dve.copy_predicated(
                                GA[rows, :, h, :], maska[rows, 1:2, :].to_broadcast([C, GP, C]).bitcast(I32),
                                PS[7][rows, 0:GP * C].rearrange("p (q t) -> p q t", q=GP))
                        ins.then_inc(s["g_att_kept"], 1)
                    if l < LJ:
                        after(dve, "x_prod", LX * c + l)
                        dve.tensor_copy(X[:], dense(PS[3], PAIRS)).then_inc(s["x_kept"], 1)
                    if l == 2 and apply:
                        normalise(c)
                    if l == 3:
                        after(dve, "k_prod", c + 1)
                        k = PS[1][:].rearrange("p (q a t) -> p q a t", q=PAIRS, a=2)
                        mask_to(AK, k, 0, None)
                        mask_to(AK, k, 1, "ak_kept")
                        if apply:
                            state(c)
                    if l == 4:
                        after(dve, "g_prod", c + 1)
                        g = PS[7][:].rearrange("p (a q v) -> p a q v", a=2, q=GP)
                        dve.tensor_copy(GO[:], g[:, 0])
                        dve.tensor_tensor(GS[:], GS[:], g[:, 1], ALU.add).then_inc(s["g_kept"], 1)
                        dve.wait_ge(s["g_kept"], c + 1)
                        dve.tensor_tensor(GS[:], GS[:], GG[:, :, ds(c, 1)].to_broadcast([P, GP, P]), ALU.mult
                                          ).then_inc(s["g_decayed"], 1)
                        dve.wait_ge(s["g_decayed"], c + 1)
                after(dve, "g_rooted", c + 1)
                dve.reciprocal(grs, grs).then_inc(s["g_inverted"], 1)
                dve.wait_ge(s["g_inverted"], c + 1)
                for q in range(GP):
                    ins = dve.tensor_scalar(GO[:, q], GO[:, q], grs[:, q:q + 1], None, ALU.mult)
                ins.then_inc(s["g_norm"], 1)

            dve.memset(BS[:], 0.0)
            dve.memset(AS[:], 0.0).then_inc(s["zero_b"], 1)
            dve.wait_ge(s["zero_b"], 1)
            for h, rows in halves():
                ins = dve.tensor_copy(BS[rows, :, h, :], BK[rows, 0, :, 0:C])
            ins.then_inc(s["staged_b"], 1)
            dve.memset(leps, LN_EPS)
            for b in (AB, AK, S, OB):
                dve.memset(b[:], 0.0)
            dve.wait_ge(gate_out, 16 * KT)
            for b in (GA, GS):
                dve.memset(b[:], 0.0)
            dve.memset(geps, EPS).then_inc(s["zeroed"], 1)
            dve.wait_ge(s["zeroed"], 1)
            dve.wait_ge(s["joints_set"], 1)
            dve.wait_ge(s["masks_in"], 48)
            body(0, apply=False)
            dve.wait_ge(s["gate_in"], 16)
            with dve.Fori(1, NC) as c:
                body(c)
            gate_gla(NC)
            statistics(NC)
            normalise(NC)
            state(NC)

        @block.scalar
        def _(act):
            def keep(dst, src, done):
                act.activation(dst, src, ACT.Copy).then_inc(s[done], 1)

            def keep_diagonal(dst, bank, done):
                b = PS[bank][:].rearrange("p (q h t) -> p q h t", q=PAIRS, h=2)
                for h, rows in halves():
                    ins = act.activation(dst[rows], b[rows, :, h, :], ACT.Copy)
                ins.then_inc(s[done], 1)

            def keep_u(n):
                after(act, "u_prod", n)
                keep(U[:], PS[5][:, PAIRS * C:2 * PAIRS * C].rearrange("p (q v) -> p q v", q=PAIRS), "u_kept")

            def root(n):
                after(act, "stats", 2 * n)
                act.activation(lsd, mv[:, :, 1], ACT.Sqrt, bias=leps).then_inc(s["rooted"], 1)

            def keep_output(n):
                after(act, "ot_prod", n)
                keep_diagonal(AR[:, 0, :, ds((n - 1) * C, C)], 0, "out_kept")

            def stage_a(c):
                for h, rows in halves():
                    ins = act.activation(AS[rows, :, h, :], AR[rows, 0, :, ds(c * C, C)], ACT.Copy)
                ins.then_inc(s["staged_a"], 1)

            def body(c, apply=True, last=False):
                if apply:
                    keep_u(c)
                for l in range(1, LEVELS):
                    if l == LJ:
                        after(act, "r_prod", c + 1)
                        keep(RR[:], dense(PS[5], PAIRS), "r_kept")
                        if not last:
                            stage_a(c + 1)
                    if l == 1 and apply:
                        root(c)
                    after(act, "xt_prod", LJ * c + l)
                    keep(flat(XT), PS[4][:], "xt_kept")
                    if l == 2:
                        after(act, "g_turn", c + 1)
                        act.activation(GVT[:].rearrange("p q v -> p (q v)"), PS[7][:, 0:GP * P], ACT.Copy)
                        keep(flat(GKS), PS[7][:, GP * P:2 * GP * P], "g_turn_kept")
                        after(act, "k_turn", c + 1)
                        keep(flat(KTB), PS[5][:], "kt_kept")
                    if l == 3:
                        after(act, "v_prod", c + 1)
                        keep_diagonal(V[:], 0, "v_kept")
                    if l == 4:
                        after(act, "b_turn", c + 1)
                        keep(flat(BT), PS[6][:], "bt_kept")
                        if apply:
                            keep_output(c)
                        after(act, "g_kept", c + 1)
                        for q in range(GP):
                            ins = act.activation(GVT[:, q], GO[:, q], ACT.Square, accum_out=gss[:, q:q + 1])
                        ins.then_inc(s["g_squared"], 1)
                        act.wait_ge(s["g_squared"], c + 1)
                        act.activation(grs, gss, ACT.Sqrt, scale=1.0 / P, bias=geps).then_inc(s["g_rooted"], 1)

            act.wait_ge(s["zero_b"], 1)
            stage_a(0)
            for b in TM:
                act.activation(b[:], istack[:].unsqueeze(1).to_broadcast([P, PAIRS, C]), ACT.Copy)
            for b in TB:
                ins = act.activation(b[:].rearrange("p q h t -> p q (h t)"),
                                     ident[:].unsqueeze(1).to_broadcast([P, PAIRS, P]), ACT.Copy)
            ins.then_inc(s["joints_set"], 1)
            act.wait_ge(s["zeroed"], 1)
            body(0, apply=False)
            with act.Fori(1, NC - 1) as c:
                body(c)
            body(NC - 1, last=True)
            keep_u(NC)
            root(NC)
            keep_output(NC)


def dense(bank, n):
    return bank[:, 0:n * C].rearrange("p (q t) -> p q t", t=C)
def mix_and_out_project(nc, sem, PS, AR, VT, SG, bdones, col, small, x_dram, XR, W, H1, normed_rows, scratch,
                        w_in, row_in, turn, next_loads, rms, r, rows, h1_dram, h1_out):
    names = ("rk summed affine bonus chain gated")
    s = {n: sem("m_" + n) for n in names.split()}
    s.update(rms)
    s.update(rows)
    AHEAD = 3
    ms, sd, rs, eps = small[:, 0:8], small[:, 8:16], small[:, 16:24], small[:, 24:25]
    with nc.Block() as block:
        @block.sync
        def _(sp):
            sp.wait_ge(s["gated"], 2 * PAIRS)
            for t in range(TT):
                sp.dma_start(XR[:, t, :], x_dram[:, t, :]).then_inc(row_in[t], 16)
            next_loads(sp)
            for t in range(TT):
                sp.wait_ge(s["added"], t + 1)
                sp.dma_start(h1_dram[:, t, :], H1[:, t, :]).then_inc(h1_out, 16)

        @block.tensor
        def _(pe):
            def products(t, ks):
                for h in range(2):
                    for k in ks:
                        last = pe.matmul(PS[2 * (t % 4) + h][:], SG[:, k, t * P:(t + 1) * P], W[:, k, h * HB:(h + 1) * HB],
                                         start=(k == 0), stop=(k == KT - 1))
                return last

            def sums(i):
                h, p = divmod(i, PAIRS)
                pe.wait_ge(s["rk"], i + 1)
                if i >= 2:
                    pe.wait_ge(s["bonus"], i - 1)
                pe.matmul(PS[6 + i % 2][:], bdones[:], AR[:, 1, p, h * HB:(h + 1) * HB], start=True, stop=True
                          ).then_inc(s["summed"], 1)

            for loaded in w_in:
                pe.wait_ge(loaded, 16)
            for t in range(AHEAD):
                products(t, range(4))
                sums(2 * t)
                sums(2 * t + 1)
            for t in range(TT):
                if t == 0 or t == 4:
                    pe.wait_ge(s["gated"], PAIRS * (t // 4 + 1))
                if t == 3:
                    pe.wait_ge(s["bonus"], 2 * PAIRS)
                if t >= 4:
                    pe.wait_ge(s["added"], t - 3)
                products(t, range(4, KT) if t < AHEAD else range(KT)).then_inc(s["done"], 1)
                if t == 0:
                    sums(2 * PAIRS - 2)
                    sums(2 * PAIRS - 1)

        @block.scalar
        def _(act):
            for h in range(2):
                for p in range(PAIRS):
                    rk, o = (AR[:, i, p, h * HB:(h + 1) * HB] for i in (1, 0))
                    act.activation(rk, rk, ACT.Copy, scale=col("r_k", p)).then_inc(s["rk"], 1)
                    act.activation(o, o, ACT.Identity, scale=col("ln_w", p), bias=col("ln_b", p)).then_inc(s["affine"], 1)
            for t in range(TT):
                act.wait_ge(s["added"], t + 1)
                if t:
                    act.wait_ge(s["squared"], r + t)
                act.activation(scratch[:], H1[:, t, :], ACT.Square, accum_out=ms[:, t:t + 1]).then_inc(s["squared"], 1)
                act.wait_ge(s["squared"], r + t + 1)
                act.activation(sd[:, t:t + 1], ms[:, t:t + 1], ACT.Sqrt, bias=eps, scale=1.0 / D).then_inc(s["rooted"], 1)

        @block.vector
        def _(dve):
            count = [0]

            def link(ins):
                count[0] += 1
                ins.then_inc(s["chain"], 1)
                dve.wait_ge(s["chain"], count[0])

            for i in range(2 * PAIRS):
                h, p = divmod(i, PAIRS)
                cols = slice(h * HB, (h + 1) * HB)
                o, v, sg = AR[:, 0, p, cols], VT[:, p, cols], SG[:, 4 + p, cols]
                dve.wait_ge(s["summed"], i + 1)
                dve.tensor_tensor(v, v, PS[6 + i % 2][:], ALU.mult).then_inc(s["bonus"], 1)
                dve.wait_ge(s["bonus"], i + 1)
                dve.wait_ge(s["affine"], i + 1)
                link(dve.tensor_tensor(o, o, v, ALU.add))
                dve.tensor_tensor(sg, sg, o, ALU.mult).then_inc(s["gated"], 1)

            def norm(t):
                dve.wait_ge(s["rooted"], r + t + 1)
                dve.reciprocal(rs[:, t:t + 1], sd[:, t:t + 1]).then_inc(s["inverted"], 1)
                dve.wait_ge(s["inverted"], r + t + 1)
                dve.tensor_scalar(normed_rows[:, t, :], H1[:, t, :], rs[:, t:t + 1], None, ALU.mult
                                  ).then_inc(s["normed"], 1)

            dve.wait_ge(s["gated"], 2 * PAIRS)
            for t in range(TT):
                dve.wait_ge(row_in[t], 16 * turn)
                dve.wait_ge(s["done"], t + 1)
                for h in range(2):
                    ins = dve.tensor_tensor(H1[:, t, h * HB:(h + 1) * HB], PS[2 * (t % 4) + h][:],
                                            XR[:, t, h * HB:(h + 1) * HB], ALU.add)
                ins.then_inc(s["added"], 1)
                if t:
                    norm(t - 1)
            norm(TT - 1)


def split_parts(eng, raw, high, low, n, parts, carry=None):
    eng.tensor_copy(high, raw).then_inc(parts, 1)
    eng.wait_ge(parts, n + 1)
    if carry is not None:
        eng.sem_inc(carry, 1)
    eng.tensor_tensor(low, raw, high.bitcast(F), ALU.subtract).then_inc(parts, 1)


def products3(pe, out, highs, lows, n):
    for k in range(n):
        (ah, bh), (al, bl) = highs(k), lows(k)
        for i, (a, b) in enumerate(((ah, bh), (al, bh), (ah, bl))):
            last = pe.matmul(out, a, b, start=(k == 0 and i == 0), stop=(k == n - 1 and i == 2))
    return last


def out_project(nc, sem, PS, A, AH, AL, WH, WL, R, tables, tables_dram, small, scratch, out, split, rms, r, rows,
                row_in, turn):
    BO, FN = tables
    names = "high low biased stored tables_in"
    s = {n: sem("o1_" + n) for n in names.split()}
    s.update(rms)
    s.update(rows)
    ms, sd, eps = (small[:, i:j] for i, j in ((0, 8), (8, 16), (24, 25)))
    with nc.Block() as block:
        @block.sync
        def _(sp):
            for dst, src in zip(tables, tables_dram):
                sp.dma_start(dst, src).then_inc(s["tables_in"], 16)
            for t in range(TT):
                sp.wait_ge(s["normed"], TT + t + 1)
                sp.dma_start(out[:, t, :], R[:, t, :]).then_inc(s["stored"], 16)
            sp.wait_ge(s["stored"], 16 * TT)

        @block.tensor
        def _(pe):
            pe.wait_ge(split, 2 * KT)
            for t in range(TT):
                pe.wait_ge(s["low"], t + 1)
                if t >= 4:
                    pe.wait_ge(s["added"], TT + t - 3)
                for h in range(2):
                    cols = slice(h * HB, (h + 1) * HB)
                    last = products3(pe, PS[2 * (t % 4) + h][:], lambda k: (AH[:, t % 2, k, :], WH[:, k, cols]),
                                     lambda k: (AL[:, t % 2, k, :], WL[:, k, cols]), KT)
                last.then_inc(s["done"], 1)

        @block.gpsimd
        def _(pool):
            pool.wait_ge(s["tables_in"], 32)
            for t in range(TT):
                pool.wait_ge(row_in[t], 16 * turn)
                pool.tensor_tensor(R[:, t, :], R[:, t, :], BO, ALU.add).then_inc(s["biased"], 1)

        @block.scalar
        def _(act):
            def high(t):
                if t >= 2:
                    act.wait_ge(s["done"], TT + t - 1)
                act.activation(AH[:, t % 2], A[:, :, t * P:(t + 1) * P], ACT.Copy).then_inc(s["high"], 1)

            high(0)
            high(1)
            for t in range(TT):
                act.wait_ge(s["added"], TT + t + 1)
                act.activation(scratch, R[:, t, :], ACT.Square, accum_out=ms[:, t:t + 1]).then_inc(s["squared"], 1)
                act.wait_ge(s["squared"], r + t + 1)
                act.activation(sd[:, t:t + 1], ms[:, t:t + 1], ACT.Sqrt, bias=eps, scale=1.0 / D).then_inc(s["rooted"], 1)
                if t + 2 < TT:
                    high(t + 2)

        @block.vector
        def _(dve):
            def low(t):
                dve.wait_ge(s["high"], t + 1)
                dve.tensor_tensor(AL[:, t % 2], A[:, :, t * P:(t + 1) * P], AH[:, t % 2].bitcast(F), ALU.subtract
                                  ).then_inc(s["low"], 1)

            def finish(t):
                dve.wait_ge(s["rooted"], r + t + 1)
                dve.reciprocal(sd[:, t:t + 1], sd[:, t:t + 1]).then_inc(s["inverted"], 1)
                dve.wait_ge(s["inverted"], r + t + 1)
                dve.scalar_tensor_tensor(out=R[:, t, :], in0=R[:, t, :], scalar=sd[:, t:t + 1], in1=FN,
                                         op0=ALU.mult, op1=ALU.mult).then_inc(s["normed"], 1)

            low(0)
            low(1)
            for t in range(TT):
                dve.wait_ge(s["biased"], t + 1)
                dve.wait_ge(s["done"], TT + t + 1)
                for h in range(2):
                    cols = slice(h * HB, (h + 1) * HB)
                    ins = dve.tensor_tensor(R[:, t, cols], R[:, t, cols], PS[2 * (t % 4) + h][:], ALU.add)
                ins.then_inc(s["added"], 1)
                if t + 2 < TT:
                    low(t + 2)
                if t:
                    finish(t - 1)
            finish(TT - 1)


def project_values(nc, sem, PS, HNH, HNL, WVH, WVL, BV, KTT, V1, band, band_d, band_in, rope_in, extra_pool):
    v_done, v_kept = sem("p1_v_done"), sem("p1_v_kept")
    with nc.Block() as block:
        @block.sync
        def _(sp):
            sp.dma_start(band, band_d).then_inc(band_in, 16)

        @block.gpsimd
        def _(pool):
            extra_pool(pool)

        @block.tensor
        def _(pe):
            for t in range(TT):
                if t >= 2:
                    pe.wait_ge(v_kept, t - 1)
                tokens = slice(t * P, (t + 1) * P)
                products3(pe, PS[4 + t % 2][:, 0:256], lambda k: (HNH[:, k, tokens], WVH[:, k, :]),
                          lambda k: (HNL[:, k, tokens], WVL[:, k, :]), KT).then_inc(v_done, 1)

        @block.vector
        def _(dve):
            dve.memset(KTT[:, :, 0:P], 0.0)
            dve.memset(V1[:, 0, :], 0.0)
            dve.wait_ge(rope_in, 48)
            for t in range(TT):
                dve.wait_ge(v_done, t + 1)
                dve.tensor_tensor(V1[:, t + 1, :], PS[4 + t % 2][:, 0:256], BV[:], ALU.add).then_inc(v_kept, 1)


def project1(nc, sem, PS, HNH, HNL, W1, WH, WL, COS, SIN, SW, QT, KTT, SG1, small, w1t, col, w_in, w_turns, parts,
             KH, KL, staged):
    tile_done, tile_kept = sem("p1_tile_done"), sem("p1_tile_kept")
    bq = sem("p1_bq")
    chain = sem("p1_chain")
    step = sem("step")
    bqs = small[:, 32:40]
    swap = [8 + i for i in range(8)] + list(range(8)) + list(range(16, 32))
    with nc.Block() as block:
        @block.sync
        def _(sp):
            with sp.Fori(1, W1_TILES // 2) as i:
                for n in range(2):
                    sp.wait_ge(parts, 4 * i + (2 * W0_TILES + 2 * n))
                    sp.sem_inc(step, 1)
                    sp.dma_start(W1[:, n], w1t[ds(2 * i + n, 1)].rearrange("o p k c -> (o p) k c")).then_inc(w_in[n], 16)
        @block.tensor
        def _(pe):
            def tile(n, par, turn):
                pe.wait_ge(parts, 2 * n + (2 * W0_TILES + 4))
                if not isinstance(n, int):
                    pe.wait_ge(tile_kept, n - 1)
                for h in range(2):
                    cols = slice(h * HB, (h + 1) * HB)
                    last = products3(pe, PS[2 * par + h][:], lambda k: (WH[:, par, k, :], HNH[:, k, cols]),
                                     lambda k: (WL[:, par, k, :], HNL[:, k, cols]), KT)
                last.then_inc(tile_done, 1)

            for n in range(2):
                tile(n, n, 0)
            with pe.Fori(1, W1_TILES // 2) as i:
                for n in range(2):
                    tile(2 * i + n, n, i)

        @block.gpsimd
        def _(pool):
            with pool.Fori(1, W1_TILES // 2) as i:
                for n in range(2):
                    pool.wait_ge(w_in[n], 16 * i + (16 * w_turns + 16))
                    pool.sem_inc(step, 1)
                    pool.wait_ge(tile_done, 2 * i + (n - 1))
                    pool.sem_inc(step, 1)
                    split_parts(pool, W1[:, n], WH[:, n], WL[:, n], 4 * i + (2 * W0_TILES + 2 * n + 2), parts,
                                carry=step)
            pool.wait_ge(chain, 4 * (Q_TILES + 2))
            pool.wait_ge(tile_done, W1_TILES - 1)
            stage_block(pool, 0, 0, QT, KTT, WH, WL, KH, KL, staged, step)

        @block.scalar
        def _(act):
            def keep(n, dst, func, **kw):
                act.wait_ge(tile_done, n + 1)
                for h in range(2):
                    ins = act.activation(dst[:, h * HB:(h + 1) * HB], PS[2 * (n % 2) + h][:], func, **kw)
                ins.then_inc(tile_kept, 1)

            act.wait_ge(bq, 1)
            for j in range(Q_TILES):
                keep(W1_Q + j, QT[:, j, :], ACT.Identity, scale=GLA_SCALE, bias=bqs[:, j:j + 1])
            for j in range(2):
                keep(W1_K + j, KTT[:, j, P:], ACT.Identity, bias=col("b_k", j))
            for j in range(KT):
                keep(W1_GATE + j, SG1[:, j, :], ACT.Silu)

        @block.vector
        def _(dve):
            count = [0]

            def link(ins):
                count[0] += 1
                ins.then_inc(chain, 1)
                dve.wait_ge(chain, count[0])

            dve.tensor_scalar(bqs, col("b_q", 0, 8), GLA_SCALE, None, ALU.mult).then_inc(bq, 1)
            for j in range(Q_TILES + 2):
                x = QT[:, j, :] if j < Q_TILES else KTT[:, j - Q_TILES, P:]
                dve.wait_ge(tile_kept, j + 1)
                link(dve.stream_shuffle(SW[:], x, swap))
                link(dve.tensor_tensor(SW[:], SW[:], SIN[:], ALU.mult))
                link(dve.tensor_tensor(x, x, COS[:], ALU.mult))
                link(dve.tensor_tensor(x, x, SW[:], ALU.add))


def stage_block(pool, n, u, QT, KTT, QH, QL, KH, KL, staged, step):
    q, k = QT[:, :, ds(n * P, P)], KTT[:, :, ds(n * P, 2 * P)]
    pool.tensor_copy(QH[:, u], q).then_inc(staged, 1)
    pool.tensor_copy(KH[:, u], k).then_inc(staged, 1)
    pool.wait_ge(staged, 4 * n + 2)
    pool.sem_inc(step, 1)
    pool.tensor_tensor(QL[:, u], q, QH[:, u].bitcast(F), ALU.subtract).then_inc(staged, 1)
    pool.tensor_tensor(KL[:, u], k, KH[:, u].bitcast(F), ALU.subtract).then_inc(staged, 1)


def attend(nc, sb, sem, ctx, staged, QH, QL, KH, KL, PS, QT, KTT, V1, SG1, band, band_in, small, col, ident, free,
           h1_dram, row_in, WOH, WOL, raw, raw_in,
           raw_turns, w_dram, split):
    NB = T // P
    SC, PR, PT = (b.rearrange("p (u a k) -> p u a k", u=2, a=2) for b in free[0:3])
    OS = free[3].rearrange("p (j q) -> p j q", j=Q_TILES)
    nm, rs, es = (sb(n, [P, 16], F, ctx=ctx) for n in ("nm", "rs_", "es"))
    nsink = sb("nsink", [P, 16], F, ctx=ctx)
    names = ("s_prod scored exped turned pt_kept pv_done o_kept o_turned gated es_in es_exp "
             "es_added es_ready setup")
    s = {n: sem("a_" + n) for n in names.split()}
    s["step"] = sem("step")
    HT = Q_TILES // 2
    STEPS = Q_TILES * NB
    with nc.Block() as block:
        def after(eng, name, n, plain=False):
            if not isinstance(n, int) or n > 0:
                eng.wait_ge(s[name], n)
                if plain:
                    eng.sem_inc(s["step"], 1)

        def there(i, count):
            return not isinstance(i, int) or 0 <= i < count

        def over_blocks(eng, body):
            for n in range(2):
                body(n, n, 0, range(Q_TILES))
            with eng.Fori(1, NB // 2) as i:
                for n in range(2):
                    body(2 * i + n, n, i, range(Q_TILES))
            body(NB, 0, 0, range(HT + 2))

        @block.sync
        def _(sp):
            for k in range(2):
                sp.dma_start(raw[k][:], w_dram[:, k, :]).then_inc(raw_in[k], 16)
            with sp.Fori(1, KT // 2) as i:
                for u in range(2):
                    sp.wait_ge(split, 4 * i + (2 * u - 2))
                    sp.sem_inc(s["step"], 1)
                    sp.dma_start(raw[u][:], w_dram[:, ds(2 * i + u, 1), :].rearrange("p o c -> p (o c)")
                                 ).then_inc(raw_in[u], 16)
            sp.wait_ge(staged, 4 * NB)
            for t in range(TT):
                sp.dma_start(QT[:, t, :], h1_dram[:, t, :]).then_inc(row_in[t], 16)

        @block.gpsimd
        def _(pool):
            def weights(k, u, turn):
                pool.wait_ge(raw_in[u], 16 * turn + 16 * (raw_turns + 1))
                pool.sem_inc(s["step"], 1)
                high, low = (w[:, ds(k, 1), :].rearrange("p o c -> p (o c)") for w in (WOH, WOL))
                split_parts(pool, raw[u][:], high, low, 2 * k, split, carry=s["step"])

            stage_block(pool, 1, 1, QT, KTT, QH, QL, KH, KL, staged, s["step"])
            for u in range(2):
                weights(u, u, 0)
            with pool.Fori(1, NB // 2) as i:
                for u in range(2):
                    after(pool, "s_prod", Q_TILES * (2 * i + (u - 1)), plain=True)
                    stage_block(pool, 2 * i + u, u, QT, KTT, QH, QL, KH, KL, staged, s["step"])
                    weights(2 * i + u, u, i)

        @block.tensor
        def _(pe):
            def scores(g, j, u):
                after(pe, "scored", g - 1)
                for a in range(2):
                    rows = slice(a * C, (a + 1) * C)
                    last = products3(pe, PS[2 * (j % 2) + a][:, 0:2 * P],
                                     lambda k: (QH[rows, u, j, :], KH[rows, u, j // 4, :]),
                                     lambda k: (QL[rows, u, j, :], KL[rows, u, j // 4, :]), 1)
                last.then_inc(s["s_prod"], 1)

            def turn_probs(t, j):
                after(pe, "exped", t + 1)
                after(pe, "pt_kept", t - 1)
                for a in range(2):
                    for b in range(2):
                        last = pe.transpose(PS[4 + j % 2][:, (2 * a + b) * P:(2 * a + b + 1) * P],
                                            PR[:, j % 2, a, b * P:(b + 1) * P], ident[:])
                last.then_inc(s["turned"], 1)

            def values(t, j, n, half):
                after(pe, "pt_kept", t + 1)
                if j % HT == 0:
                    after(pe, "gated", half - 1)
                for a in range(2):
                    kv = 2 * (j // 4) + a
                    for b in range(2):
                        last = pe.matmul(PS[6 + j // HT][:, (j % HT) * P + a * C:(j % HT) * P + (a + 1) * C],
                                         PT[:, j % 2, a, b * P:(b + 1) * P],
                                         V1[:, ds(n + b, 1), kv * C:(kv + 1) * C].rearrange("p o v -> p (o v)"),
                                         start=(b == 0), stop=(b == 1))
                last.then_inc(s["pv_done"], 1)

            def turn_output(half, b):
                after(pe, "o_kept", half + 1)
                for j in range(HT):
                    last = pe.transpose(PS[6 + b][:, j * P:(j + 1) * P], OS[:, HT * b + j, :], ident[:])
                last.then_inc(s["o_turned"], 1)

            def body(n, u, turn, steps):
                for j in steps:
                    g, half = Q_TILES * n + j, 2 * n + j // HT
                    if there(g, STEPS):
                        if j == 0:
                            pe.wait_ge(staged, 4 * n + 4)
                        scores(g, j, u)
                    if there(g - 2, STEPS):
                        turn_probs(g - 2, (j - 2) % Q_TILES)
                    if there(g - 3, STEPS):
                        before = j < 3
                        values(g - 3, (j - 3) % Q_TILES, n - before, 2 * (n - before) + (j - 3) % Q_TILES // HT)
                    if j % HT == 0 and there(half - 2, 2 * NB):
                        turn_output(half - 2, j // HT)

            over_blocks(pe, body)

        @block.scalar
        def _(act):
            def body(n, u, turn, steps):
                for j in steps:
                    g = Q_TILES * n + j
                    if not there(g, STEPS):
                        continue
                    after(act, "scored", g + 1)
                    after(act, "turned", g - 1)
                    for a in range(2):
                        h = 2 * j + a
                        ins = act.activation(PR[:, j % 2, a, :], SC[:, j % 2, a, :], ACT.Exp, scale=-1.0, bias=nm[:, h:h + 1],
                                             accum_out=rs[:, h:h + 1])
                    ins.then_inc(s["exped"], 1)
                    if j % HT == HT - 1:
                        half, hs = 2 * n + j // HT, slice(2 * (j + 1 - HT), 2 * (j + 1))
                        after(act, "es_in", half + 1)
                        act.activation(es[:, hs], es[:, hs], ACT.Exp).then_inc(s["es_exp"], 1)

            over_blocks(act, body)

        @block.vector
        def _(dve):
            def heads(b):
                return slice(2 * HT * b, 2 * HT * (b + 1))

            def mask_and_max(g, j, first):
                after(dve, "s_prod", g + 1, plain=True)
                after(dve, "exped", g - 1, plain=True)
                for a in range(2):
                    h = 2 * j + a
                    ins = dve.tensor_tensor_reduce(SC[:, j % 2, a, :], PS[2 * (j % 2) + a][:, 0:2 * P],
                                                   band[:, 0 if first else 1, :], -1.0, nsink[:, h:h + 1],
                                                   ALU.add, ALU.min, nm[:, h:h + 1])
                ins.then_inc(s["scored"], 1)

            def sink_logits(half, b):
                after(dve, "scored", HT * (half + 1))
                dve.tensor_tensor(es[:, heads(b)], nm[:, heads(b)], nsink[:, heads(b)], ALU.subtract
                                  ).then_inc(s["es_in"], 1)

            def keep_probs(t, j):
                after(dve, "turned", t + 1)
                after(dve, "pv_done", t - 1)
                dve.tensor_copy(PT[:, j % 2].rearrange("p a k -> p (a k)"), PS[4 + j % 2][:]).then_inc(s["pt_kept"], 1)

            def denominators(half, b):
                after(dve, "es_exp", half + 1)
                dve.tensor_tensor(es[:, heads(b)], es[:, heads(b)], rs[:, heads(b)], ALU.add).then_inc(s["es_added"], 1)
                dve.wait_ge(s["es_added"], half + 1)
                dve.reciprocal(es[:, heads(b)], es[:, heads(b)]).then_inc(s["es_ready"], 1)

            def divide(half, b):
                after(dve, "es_ready", half + 1)
                after(dve, "pv_done", HT * (half + 1))
                dve.tensor_tensor(OS[:, HT * b:HT * (b + 1), :].rearrange("p j (a v) -> p (j a) v", a=2),
                                  PS[6 + b][:].rearrange("p (h v) -> p h v", v=C),
                                  es[:, heads(b)].unsqueeze(2).to_broadcast([P, 2 * HT, C]), ALU.mult
                                  ).then_inc(s["o_kept"], 1)

            def gate(half, b, n):
                after(dve, "o_turned", half + 1)
                sg = SG1[:, HT * b:HT * (b + 1), ds(n * P, P)]
                dve.tensor_tensor(sg, sg, PS[6 + b][:].rearrange("p (j q) -> p j q", j=HT), ALU.mult
                                  ).then_inc(s["gated"], 1)

            def body(n, u, turn, steps):
                for j in steps:
                    g, half = Q_TILES * n + j, 2 * n + j // HT
                    if there(g, STEPS):
                        mask_and_max(g, j, isinstance(n, int) and n == 0)
                        if j % HT == HT - 1:
                            sink_logits(half, j // HT)
                    if there(g - 2, STEPS):
                        keep_probs(g - 2, (j - 2) % Q_TILES)
                    if j % HT == 1 and there(half - 1, 2 * NB):
                        denominators(half - 1, 1 - j // HT)
                    if j % HT == HT - 1 and there(half - 1, 2 * NB):
                        divide(half - 1, 1 - j // HT)
                    if j % HT == 1 and there(half - 2, 2 * NB):
                        gate(half - 2, j // HT, n - 1)

            dve.tensor_scalar(nsink[:], col("sinks", 0, 16), -1.0, None, ALU.mult).then_inc(s["setup"], 1)
            dve.wait_ge(s["setup"], 1)
            dve.wait_ge(band_in, 16)
            over_blocks(dve, body)


def _layout(inputs):
    import numpy as np

    f = {k: np.ascontiguousarray(v) for k, v in inputs.items()}

    def tiles(w, cols):
        out = np.zeros((len(cols), P, KT, P), np.float32)
        for i, c in enumerate(cols):
            out[i, :, :, :len(c)] = w[:, c].reshape(KT, P, len(c)).transpose(1, 0, 2)
        return out

    def run(a, n=P):
        return list(range(a, a + n))

    gq, gk, gv, gl, r, k, v, xx, gate = 0, 256, 512, 1024, 1040, 1552, 2064, 2576, 2704
    cols = [run(xx)]
    for p in range(PAIRS):
        cols += [run(k + p * P), run(r + p * P), run(v + p * P)]
    cols += [run(gl, 16)] + [run(gq + i * P) for i in range(8)] + [run(gate + i * P) for i in range(8)]
    w0t = tiles(f["w_in0"][0], cols)

    order = []
    for j in range(Q_TILES):
        a = 8 * (j // 4) + j % 4
        order += run(a * C, C) + run((a + 4) * C, C)
    heads = [order[i * C] // C for i in range(16)]
    w1 = f["w_in1"][0]
    kq, vq, gq1 = 1024, 1280, 1536
    w1t = tiles(w1, [order[i * P:(i + 1) * P] for i in range(8)] + [run(kq + i * P) for i in range(2)]
                + [[gq1 + o for o in order[i * P:(i + 1) * P]] for i in range(8)])
    wv1 = np.ascontiguousarray(w1[:, vq:vq + 256].reshape(KT, P, 256).transpose(1, 0, 2))
    wout0 = np.ascontiguousarray(f["w_out0"][0].reshape(KT, P, D).transpose(1, 0, 2))
    wout1 = np.ascontiguousarray(f["w_out1"][0][order].reshape(KT, P, D).transpose(1, 0, 2))

    wup = np.zeros((P, 2, PAIRS * P), np.float32)
    wup[:C, 0], wup[C:, 1] = f["rwkv_w_up"][0], f["rwkv_a_up"][0]
    wup = wup.reshape(P, 2 * PAIRS * P)
    b_in = f["b_in1"][0]
    mu = f["rwkv_mu"][0]
    vectors = {
        "norm0": f["norm_w"][0], "norm1": f["norm_w"][1], "mu_x": mu[1536:1664], "mu_k": mu[512:1024], "mu_r": mu[:512],
        "mu_v": mu[1024:1536], "w0": f["rwkv_w0"][0], "a0": f["rwkv_a0"][0], "k_k": f["rwkv_k_k"][0],
        "k_a": f["rwkv_k_a"][0], "r_k": f["rwkv_r_k"][0].reshape(-1), "ln_w": f["rwkv_ln_w"][0], "ln_b": f["rwkv_ln_b"][0],
        "gk_bias": f["gla_gk_bias"][0], "gla_norm": f["gla_norm_w"][0], "b_q": b_in[order], "b_k": b_in[1024:1280],
    }
    par = np.zeros((P, NPAR), np.float32)
    for name, vec in vectors.items():
        n = vec.size // P
        par[:, _COLS[name]:_COLS[name] + n] = vec.reshape(n, P).T
    par[:, _COLS["sinks"]:_COLS["sinks"] + 16] = f["attn_sinks"][0][heads]

    one = np.arange(P)
    h, t = one // C, one % C
    ident = np.eye(P, dtype=np.float32)
    istack = (t[:, None] == np.arange(C)).astype(np.float32)
    bdones = (h[:, None] == h[None, :]).astype(np.float32)
    cc = np.arange(C)
    maska = np.stack([t[:, None] < cc, t[:, None] <= cc], 1).astype(np.float32)
    scanm = np.broadcast_to((np.arange(T) % C != 0).astype(np.float32), (P, T)).copy()
    maskd = np.zeros((P, LEVELS, C), np.int32)
    maskb = np.zeros((P, LEVELS, 2, C), np.int32)
    for l in range(LEVELS):
        b = 1 << l

        def joint(row, c):
            return (row // (2 * b) == c // (2 * b)) & ((row // b) % 2 == 1) & ((c // b) % 2 == 0)

        maskd[:, l] = joint(t[:, None], cc[None])
        m = joint(cc[None], t[:, None]) if l == 0 else joint(t[:, None], cc[None])
        for hh in range(2):
            maskb[:, l, hh] = m & (h[:, None] == hh)
    half = 8
    inv_freq = (np.float32(500000.0) ** (-np.arange(half, dtype=np.float32) / np.float32(half))).astype(np.float32)
    ang = (np.arange(T, dtype=np.float32)[None, :] * inv_freq[:, None]).astype(np.float32).astype(np.float64)
    cos, sin = np.ones((P, T), np.float32), np.zeros((P, T), np.float32)
    for base in (0, C):
        for i in range(16):
            cos[base + i] = np.cos(ang[i % 8])
            sin[base + i] = np.sin(ang[i % 8]) * (-1.0 if i < 8 else 1.0)
    i, j = np.arange(P)[:, None], np.arange(2 * P)[None, :]
    inside = (i + P - j >= 0) & (i + P - j < P)
    band = np.stack([np.where(inside & (j >= P), 0.0, NEG), np.where(inside, 0.0, NEG)], 1).astype(np.float32)

    return {
        "x": f["x"][0], "w0t": w0t, "wup": wup,
        "gkup": f["gla_gk_up"][0], "wout0": wout0, "w1t": w1t, "wv1": wv1,
        "bv1": np.broadcast_to(b_in[1280:1536], (P, 256)).copy(), "wout1": wout1, "par": par,
        "bout1": np.broadcast_to(f["b_out1"][0], (P, D)).copy(), "fnorm": np.broadcast_to(f["final_norm_w"], (P, D)).copy(),
        "ident_d": ident, "istack_d": istack, "bdones_d": bdones, "maska_d": maska, "scan_d": scanm, "maskd_d": maskd,
        "maskb_d": maskb, "cos_d": cos, "sin_d": sin, "band_d": band,
    }


def kernel(**inputs):
    import concourse.bacc as bacc
    import numpy as np
    from concourse.bass_utils import run_bass_kernel_spmd

    nc = bacc.Bacc("TRN2", target_bir_lowering=False, num_devices=1)
    arrays = {"in_" + k: np.ascontiguousarray(v) for k, v in _layout(inputs).items()}
    args = {k[3:]: nc.dram_tensor(k, a.shape, mybir.dt.from_np(a.dtype), kind="ExternalInput").ap()
            for k, a in arrays.items()}
    out = nc.dram_tensor("out", (T, D), F, kind="ExternalOutput").ap()
    trunk(nc, **args, out=out)
    got = run_bass_kernel_spmd(nc, [arrays], core_ids=[0])
    return got.results[0]["out"].reshape(1, T, D)
```
